# Optimizing a Trainium2 kernel written in Bass

```python
import math
import jax
import jax.numpy as jnp
from jax import lax
import numpy as np

D_MODEL = 1024
BATCH = 1
SEQ = 1024
DEPTH = 1
DEC_BATCH = 8
DEC_SEQ = 4
PAST_LEN = 8192
PAGE_SIZE = 128

N_META = 16
N_BRANCH = 4
N_HEADS = 4
BRANCH_W = D_MODEL // N_BRANCH
HEAD_V = BRANCH_W // N_HEADS
HGRN_DK = HEAD_V
RWKV_N = HEAD_V
GLA_DK = HEAD_V // 2
MLSTM_DK = HEAD_V // 2
RWKV_W_LORA = D_MODEL // 16
RWKV_A_LORA = D_MODEL // 16
RWKV_G_LORA = D_MODEL // 8
RWKV_LN_EPS = 64e-5
GLA_GATE_RANK = 16
GLA_GATE_TAU = 16.0
CONV_W = 4
D_FF = 4 * D_MODEL
CHUNK = 64
EPS = 1e-6

HG_SIZES = (N_HEADS * HGRN_DK, N_HEADS * HGRN_DK, BRANCH_W, BRANCH_W)
RW_SIZES = (BRANCH_W, BRANCH_W, BRANCH_W, RWKV_W_LORA, RWKV_A_LORA, RWKV_G_LORA)
GL_SIZES = (N_HEADS * GLA_DK, N_HEADS * GLA_DK, BRANCH_W, GLA_GATE_RANK, BRANCH_W)
ML_SIZES = (2 * N_HEADS * MLSTM_DK, BRANCH_W, N_HEADS, N_HEADS, BRANCH_W)
RW_W = sum(RW_SIZES)
IN_SIZES = (sum(HG_SIZES), RW_W, sum(GL_SIZES), sum(ML_SIZES), N_BRANCH * D_MODEL)
IN_COLS = sum(IN_SIZES)

kernel_name = 'hybrid_hgrn2_rwkv7_gla_mlstm_step'

def _rms(x, g):
    xf = x.astype(jnp.float32)
    y = xf * lax.rsqrt(jnp.mean(xf * xf, axis=-1, keepdims=True) + EPS)
    return (y * g.astype(jnp.float32)).astype(x.dtype)

def _heads(t):
    return t.reshape(t.shape[:-1] + (N_HEADS, t.shape[-1] // N_HEADS))

def _head_rms(o, g):
    y = o * lax.rsqrt(jnp.mean(o * o, axis=-1, keepdims=True) + EPS)
    return y.reshape(y.shape[:-2] + (-1,)) * g

def _head_ln(o, w, b):
    mu = jnp.mean(o, axis=-1, keepdims=True)
    d = o - mu
    y = d * lax.rsqrt(jnp.mean(d * d, axis=-1, keepdims=True) + RWKV_LN_EPS)
    return y.reshape(y.shape[:-2] + (-1,)) * w + b

def _split(z, sizes):
    return jnp.split(z, np.cumsum(sizes)[:-1].tolist(), axis=-1)

def _to_chunks(t, c):
    b, T = t.shape[:2]
    return jnp.moveaxis(t.reshape((b, T // c, c) + t.shape[2:]), 1, 0)

def _from_chunks(t):
    n, b, c = t.shape[:3]
    return jnp.moveaxis(t, 0, 1).reshape((b, n * c) + t.shape[3:])

def _gla_core(seqs, s0):
    T = seqs[0].shape[1]
    c = math.gcd(T, CHUNK)
    mask = jnp.tril(jnp.ones((c, c), dtype=bool))[None, :, :, None, None]

    def step(s, inp):
        qc, kc, vc, ac = inp
        b = jnp.cumsum(ac, axis=1)
        decay = jnp.exp(jnp.where(mask, b[:, :, None] - b[:, None], -jnp.inf))
        att = jnp.einsum('bthk,bshk,btshk->bhts', qc, kc, decay)
        o = jnp.einsum('bhts,bshv->bthv', att, vc) + jnp.einsum('bthk,bhkv->bthv', qc * jnp.exp(b), s)
        bl = b[:, -1]
        s = s * jnp.exp(bl)[..., None] + jnp.einsum('bshk,bshv->bhkv', kc * jnp.exp(bl[:, None] - b), vc)
        return s, o

    s, o = lax.scan(step, s0, tuple(_to_chunks(t, c) for t in seqs))
    return _from_chunks(o), s

def _mlstm_core(seqs, state):
    T = seqs[0].shape[1]
    c = math.gcd(T, CHUNK)
    mask = jnp.tril(jnp.ones((c, c), dtype=bool))[None, :, :, None]

    def step(carry, inp):
        cm, nm, mm = carry
        qc, kc, vc, ic, fc = inp
        b = jnp.cumsum(fc, axis=1)
        dmat = jnp.where(mask, b[:, :, None] - b[:, None] + ic[:, None], -jnp.inf)
        inter = b + mm[:, None]
        m_t = jnp.maximum(inter, jnp.max(dmat, axis=2))
        wts = jnp.exp(dmat - m_t[:, :, None])
        sc = jnp.exp(inter - m_t)
        qk = jnp.einsum('bthk,bshk->btsh', qc, kc) * wts
        num = jnp.einsum('btsh,bshv->bthv', qk, vc) + sc[..., None] * jnp.einsum('bthk,bhkv->bthv', qc, cm)
        den = jnp.sum(qk, axis=2) + sc * jnp.einsum('bthk,bhk->bth', qc, nm)
        hc = num / jnp.maximum(jnp.abs(den), jnp.exp(-m_t))[..., None]
        m_new = m_t[:, -1]
        wl = jnp.exp(b[:, -1:] - b + ic - m_new[:, None])
        sl = jnp.exp(b[:, -1] + mm - m_new)
        cm = sl[..., None, None] * cm + jnp.einsum('bsh,bshk,bshv->bhkv', wl, kc, vc)
        nm = sl[..., None] * nm + jnp.einsum('bsh,bshk->bhk', wl, kc)
        return (cm, nm, m_new), hc

    st, o = lax.scan(step, state, tuple(_to_chunks(t, c) for t in seqs))
    return _from_chunks(o), st

def _run_chunked(core, seqs, state, lead):
    if lead:
        o1, state = core(tuple(t[:, :lead] for t in seqs), state)
        o2, state = core(tuple(t[:, lead:] for t in seqs), state)
        return jnp.concatenate([o1, o2], axis=1), state
    return core(seqs, state)

def _rwkv_scan(seqs, s0):
    def step(s, inp):
        rt, lwt, kt, vt, kkt, at = inp
        sa = jnp.einsum('bhvk,bhk->bhv', s, kkt)
        s = (s * jnp.exp(lwt)[:, :, None, :] - sa[..., None] * (kkt * at)[:, :, None, :]
             + vt[..., None] * kt[:, :, None, :])
        return s, jnp.einsum('bhvk,bhk->bhv', s, rt)

    s, ys = lax.scan(step, s0, tuple(jnp.moveaxis(t, 1, 0) for t in seqs))
    return jnp.moveaxis(ys, 0, 1), s

def _mixer(h, st, lead, lb, p):
    f32 = jnp.float32
    s_hg, s_rw, shift, s_gl, c_ml, n_ml, m_ml, conv_buf = st
    B, T, _ = h.shape
    z = h @ p['w_in']
    zh, zr, zg, zm, zgate = _split(z, IN_SIZES)

    hq, hf, hi, hg = _split(zh.astype(f32), HG_SIZES)
    log_f = jnp.logaddexp(jnp.log(lb), jnp.log1p(-lb) + jax.nn.log_sigmoid(hf))
    k_hg = (1.0 - lb) * jax.nn.sigmoid(-hf)
    o_hg, s_hg = _run_chunked(_gla_core, (_heads(hq), _heads(k_hg), _heads(hi), _heads(log_f)),
                              s_hg.astype(f32), lead)
    o_hg = _head_rms(o_hg, p['hgrn_norm']) * jax.nn.silu(hg)

    zr32 = zr.astype(f32)
    prev = jnp.concatenate([shift.astype(f32)[:, None], zr32[:, :-1]], axis=1)
    new_shift = zr32[:, -1]
    zs = zr32 + (prev - zr32) * p['rwkv_mu']
    r, k, v, wd, ad, gd = _split(zs, RW_SIZES)
    w = -jax.nn.softplus(-(p['rwkv_w0'] + jnp.tanh(wd) @ p['rwkv_w_up'])) - 0.5
    log_w = -jnp.exp(w)
    a = jax.nn.sigmoid(p['rwkv_a0'] + ad @ p['rwkv_a_up'])
    g = jax.nn.sigmoid(gd) @ p['rwkv_g_up']
    kk = _heads(k * p['rwkv_k_k'])
    kk = kk / jnp.maximum(jnp.linalg.norm(kk, axis=-1, keepdims=True), 1e-12)
    k = k * (1.0 + (a - 1.0) * p['rwkv_k_a'])
    rh, kh, vh = _heads(r), _heads(k), _heads(v)
    y_rw, s_rw = _rwkv_scan((rh, _heads(log_w), kh, vh, kk, _heads(a)), s_rw.astype(f32))
    bonus = jnp.sum(rh * kh * _heads(p['rwkv_r_k']), axis=-1, keepdims=True) * vh
    o_rw = (_head_ln(y_rw, p['rwkv_ln_w'], p['rwkv_ln_b']) + bonus.reshape(B, T, -1)) * g

    gq, gk, gv, ga, gg = _split(zg.astype(f32), GL_SIZES)
    log_a = jax.nn.log_sigmoid(ga @ p['gla_gate_up'] + p['gla_gate_b']) / GLA_GATE_TAU
    o_gl, s_gl = _run_chunked(_gla_core, (_heads(gq) * GLA_DK ** -0.5, _heads(gk), _heads(gv), _heads(log_a)),
                              s_gl.astype(f32), lead)
    o_gl = _head_rms(o_gl, p['gla_norm']) * jax.nn.silu(gg)

    mqk, mv, mi, mf, mo = _split(zm.astype(f32), ML_SIZES)
    full = jnp.concatenate([conv_buf.astype(f32), mqk], axis=1)
    new_buf = full[:, T:]
    conv = p['mlstm_conv_b'] + full[:, 0:T] * p['mlstm_conv_w'][0]
    for j in range(1, CONV_W):
        conv = conv + full[:, j:j + T] * p['mlstm_conv_w'][j]
    mq, mk = jnp.split(jax.nn.silu(conv), 2, axis=-1)
    ig = mi + p['mlstm_i_b']
    lf = jax.nn.log_sigmoid(mf + p['mlstm_f_b'])
    o_ml, (c_ml, n_ml, m_ml) = _run_chunked(
        _mlstm_core, (_heads(mq), _heads(mk) * MLSTM_DK ** -0.5, _heads(mv), ig, lf),
        (c_ml.astype(f32), n_ml.astype(f32), m_ml.astype(f32)), lead)
    o_ml = _head_rms(o_ml, p['mlstm_norm']) * jax.nn.sigmoid(mo)

    outs = jnp.stack([o_hg, o_rw, o_gl, o_ml], axis=2).astype(h.dtype)
    proj = jnp.einsum('btnc,ncd->btnd', outs, p['w_branch'])
    gates = jax.nn.sigmoid(zgate).reshape(B, T, N_BRANCH, D_MODEL)
    mix = jnp.sum(proj * gates, axis=2) @ p['w_out']
    return mix, (s_hg, s_rw, new_shift, s_gl, c_ml, n_ml, m_ml, new_buf)

def _trunk(x, init, lead, lb_all, P):
    new = [[] for _ in init]
    for l in range(DEPTH):
        p = {name: arr[l] for name, arr in P.items()}
        mix, st = _mixer(_rms(x, p['norm_mix']), tuple(s[l] for s in init), lead, lb_all[l], p)
        x = x + mix.astype(x.dtype)
        hn = _rms(x, p['norm_mlp'])
        x = x + jnp.square(jax.nn.relu(hn @ p['w_up'])) @ p['w_down']
        for lst, s in zip(new, st):
            lst.append(s)
    return x, [jnp.stack(lst).astype(x.dtype) for lst in new]

def setup_inputs(seed: int = 0) -> dict:
    key = jax.random.key(seed)
    ks = iter(jax.random.split(key, 64))
    f32 = jnp.float32
    L, H = DEPTH, N_HEADS

    def nrm(shape, scale):
        return jax.random.normal(next(ks), shape, f32) * scale

    return {
        'x_prompt': nrm((BATCH, SEQ, D_MODEL), 1.0),
        'x_sample': nrm((DEC_BATCH, DEC_SEQ, D_MODEL), 1.0),
        'state_hgrn': nrm((L, DEC_BATCH, H, HGRN_DK, HEAD_V), 0.3),
        'state_rwkv': nrm((L, DEC_BATCH, H, RWKV_N, RWKV_N), 0.3),
        'state_rwkv_shift': nrm((L, DEC_BATCH, RW_W), 1.0),
        'state_gla': nrm((L, DEC_BATCH, H, GLA_DK, HEAD_V), 0.3),
        'state_mlstm_c': nrm((L, DEC_BATCH, H, MLSTM_DK, HEAD_V), 0.3),
        'state_mlstm_n': nrm((L, DEC_BATCH, H, MLSTM_DK), 0.3),
        'state_mlstm_m': 1.0 + nrm((L, DEC_BATCH, H), 0.5),
        'state_mlstm_conv': nrm((L, DEC_BATCH, CONV_W - 1, 2 * H * MLSTM_DK), 1.0),
        'meta_tokens': nrm((N_META, D_MODEL), 1.0),
        'norm_mix': 1.0 + nrm((L, D_MODEL), 0.05),
        'norm_mlp': 1.0 + nrm((L, D_MODEL), 0.05),
        'norm_final': 1.0 + nrm((D_MODEL,), 0.05),
        'w_in': nrm((L, D_MODEL, IN_COLS), D_MODEL ** -0.5),
        'hgrn_lb': nrm((L, H * HGRN_DK), 0.5),
        'hgrn_norm': 1.0 + nrm((L, BRANCH_W), 0.05),
        'rwkv_mu': jax.random.uniform(next(ks), (L, RW_W), f32),
        'rwkv_w0': nrm((L, BRANCH_W), 0.5) - 0.5,
        'rwkv_w_up': nrm((L, RWKV_W_LORA, BRANCH_W), 0.5 * RWKV_W_LORA ** -0.5),
        'rwkv_a0': nrm((L, BRANCH_W), 0.5),
        'rwkv_a_up': nrm((L, RWKV_A_LORA, BRANCH_W), 0.5 * RWKV_A_LORA ** -0.5),
        'rwkv_g_up': nrm((L, RWKV_G_LORA, BRANCH_W), RWKV_G_LORA ** -0.5),
        'rwkv_k_k': 0.85 + nrm((L, BRANCH_W), 0.05),
        'rwkv_k_a': 1.0 + nrm((L, BRANCH_W), 0.05),
        'rwkv_r_k': nrm((L, BRANCH_W), 0.1),
        'rwkv_ln_w': 1.0 + nrm((L, BRANCH_W), 0.05),
        'rwkv_ln_b': nrm((L, BRANCH_W), 0.02),
        'gla_gate_up': nrm((L, GLA_GATE_RANK, H * GLA_DK), GLA_GATE_RANK ** -0.5),
        'gla_gate_b': 1.0 + nrm((L, H * GLA_DK), 1.0),
        'gla_norm': 1.0 + nrm((L, BRANCH_W), 0.05),
        'mlstm_conv_w': nrm((L, CONV_W, 2 * H * MLSTM_DK), CONV_W ** -0.5),
        'mlstm_conv_b': nrm((L, 2 * H * MLSTM_DK), 0.02),
        'mlstm_i_b': nrm((L, H), 0.1) - 1.0,
        'mlstm_f_b': 3.0 + nrm((L, H), 0.5),
        'mlstm_norm': 1.0 + nrm((L, BRANCH_W), 0.05),
        'w_branch': nrm((L, N_BRANCH, BRANCH_W, D_MODEL), BRANCH_W ** -0.5),
        'w_out': nrm((L, D_MODEL, D_MODEL), D_MODEL ** -0.5),
        'w_up': nrm((L, D_MODEL, D_FF), D_MODEL ** -0.5),
        'w_down': nrm((L, D_FF, D_MODEL), 0.5 * D_FF ** -0.5),
    }

def reference(x_prompt, x_sample, state_hgrn, state_rwkv, state_rwkv_shift, state_gla,
              state_mlstm_c, state_mlstm_n, state_mlstm_m, state_mlstm_conv,
              meta_tokens, norm_mix, norm_mlp, norm_final, w_in, hgrn_lb, hgrn_norm,
              rwkv_mu, rwkv_w0, rwkv_w_up, rwkv_a0, rwkv_a_up, rwkv_g_up, rwkv_k_k, rwkv_k_a,
              rwkv_r_k, rwkv_ln_w, rwkv_ln_b, gla_gate_up, gla_gate_b, gla_norm,
              mlstm_conv_w, mlstm_conv_b, mlstm_i_b, mlstm_f_b, mlstm_norm,
              w_branch, w_out, w_up, w_down):
    P = {
        'norm_mix': norm_mix, 'norm_mlp': norm_mlp, 'w_in': w_in, 'hgrn_norm': hgrn_norm,
        'rwkv_mu': rwkv_mu, 'rwkv_w0': rwkv_w0, 'rwkv_w_up': rwkv_w_up, 'rwkv_a0': rwkv_a0,
        'rwkv_a_up': rwkv_a_up, 'rwkv_g_up': rwkv_g_up, 'rwkv_k_k': rwkv_k_k, 'rwkv_k_a': rwkv_k_a,
        'rwkv_r_k': rwkv_r_k, 'rwkv_ln_w': rwkv_ln_w, 'rwkv_ln_b': rwkv_ln_b,
        'gla_gate_up': gla_gate_up, 'gla_gate_b': gla_gate_b, 'gla_norm': gla_norm,
        'mlstm_conv_w': mlstm_conv_w, 'mlstm_conv_b': mlstm_conv_b, 'mlstm_i_b': mlstm_i_b,
        'mlstm_f_b': mlstm_f_b, 'mlstm_norm': mlstm_norm,
        'w_branch': w_branch, 'w_out': w_out, 'w_up': w_up, 'w_down': w_down,
    }
    lb_cs = jnp.cumsum(jax.nn.softmax(hgrn_lb.astype(jnp.float32), axis=0), axis=0)
    lb_all = lb_cs - lb_cs[:1]

    sample_states = (state_hgrn, state_rwkv, state_rwkv_shift, state_gla,
                     state_mlstm_c, state_mlstm_n, state_mlstm_m, state_mlstm_conv)

    B = x_prompt.shape[0]
    meta = jnp.broadcast_to(meta_tokens.astype(x_prompt.dtype)[None], (B, N_META, D_MODEL))
    xp = jnp.concatenate([meta, x_prompt], axis=1)
    init_p = [jnp.zeros((DEPTH, B) + s.shape[2:], x_prompt.dtype) for s in sample_states]
    hp, st_p = _trunk(xp, init_p, N_META, lb_all, P)
    y_prompt = _rms(hp[:, N_META:], norm_final)

    hs, st_s = _trunk(x_sample, list(sample_states), 0, lb_all, P)
    y_sample = _rms(hs, norm_final)

    hgrn_p, rwkv_p, shift_p, gla_p, mc_p, mn_p, mm_p, conv_p = st_p
    hgrn_s, rwkv_s, shift_s, gla_s, mc_s, mn_s, mm_s, conv_s = st_s
    return (y_prompt, y_sample,
            hgrn_p, rwkv_p, shift_p, gla_p, mc_p, mn_p, mm_p, conv_p,
            hgrn_s, rwkv_s, shift_s, gla_s, mc_s, mn_s, mm_s, conv_s)


_drawn_inputs = setup_inputs


def setup_inputs(seed=0):
    import zlib

    import numpy as np

    out = dict(_drawn_inputs(seed))
    spreads = {}
    factors = {'hgrn_norm': 3.922,
     'rwkv_k_k': 18.045,
     'rwkv_ln_w': 4.829,
     'rwkv_ln_b': 26.43,
     'gla_norm': 3.843,
     'mlstm_norm': 4.532,
     'norm_mlp': 4.675}
    for name, (base, spread) in spreads.items():
        noise = np.random.default_rng([zlib.crc32(name.encode()), seed]).standard_normal(out[name].shape)
        drawn = base * np.exp(spread * noise) if base else spread * noise
        out[name] = jnp.asarray(drawn.astype(out[name].dtype))
    for name, factor in factors.items():
        out[name] = (out[name] * factor).astype(out[name].dtype)
    return out
```

```python
import numpy as np
import concourse.bass as bass
from concourse import mybir
from contextlib import ExitStack

F32 = mybir.dt.float32
U8 = mybir.dt.uint8
ALU = mybir.AluOpType
ACT = mybir.ActivationFunctionType
AX = mybir.AxisListType

D, META, SEQ, NSEQ, DSEQ, FF = 1024, 16, 1024, 8, 4, 4096
P = 128
NP = META + SEQ
NT = NP + NSEQ * DSEQ
GRP = 358
W = 3 * GRP
TILES = NT // P
LASTW = NT - TILES * P
TAIL = NP - TILES * P
SEGS = 1 + NSEQ
KD = D // P
EPS, LN_EPS = 1e-6, 64e-5
DECAY = float(np.exp(-0.5))
HALVES = [1, 2, 4, 8, 16, 32, 64]
LHALVES = [1, 2, 4, 8]
BIG = 1e30
DEPTH = 1

O_HG, O_RW, O_GL, O_ML, O_GATE = 0, 1024, 2048, 2832, 3608
ML_T = [O_ML, O_ML + 128, O_ML + 520, O_ML + 648]
ML_V = [O_ML + 256, O_ML + 384]
GL_T = [O_HG, O_HG + 128, O_HG + 256, O_HG + 384, O_HG + 768, O_HG + 896,
        O_GL, O_GL + 128, O_GL + 528, O_GL + 656]
GL_V = [O_HG + 512, O_HG + 640, O_GL + 256, O_GL + 384]
RW_T = [O_RW + 128 * j for j in range(8)]
SMALL = [(O_GL + 512, 16, 0), (O_ML + 512, 4, 32), (O_ML + 516, 4, 64)]

COLS = {}
for _name, _n in [("norm_mix", 8), ("norm_mlp", 8), ("norm_final", 8), ("hgrn_norm", 2), ("gla_norm", 2),
                  ("mlstm_norm", 2), ("rwkv_mu", 8), ("rwkv_w0", 2), ("rwkv_a0", 2), ("rwkv_k_k", 2),
                  ("rwkv_k_a", 2), ("rwkv_r_k", 2), ("rwkv_ln_w", 2), ("rwkv_ln_b", 2), ("gla_gate_b", 1),
                  ("mlstm_conv_w", 8), ("mlstm_conv_b", 2), ("mlstm_i_b", 1), ("mlstm_f_b", 1)]:
    COLS[_name] = (sum(n for _, n in COLS.values()), _n)
NCOLS = sum(n for _, n in COLS.values())


def constants():
    s, t = np.arange(P)[:, None], np.arange(P)[None, :]
    seg = np.where(np.arange(P) < TAIL, 0, 1 + (np.arange(P) - TAIL) // DSEQ)
    same = seg[:, None] == seg[None, :]

    def pair(h):
        return ((s // (2 * h)) == (t // (2 * h))) & (s % (2 * h) < h) & (t % (2 * h) >= h)

    lv = [pair(h) for h in HALVES]
    ll = [pair(h) & same for h in LHALVES]
    f = {
        "eps": np.tile(np.array([[EPS, LN_EPS]]), (P, 1)),
        "ident": np.eye(P), "ones": np.ones((P, P)),
        "bd_gl": np.concatenate([np.kron(np.eye(2), np.ones((64, 64)))] * 2
                                + [np.kron(np.eye(4), np.ones((32, 64)))], 1),
        "causal": np.stack([s < t, s <= t], 1),
        "causal_l": np.stack([(s < t) & same, (s <= t) & same], 1)[:, :, :LASTW],
        "keep": np.tile((np.where(np.arange(W) < NP, np.arange(W) % P,
                                  (np.arange(W) - NP) % DSEQ) != 0)[None], (P, 1)),
        "ind_t": np.tile((np.arange(SEGS)[:, None] == seg[None, :LASTW])[None], (P, 1, 1)),
        "ind_p": (seg[:, None] == np.arange(SEGS)[None]) & (s < LASTW),
        "bd_ml": np.kron(np.eye(4), np.ones((32, 65))),
        "neg": np.where(s <= t, 0, -BIG), "neg_l": np.where((s <= t) & same, 0, -BIG)[:, :LASTW],
        "head4": np.kron(np.eye(4), np.ones((32, 1))),
        "sel4": (t // 32 == s) & (s < 4),
        "bd4": np.kron(np.eye(P, 4), np.ones((1, P))),
        "bd4_l": np.kron(np.eye(P, 4), np.ones((1, LASTW))),
    }
    u = {"lv": np.stack(lv + [s == t], 1), "lvt": np.stack([m.T for m in lv], 1),
         "ll": np.stack(ll + [s == t], 1)[:, :, :LASTW], "llt": np.stack([m.T for m in ll], 1)[:, :, :LASTW]}
    f = {k: v.reshape(P, -1).astype(np.float32) for k, v in f.items()}
    u = {k: v.reshape(P, -1).astype(np.float32) for k, v in u.items()}
    return f, u


SEMAPHORES = """
    act_step banks_free0 banks_free1 chunk_done0 chunk_done1 chunk_loaded0 chunk_loaded1 consts
    conv_ready dn_ready down0 down1 down_used0 down_used1 dve_step gl_att gl_ds gl_dsu gl_e
    gl_f gl_final gl_go gl_in gl_kh gl_kt gl_ln gl_o gl_on gl_ot gl_qk gl_qx gl_s gl_sq gl_vx gl_x
    gl_z gl_zero gl_zz ht_ready mix_ready ml_att ml_bc ml_conv
    ml_copied ml_ds ml_dsu ml_e ml_final ml_gbd ml_go ml_if ml_in ml_kh ml_kt ml_ln ml_mt ml_o ml_on
    ml_ot ml_pre ml_qx ml_rows ml_s ml_sc ml_silu ml_sq ml_vx ml_x ml_zero out phase res_used
    rstd ml_ms ml_rs gl_ms gl_rs rw_ms rw_rs select_turn gl_third gl_dk gl_qe gt_free gt_done gt_sent z0 z1 pz0 pz1 sig0 sig1 mul0 mul1 mix_add rw_copied rw_ds rw_dsu rw_ex rw_ex_used rw_final rw_go rw_hs rw_in rw_kkr rw_kt rw_kv rw_lev
    rw_lor rw_lora rw_m rw_m1 rw_mix rw_n rw_on rw_ot rw_pre rw_qx rw_r rw_rhs rw_s rw_sq rw_t rw_u
    rw_us rw_vx rw_w rw_wlx rw_y rw_yc rw_zero shift_ready small sq_ready spilled sq_used wb0 wb1 wb_used0
    wb_used1 wga ws x0 x1 x2 x3 x4 x5 x6 x7 xj0 xj1 xr xr_ready y_out y_ready
""".split()


GL_ATT = [0, 2, 4, 1, 3, 6, 5, 7]


class Steps:

    def __init__(self, eng, sem):
        self.eng, self.sem, self.n, self.i = eng, sem, 0, None

    def did(self, ins):
        ins.then_inc(self.sem, 1)
        self.n += 1

    def settle(self):
        if self.i is None:
            self.eng.wait_ge(self.sem, self.n)
        else:
            self.eng.wait_ge(self.sem, self.i * self.per + self.n)

    def enter(self, i, per):
        self.i, self.per, self.start = i, per, self.n

    def leave(self, times):
        assert self.n - self.start == self.per, (self.n - self.start, self.per)
        self.n, self.i = self.start + self.per * times, None


def build(nc, A, OUT, fcols, ucols, fdim, udim):
    ctx = ExitStack()
    with ctx:
        def sb(name, cols, dt=F32):
            return ctx.enter_context(nc.sbuf_tensor(name, [P, cols], dt))

        sems = {name: ctx.enter_context(nc.semaphore(name)) for name in SEMAPHORES}

        def S(name):
            return sems[name]

        HT = sb("HT", KD * W)[:, :].rearrange("p (k t) -> p k t", k=KD)
        OT = sb("OT", 8 * W)[:, :].rearrange("p (k t) -> p k t", k=8)
        CF = sb("CF", fdim)
        CU = sb("CU", udim, U8)
        CC = sb("CC", NCOLS)
        WGA = sb("WGA", P)
        RING = sb("RING", 2 * 8 * P)[:, :].rearrange("p (u k c) -> p u k c", u=2, k=8)
        PSt = ctx.enter_context(nc.psum_tensor("PS", [P, 8 * 512], F32))

        def PS(b, lo=0, hi=512):
            return PSt[:, b * 512 + lo:b * 512 + hi]

        NA = (nc.sbuf_usable_end - nc.sbuf_base) // 4 - 16
        AR = sb("AR", NA)

        def const(name, rows=P):
            o, n = fcols[name]
            return CF[0:rows, o:o + n]

        def mask8(name, k, rows=P):
            o, n = ucols[name]
            w = {"lv": P, "lvt": P, "ll": LASTW, "llt": LASTW}[name]
            return CU[0:rows, o + k * w:o + (k + 1) * w]

        def col(name, j=0, rows=P, lo=0):
            o, _ = COLS[name]
            return CC[lo:rows, o + j:o + j + 1]

        ZS = CF[:, fcols["bd_ml"][0]:fcols["bd_ml"][0] + W]

        class Arena:
            def __init__(self, at=0):
                self.at = at

            def take(self, pattern=None, rows=P, **dims):
                n = 1
                for v in dims.values():
                    n *= v
                o = self.at
                self.at += n
                assert self.at <= NA, (self.at, NA)
                x = AR[0:rows, o:o + n]
                if len(dims) > 1:
                    names = " ".join(dims)
                    x = x.rearrange(f"p ({names}) -> p {names}", **dims)
                return x

        EPS_COL = {EPS: slice(0, 1), LN_EPS: slice(1, 2)}
        ident, ones, keep = const("ident"), const("ones"), const("keep")
        bd2 = const("bd_gl")[:, 0:P]

        def cols3(b):
            return PSt[:, b * 512:(b + 3) * 512].rearrange("p (g c) -> p g c", g=3)[:, :, 0:GRP]

        def half(x, h, second):
            names = " ".join("abc"[:len(x.shape) - 2])
            y = x.rearrange(f"p {names} (n t) -> p {names} n t", t=2 * h)
            return y[(slice(None),) * (len(y.shape) - 1) + (slice(h, 2 * h) if second else slice(0, h),)]

        def row3(x):
            return x.rearrange("p (g c) -> p g c", g=3)

        def bc(x, shape):
            return x.to_broadcast(shape)

        a = Arena()
        GA = a.take(c=W)
        KEEPTO = a.at
        a = Arena(KEEPTO)
        XT = a.take(k=KD, t=W)
        SQB = a.take(u=2, t=W)
        RST = a.take(t=W)
        WS = a.take(k=KD, c=68)
        CUF = a.take(c=udim)
        a = Arena(KEEPTO)
        RI, RF, RT, RB, RM, RNG, RG, RSC, RKH = (a.take(rows=4, c=W) for _ in range(9))
        a.at = max(a.at, 0)
        WS_END = KEEPTO + KD * W + 3 * W + KD * 68
        RM0 = a.take(rows=4, c=20)
        FP = a.take(g=2, c=NP + 3 + NSEQ * (DSEQ + 3))
        M4 = a.take(s=4, t=W)
        VA = a.take(t=TILES + 1, h=4, c=65)
        SM = a.take(s=SEGS, c=260)
        EMM = a.take(t=TILES + 1, h=4)
        MC = a.take(s=4, t=P)
        GBD = a.take(rows=4, h=4, t=P)
        GST = a.take(rows=4, t=P)
        MX = a.take(h=4, t=P)
        MQH = a.take(h=4, t=P)
        MATT = a.take(h=4, t=P)
        MKH = a.take(c=P)
        MON = a.take(h=4, c=64)
        MSQ = a.take(h=4, c=64)
        MTMP = a.take(c=260)
        MS = a.take(k=8, h=4)
        MQX = a.take(s=SEGS, t=LASTW)
        MVX = a.take(s=SEGS, c=260)
        MES = a.take(s=SEGS)
        MSL = a.take(n=TILES)
        a = Arena(KEEPTO)
        GQ = a.take(g=3, t=W)
        GK = a.take(g=3, t=W)
        GB0 = a.at
        GB = a.take(g=3, t=W)
        GV = a.take(t=TILES + 1, c=512)
        GX0 = a.at
        GX = a.take(g=3, l=10, t=P)
        GE0 = a.at
        GE = a.take(g=3, l=2, t=P)
        a.at = max(a.at, GE0 + 3 * W)
        GATT = a.take(h=8, t=P)
        GKH = a.take(c=3 * P)
        b = Arena(0)
        GSQ = b.take(h=8, c=64)
        GON = b.take(h=8, c=64)
        GTMP = a.take(c=512)
        GMS = a.take(k=2, h=8)
        SG = a.take(s=SEGS, c=512)
        GES = a.take(g=3, s=SEGS)
        b = Arena(GX0)
        GT = b.take(g=3, t=W)
        GTMPL = Arena(GB0).take(s=SEGS, c=256)
        GXL = Arena(GX0).take(g=3, l=7, t=LASTW)
        b = Arena(GX0 + 3 * 7 * LASTW)
        GVX = b.take(s=SEGS, c=256)
        assert b.at <= GE0
        b = Arena(GE0)
        GL_ = b.take(g=3, t=W)
        b = Arena(GE0)
        GEL = b.take(g=3, l=2, t=LASTW)
        GQX = b.take(g=3, s=SEGS, t=LASTW)
        a = Arena()
        R10 = a.take(s=10, t=W)
        RBV = a.take(g=2, t=W)
        RTMP0 = a.at
        RA = a.take(g=2, t=W)
        RWL = a.take(g=2, t=W)
        RKK = a.take(g=2, t=W)
        RE = a.take(g=2, t=W)
        RX = a.take(g=2, t=W)
        RKP = a.take(g=2, t=W)
        RCS = a.take(g=2, t=TILES)
        REC = a.take(g=2, t=TILES)
        REC2 = a.take(g=2, t=TILES)
        RES = a.take(g=2, s=SEGS)
        SHI = a.take(s=8, q=NSEQ)
        SHO = a.take(s=8, q=SEGS)
        OMK = a.take(g=2)
        RWK = a.take(w=256)
        RGU = a.take(w=256)
        RSTATE = a.take(s=SEGS, c=256)
        RXC = a.take(c=256)
        assert a.at <= NA
        b = Arena(RTMP0)
        RD = b.take(s=8, t=W)
        b = Arena(RTMP0)
        RC = b.take(s=10, t=P)
        RD0 = b.at
        RPB = b.take(h=4, k=2, t=P)
        RPK = b.take(h=4, k=2, t=P)
        RTT = b.take(h=4, t=P)
        RTI = b.take(h=4, t=P)
        RM10 = b.at
        RM1 = b.take(h=4, t=P)
        RKB = b.take(c=512)
        RV = b.take(c=256)
        RRS = b.take(c=256)
        RUS = b.take(c=256)
        RY = b.take(h=4, c=64)
        RMS_ = b.take(k=4, h=4)
        RTM = Arena(b.at).take(c=256)
        RSQ = Arena(RM10).take(h=4, c=64)
        RQX = b.take(k=2, g=2, s=SEGS, t=LASTW)
        RVX = b.take(s=SEGS, c=256)
        RUX = b.take(s=SEGS, c=256)
        RDSL = Arena(RD0).take(s=SEGS, c=P)
        assert b.at <= RTMP0 + 12 * W, b.at - RTMP0 - 12 * W
        a = Arena(0)
        MIX = a.take(k=KD, t=W)
        WB = a.take(u=2, k=8, c=P)
        GZ = a.take(u=2, t=W)
        GPR = a.take(u=3, t=W)
        XR = a.take(k=KD, t=W)
        SQ2 = a.take(u=2, t=W)
        RST2 = a.take(t=W)
        HN = HT
        HN2 = OT
        a = Arena(0)
        ACTA = a.take(k=24, t=W)
        XJ = a.take(u=2, t=W)
        SQ3 = Arena(0).take(u=2, t=W)
        SQ3R = Arena(2 * W).take(t=W)

        xs, ys = A["xT"], OUT["yT"]
        block = ctx.enter_context(nc.Block())

        def barrier(e, k):
            e.drain().then_inc(S("phase"), 1)
            e.wait_ge(S("phase"), 4 * k)

        def pe_chunk(e, u, bank):
            for g in range(3):
                for k in range(KD):
                    last = e.matmul(PS(bank + g, 0, GRP), RING[:, u, k, :], HT[:, k, g * GRP:(g + 1) * GRP],
                                    start=k == 0, stop=k == KD - 1)
            return last

        def pe_pair(e, p, ev):
            for u in range(2):
                e.wait_ge(S(f"chunk_loaded{u}"), (p + 1) * 16)
                e.wait_ge(S(f"banks_free{u}"), ev + 1)
                pe_chunk(e, u, 3 * u).then_inc(S(f"chunk_done{u}"), 1)

        def gate_work(e, n, first_pair, first_tile):
            for u in range(2):
                for g in range(3):
                    c = 3 * u + g
                    if g == 0:
                        e.wait_ge(S(f"chunk_loaded{u}"), (n + first_pair + 1) * 16)
                    e.wait_ge(S("gt_free"), (n + first_tile) * 6 + (c + 1))
                    for k in range(KD):
                        last = e.matmul(PS(6 + c % 2, 0, GRP), RING[:, u, k, :], HT[:, k, g * GRP:(g + 1) * GRP],
                                        start=k == 0, stop=k == KD - 1)
                        if k % 2 and k < KD - 1:
                            yield
                    last.then_inc(S("gt_done"), 1)
                    if g == 2:
                        e.drain().then_inc(S(f"chunk_done{u}"), 1)
                    yield

        def gate_out(e, n, c, first_tile):
            u, g = c // 3, c % 3
            if g == 0:
                e.wait_ge(S("gt_sent"), ((n + first_tile) * 2 + (u + 1)) * 16)
            e.wait_ge(S("gt_done"), (n + first_tile) * 6 + (c + 1))
            e.activation(ZS[:, g * GRP:(g + 1) * GRP], PS(6 + c % 2, 0, GRP), ACT.Copy).then_inc(S("gt_free"), 1)
            if g == 2:
                e.wait_ge(S("gt_free"), (n + first_tile) * 6 + (c + 3))
                e.dma_start(A["gates"][bass.ds(n * 2 + (2 * first_tile + u), 1)].rearrange("o p t -> (o p) t"),
                            ZS).then_inc(S("gt_sent"), 16)

        def steps(work, k):
            for _ in range(k):
                next(work, None)

        def pe_vpair(e, p, ev):
            for u in range(2):
                e.wait_ge(S(f"chunk_loaded{u}"), (p + 1) * 16)
                e.wait_ge(S(f"banks_free{u}"), ev + 1)
                for t in range(TILES + 1):
                    w = P if t < TILES else LASTW
                    o = 3 * u * 512 + t * P
                    for k in range(KD):
                        last = e.matmul(PSt[0:w, o:o + P], HT[:, k, t * P:t * P + w], RING[:, u, k, :],
                                        start=k == 0, stop=k == KD - 1)
                last.then_inc(S(f"chunk_done{u}"), 1)

        def evac(e, u, p, emit, copy_in=None):
            e.wait_ge(S(f"chunk_done{u}"), p + 1)
            emit(3 * u).then_inc(S(f"banks_free{u}"), 1)

        def act_copy(e, out, in_, func=ACT.Copy, **kw):
            return e.activation(out, in_, func, **kw)

        def evac_v(e, u, p, dst, eng_act):
            def emit(b):
                src = PSt[:, b * 512:b * 512 + TILES * P].rearrange("p (t c) -> p t c", t=TILES)
                tail = PSt[0:LASTW, b * 512 + TILES * P:b * 512 + (TILES + 1) * P]
                for t in range(2):
                    o, i = (dst(0), src) if t == 0 else (dst(1), tail)
                    if len(o.shape) - len(i.shape) == 1:
                        i = i.rearrange("p (h c) -> p h c", c=64) if t else i.rearrange("p t (h c) -> p t h c", c=64)
                    if eng_act:
                        last = e.activation(o, i, ACT.Copy)
                    else:
                        last = e.tensor_copy(o, i)
                return last
            evac(e, u, p, emit)

        def rms_pe(e, r, k8=KD):
            for k in range(KD):
                e.wait_ge(S("sq_ready"), r * KD + k + 1)
                for g in range(3):
                    last = e.matmul(PS(g, 0, GRP), ones, rms_sq[r][:, k % 2, g * GRP:(g + 1) * GRP],
                                    start=k == 0, stop=k == KD - 1)
                last.then_inc(S("sq_used"), 1)

        def rms_act(e, st, r, rst, src, ready=None):
            for k in range(KD):
                if ready is not None:
                    ready(k)
                if k >= 2:
                    e.wait_ge(S("sq_used"), r * KD + k - 1)
                e.activation(rms_sq[r][:, k % 2, :], src[:, k, :], ACT.Square,
                             scale=D ** -0.5).then_inc(S("sq_ready"), 1)
            e.wait_ge(S("sq_used"), (r + 1) * KD)
            rstd(e, st, row3(rst), cols3(0)).then_inc(S("rstd"), 1)

        def rstd(e, st, out, in_, eps=EPS):
            st.did(e.activation(out, in_, ACT.Ln, bias=const("eps", in_.shape[0])[:, EPS_COL[eps]]))
            st.settle()
            return e.activation(out, out, ACT.Exp, scale=-0.5)

        def rms_dve(e, r, rst, src, dst, name, each=None):
            e.wait_ge(S("rstd"), r + 1)
            for k in range(KD):
                ins = e.scalar_tensor_tensor(dst[:, k, :], src[:, k, :], col(name, k), rst, ALU.mult, ALU.mult)
                if each is not None:
                    each(ins)
            return ins

        rms_sq = [SQB, SQ2, SQ3]

        P_ML, P_GL, P_G1, P_RW, P_G2 = 0, 3, 10, 18, 22
        P_OUT, P_UP, P_DOWN = 30, 34, 50
        EV_RW = 10
        EV_OUT, EV_UP = 14, 18

        @block.sync
        def _(e):
            e.dma_start(CF[:, :], A["cf"]).then_inc(S("consts"), 16)
            e.dma_start(CUF, A["cu"]).then_inc(S("consts"), 16)
            e.dma_start(CC[:, :], A["cols"]).then_inc(S("consts"), 16)
            for k in range(KD):
                e.dma_start(XT[:, k, :], xs[k]).then_inc(S(f"x{k}"), 16)
            e.dma_start(WS, A["w_small"]).then_inc(S("ws"), 16)

            def load(u, p):
                e.dma_start(RING[:, u], A["w_all"][bass.ds(p * 2 + u, 1)].rearrange(
                    "o p k c -> (o p) k c")).then_inc(S(f"chunk_loaded{u}"), 16)

            for u in range(2):
                load(u, 0)
            with e.Fori(1, P_DOWN + 16) as p:
                for u in range(2):
                    e.wait_ge(S(f"chunk_done{u}"), p)
                    load(u, p)
            for k in range(KD):
                e.wait_ge(S("y_ready"), k + 1)
                e.dma_start(ys[k], HN2[:, k, 0:NT]).then_inc(S("y_out"), 16)
            e.wait_ge(S("y_out"), 16 * KD)

        def pool_program(e):
            barrier(e, 1)
            e.memset(SM, 0.0)
            e.memset(VA, 1.0)
            e.memset(MATT, 0.0)
            e.memset(M4[:, :, NT:W], 0.0)
            e.memset(RM0, 0.0)
            e.memset(FP[:, :, 0:3], 0.0).then_inc(S("ml_zero"), 1)
            e.wait_ge(S("ml_zero"), 1)
            fdec = FP[:, :, NP + 3:].rearrange("p g (q c) -> p g q c", q=NSEQ)
            for g in range(2):
                e.dma_start(fdec[:, g, :, 0:3], A["conv"][:, g]).then_inc(S("ml_in"), 16)
            for h in range(4):
                r = slice(32 * h, 32 * h + 32)
                e.dma_start(SM[r, 1:, h * 65:h * 65 + 64], A["mc"][:, h].rearrange("s k v -> k s v")).then_inc(S("ml_in"), 16)
                e.dma_start(SM[r, 1:, h * 65 + 64], A["mn"][:, h].rearrange("s k -> k s")).then_inc(S("ml_in"), 16)
            e.dma_start(RM0[:, 12:20], A["mm"].rearrange("s h -> h s")).then_inc(S("ml_in"), 16)
            e.wait_ge(S("ml_in"), 11 * 16)
            e.wait_ge(S("conv_ready"), 2)
            for g in range(2):
                e.dma_start(OUT["conv_p"][:, g], FP[:, g, NP:NP + 3]).then_inc(S("out"), 16)
                e.dma_start(OUT["conv_s"][:, g], fdec[:, g, :, DSEQ:DSEQ + 3]).then_inc(S("out"), 16)
            e.wait_ge(S("ml_final"), 1)
            for h in range(4):
                r = slice(32 * h, 32 * h + 32)
                e.dma_start(OUT["mc"][:, h].rearrange("s k v -> k s v"), SM[r, :, h * 65:h * 65 + 64]).then_inc(S("out"), 16)
                e.dma_start(OUT["mn"][:, h].rearrange("s k -> k s"), SM[r, :, h * 65 + 64]).then_inc(S("out"), 16)
            e.dma_start(OUT["mm"][0:1].rearrange("s h -> h s"), RM[:, NP - 1:NP]).then_inc(S("out"), 16)
            e.dma_start(OUT["mm"][1:].rearrange("s h -> h s"),
                        RM[:, NP:NT].rearrange("p (q c) -> p q c", q=NSEQ)[:, :, DSEQ - 1]).then_inc(S("out"), 16)
            e.wait_ge(S("out"), 14 * 16)
            barrier(e, 2)
            e.memset(SG, 0.0)
            e.memset(GATT, 0.0).then_inc(S("gl_zero"), 1)
            e.wait_ge(S("gl_zero"), 1)

            def gl_states(out):
                for h in range(4):
                    r = slice(64 * (h % 2), 64 * (h % 2) + 64)
                    c = (h // 2) * P + (h % 2) * 64
                    q = slice(32 * h, 32 * h + 32)
                    if out:
                        e.dma_start(OUT["hg"][:, h].rearrange("s k v -> k s v"), SG[r, :, c:c + 64]).then_inc(S("out"), 16)
                        e.dma_start(OUT["gl"][:, h].rearrange("s k v -> k s v"), SG[q, :, 256 + 64 * h:320 + 64 * h]).then_inc(S("out"), 16)
                    else:
                        e.dma_start(SG[r, 1:, c:c + 64], A["hg"][:, h].rearrange("s k v -> k s v")).then_inc(S("gl_in"), 16)
                        e.dma_start(SG[q, 1:, 256 + 64 * h:320 + 64 * h], A["gl"][:, h].rearrange("s k v -> k s v")).then_inc(S("gl_in"), 16)
            gl_states(False)
            e.wait_ge(S("gl_final"), 1)
            gl_states(True)
            e.wait_ge(S("out"), 22 * 16)
            barrier(e, 3)
            e.memset(RSTATE, 0.0).then_inc(S("rw_zero"), 1)
            e.wait_ge(S("rw_zero"), 1)
            e.dma_start(SHI, A["shift"]).then_inc(S("rw_w"), 16)
            e.dma_start(RWK, A["rw_wa"]).then_inc(S("rw_w"), 16)
            e.dma_start(RGU, A["rw_g"]).then_inc(S("rw_w"), 16)

            def rw_states(out):
                for h in range(4):
                    r = slice(64 * (h % 2), 64 * (h % 2) + 64)
                    c = (h // 2) * P + (h % 2) * 64
                    if out:
                        e.dma_start(OUT["rw"][:, h].rearrange("s k v -> k s v"), RSTATE[r, :, c:c + 64]).then_inc(S("out"), 16)
                    else:
                        e.dma_start(RSTATE[r, 1:, c:c + 64], A["rw"][:, h].rearrange("s k v -> k s v")).then_inc(S("rw_in"), 16)
            rw_states(False)
            e.wait_ge(S("shift_ready"), 1)
            e.dma_start(OUT["shift"], SHO).then_inc(S("out"), 16)
            e.wait_ge(S("rw_final"), 1)
            rw_states(True)
            e.wait_ge(S("out"), 27 * 16)
            barrier(e, 4)
            def wb(j, u):
                e.dma_start(WB[:, u], A["w_br"][bass.ds(j, 1)].rearrange("o p k c -> (o p) k c")).then_inc(S(f"wb{u}"), 16)

            def zrow(r, u):
                e.dma_start(GZ[:, u], A["gates"][bass.ds(r, 1)].rearrange("o p t -> (o p) t")).then_inc(S(f"z{u}"), 16)
            e.wait_ge(S("gt_sent"), (1 + 4 * KD) * 16)
            for u in range(2):
                wb(u, u)
                zrow(u, u)
            for k in range(KD):
                e.dma_start(XR[:, k, :], xs[k]).then_inc(S("xr"), 16)
            for c in range(2, 8):
                e.wait_ge(S(f"mul{c % 2}"), c // 2 + 1)
                zrow(c, c % 2)
            with e.Fori(1, 4) as jj:
                for c in range(8):
                    if c % 4 == 0:
                        e.wait_ge(S(f"wb_used{c // 4}"), jj)
                        wb(jj * 2 + c // 4, c // 4)
                    e.wait_ge(S(f"mul{c % 2}"), jj * 4 + (c // 2 + 1))
                    zrow(jj * 8 + c, c % 2)
            e.wait_ge(S("xr_ready"), 8)
            for k in range(KD):
                e.dma_start(A["x2"][k], XR[:, k, :]).then_inc(S("spilled"), 16)
            e.wait_ge(S("spilled"), 16 * KD)
            barrier(e, 5)
            barrier(e, 6)
            for k in range(KD):
                if k >= 2:
                    e.wait_ge(S("res_used"), k - 1)
                e.dma_start(XJ[:, k % 2], A["x2"][k]).then_inc(S(f"xj{k % 2}"), 16)

        @block.gpsimd
        def _(e):
            with nc.allow_non_contiguous_dma(reason="normalisers and stabilisers: a few hundred values"):
                pool_program(e)

        @block.tensor
        def _(e):
            e.wait_ge(S("consts"), 48)
            rms_pe(e, 0)
            e.wait_ge(S("ht_ready"), 1)
            e.wait_ge(S("ws"), 16)
            for g in range(3):
                for k in range(KD):
                    last = e.matmul(PS(3 + g, 0, GRP)[0:68], WS[:, k, :], HT[:, k, g * GRP:(g + 1) * GRP],
                                    start=k == 0, stop=k == KD - 1)
            last.then_inc(S("small"), 1)
            barrier(e, 1)
            for p in range(2):
                pe_pair(e, P_ML + p, P_ML + p)
            pe_vpair(e, P_ML + 2, P_ML + 2)
            e.wait_ge(S("ml_rows"), 1)
            e.wait_ge(S("banks_free1"), 3 + 1)
            for q, src in enumerate((RSC, RKH)):
                for g in range(3):
                    last = e.matmul(PS(3 * q + g, 0, GRP), const("sel4", 4), src[:, g * GRP:(g + 1) * GRP],
                                    start=True, stop=True)
            last.then_inc(S("ml_bc"), 1)
            for t in range(TILES + 1):
                w = P if t < TILES else LASTW
                last = e.transpose(PS(6)[0:w, 4 * t:4 * t + 4], RM[:, t * P:t * P + w], ident[0:4, 0:4])
            last.then_inc(S("ml_mt"), 1)
            e.wait_ge(S("ml_go"), 2)

            def ml_tile(n, w, last_tile):
                v = VA[0:w, bass.ds(n, 1)].rearrange("p o h c -> p (o h) c") if not last_tile else VA[0:w, TILES]
                bd4 = const("bd4_l" if last_tile else "bd4", 4)
                e.wait_ge(S("ml_copied"), n + 1)
                e.wait_ge(S("ml_gbd"), n + 1)
                mqh = MQH.rearrange("p h t -> p (h t)")[:, 0:4 * w]
                e.matmul(PS(0, 0, 4 * w)[0:w], MC[:, 1, 0:w], mqh, start=True, stop=True)
                gbd = GBD.rearrange("p h t -> p (h t)")[:, 0:4 * w]
                e.matmul(PS(1, 0, 4 * w)[0:w], ones[0:4, 0:w], gbd, start=True, stop=False)
                e.matmul(PS(1, 0, 4 * w)[0:w], GST[:, 0:w], bd4, start=False, stop=True).then_inc(S("ml_s"), 1)
                e.transpose(PS(2, 0, P)[0:w], MC[:, 3, 0:w], ident).then_inc(S("ml_kt"), 1)
                e.wait_ge(S("ml_att"), n + 1)
                att = MATT.rearrange("p h t -> p (h t)")
                for h in range(4):
                    e.matmul(PS(3, h * 65, h * 65 + 65)[0:w], att[0:w, h * w:h * w + w], v[:, h, :],
                             start=h == 0, stop=False, skip_group_check=True)
                if last_tile:
                    e.wait_ge(S("ml_qx"), 1)
                    for s in range(SEGS):
                        last = e.matmul(PS(3, 0, 260)[0:w], MQX[:, s, :], SM[:, s, :], start=False, stop=s == SEGS - 1,
                                        skip_group_check=True)
                else:
                    last = e.matmul(PS(3, 0, 260)[0:w], MC[:, 2, 0:w], SM[:, 0, :], start=False, stop=True,
                                    skip_group_check=True)
                last.then_inc(S("ml_o"), 1)
                e.wait_ge(S("ml_kh"), n + 1)
                if last_tile:
                    e.wait_ge(S("ml_vx"), 1)
                    for s in range(SEGS):
                        b = [4, 5, 6, 7, 0][s // 2]
                        last = e.matmul(PS(b, (s % 2) * 256, (s % 2) * 256 + 256), MKH[0:w, :], MVX[0:w, s, 0:256],
                                        start=True, stop=True)
                    last.then_inc(S("ml_ds"), 1)
                    e.wait_ge(S("ml_dsu"), 1)
                    for s in range(SEGS):
                        last = e.matmul(PS(4, 4 * s, 4 * s + 4), MKH[0:w, :], MVX[0:w, s, 256:260], start=True, stop=True)
                    last.then_inc(S("ml_ds"), 1)
                else:
                    e.matmul(PS(4, 0, 260), MKH[0:w, :], v.rearrange("p h c -> p (h c)"), start=True, stop=True).then_inc(S("ml_ds"), 1)
                e.wait_ge(S("ml_on"), n + 1)
                for g in range(2):
                    last = e.transpose(PS(5, g * P, g * P + w), MON.rearrange("p h c -> p (h c)")[0:w, g * P:g * P + P],
                                       ident[0:w, 0:w])
                last.then_inc(S("ml_ot"), 1)

            with e.Fori(0, TILES) as n:
                ml_tile(n, P, False)
            ml_tile(TILES, LASTW, True)
            barrier(e, 2)
            with e.Fori(0, 5) as i:
                pe_pair(e, i + P_GL, i + P_GL)
            for q in range(2):
                pe_vpair(e, P_GL + 5 + q, P_GL + 5 + q)
            e.wait_ge(S("wga"), 16)
            for g in range(2):
                last = e.matmul(PS(6 + g, 0, GRP), WGA[0:16, :], GA[0:16, g * GRP:(g + 1) * GRP], start=True, stop=True)
            last.then_inc(S("gl_z"), 1)
            e.wait_ge(S("banks_free0"), 10 + 1)
            e.matmul(PS(0, 0, GRP), WGA[0:16, :], GA[0:16, 2 * GRP:W], start=True, stop=True).then_inc(S("gl_z"), 1)
            e.wait_ge(S("gl_go"), 1)

            def gl_tile(n, w, last_tile):
                x, q = (GXL, GEL) if last_tile else (GX, GE)
                halves = LHALVES if last_tile else HALVES
                nl = len(halves) + 1
                v = GV[0:w, TILES] if last_tile else GV[0:w, bass.ds(n, 1)].rearrange("p o c -> p (o c)")
                att = GATT.rearrange("p h t -> p (h t)")[0:w, 0:8 * w]
                gate = gate_work(e, n, P_G1, 0) if not last_tile else iter(())
                steps(gate, 8)
                for l in range(1, nl + 1):
                    if l < nl:
                        e.wait_ge(S("gl_qk"), n * 7 + l)
                    else:
                        e.wait_ge(S("gl_dk"), n + 1)
                    if l >= 3:
                        e.wait_ge(S("gl_att"), n * 8 + l - 2)
                    for a_ in (6, 0, 1, 2, 3, 4, 5, 7):
                        h = GL_ATT[a_]
                        if h < 4:
                            r, g = slice(64 * (h % 2), 64 * (h % 2) + 64), h // 2
                        else:
                            r, g = slice(32 * (h - 4), 32 * (h - 4) + 32), 2
                        m = w if l == nl else w // 2
                        o = (3 * (l % 2) + a_ // 3) * 512 + (a_ % 3) * m
                        if a_ == 7:
                            e.wait_ge(S("gl_third"), n * 8 + l)
                        if l < nl:
                            last = e.matmul(PSt[0:w, o:o + m], x[r, g, l, 0:w], half(x[r, g, l, 0:w], halves[l - 1], True),
                                            start=True, stop=True)
                        else:
                            last = e.matmul(PSt[0:w, o:o + m], x[r, g, nl + 1, 0:w], q[r, g, 1, 0:w], start=True, stop=True)
                        if a_ == 6:
                            last.then_inc(S("gl_third"), 1)
                    last.then_inc(S("gl_s"), 1)
                    steps(gate, 1)
                steps(gate, 1)
                e.wait_ge(S("gl_att"), n * 8 + nl)
                e.wait_ge(S("gl_qe"), n + 1)
                for g in range(3):
                    last = e.transpose(PS(2, g * P, g * P + P)[0:w], x[:, g, nl, 0:w], ident)
                last.then_inc(S("gl_kt"), 1)
                if last_tile:
                    e.wait_ge(S("gl_qx"), 1)
                for h in range(8):
                    ao = GL_ATT.index(h) * w
                    e.matmul(PS(3, h * 64, h * 64 + 64)[0:w], att[:, ao:ao + w], v[:, h * 64:h * 64 + 64],
                             start=h == 0, stop=False, skip_group_check=True)
                for g in range(3):
                    lo, hi = (g * P, g * P + P) if g < 2 else (256, 512)
                    ns = SEGS if last_tile else 1
                    for s in range(ns):
                        qs = GQX[:, g, s, :] if last_tile else q[:, g, 0, 0:w]
                        last = e.matmul(PS(3, lo, hi)[0:w], qs, SG[:, s, lo:hi], start=False, stop=s == ns - 1,
                                        skip_group_check=True)
                last.then_inc(S("gl_o"), 1)
                e.wait_ge(S("gl_kh"), n + 1)
                if last_tile:
                    for g in range(2):
                        e.wait_ge(S("gl_vx"), 2 * g + 1)
                        for s in range(SEGS):
                            b = [0, 1, 2][s // 4]
                            last = e.matmul(PS(b, (s % 4) * P, (s % 4) * P + P), GKH[0:w, g * P:g * P + P],
                                            GVX[0:w, s, 0:P], start=True, stop=True)
                        last.then_inc(S("gl_ds"), 1)
                        e.wait_ge(S("gl_dsu"), g + 1)
                    e.wait_ge(S("gl_vx"), 5)
                    for s in range(SEGS):
                        b = [0, 1, 2, 3, 4][s // 2]
                        last = e.matmul(PS(b, (s % 2) * 256, (s % 2) * 256 + 256), GKH[0:w, 2 * P:3 * P],
                                        GVX[0:w, s, :], start=True, stop=True)
                    last.then_inc(S("gl_ds"), 1)
                else:
                    for g in range(3):
                        lo, hi = (g * P, g * P + P) if g < 2 else (256, 512)
                        last = e.matmul(PS(4, lo, hi), GKH[0:w, g * P:g * P + P], v[:, lo:hi], start=True, stop=True)
                    last.then_inc(S("gl_ds"), 1)
                steps(gate, 3)
                e.wait_ge(S("gl_on"), n + 1)
                on = GON.rearrange("p h c -> p (h c)")
                for j in range(4):
                    last = e.transpose(PS(5, j * P, j * P + w), on[0:w, j * P:j * P + P], ident[0:w, 0:w])
                last.then_inc(S("gl_ot"), 1)
                steps(gate, 24)

            with e.Fori(0, TILES) as n:
                gl_tile(n, P, False)
            gl_tile(TILES, LASTW, True)
            barrier(e, 3)
            with e.Fori(0, 4) as i:
                pe_pair(e, i + P_RW, i + EV_RW)
            e.wait_ge(S("rw_w"), 48)
            e.wait_ge(S("rw_lora"), 1)
            e.wait_ge(S("banks_free0"), 14 + 1)
            e.wait_ge(S("banks_free1"), 14 + 1)
            c = 0
            for kind in range(3):
                for g in range(2):
                    if c >= 2:
                        e.wait_ge(S("rw_lev"), c - 1)
                    for tg in range(3):
                        rows = [slice(0, 64), slice(64, 128), slice(0, 128)][kind]
                        wl = (RGU if kind == 2 else RWK)[rows, g * P:g * P + P]
                        src = R10[rows, 7 if kind == 2 else 6, tg * GRP:(tg + 1) * GRP]
                        last = e.matmul(PS(3 * (c % 2) + tg, 0, GRP), wl, src, start=True, stop=True)
                    last.then_inc(S("rw_lor"), 1)
                    c += 1
            for kind in range(2):
                for g in range(2):
                    e.wait_ge(S("rw_lev"), c - 1)
                    e.wait_ge(S("rw_hs"), 2 * kind + g + 1)
                    for tg in range(3):
                        last = e.matmul(PS(3 * (c % 2) + tg, 0, GRP), bd2, RX[:, g, tg * GRP:(tg + 1) * GRP],
                                        start=True, stop=True)
                    last.then_inc(S("rw_lor"), 1)
                    c += 1
            e.wait_ge(S("rw_go"), 1)

            def rw_tile(n, w, last_tile):
                levels = LHALVES if last_tile else HALVES
                gate = gate_work(e, n, P_G2, TILES) if not last_tile else iter(())
                e.wait_ge(S("rw_copied"), n + 1)
                for h in range(4):
                    r, g = slice(64 * (h % 2), 64 * (h % 2) + 64), h // 2
                    rhs = RC[r, g:g + 3:2, 0:w]
                    e.matmul(PS(h % 2, g * 2 * w, (g + 1) * 2 * w)[0:w], RC[r, 6 + g, 0:w], rhs, start=True, stop=True)
                    e.matmul(PS(2 + h % 2, g * 2 * w, (g + 1) * 2 * w)[0:w], RC[r, 4 + g, 0:w], rhs, start=True, stop=True)
                    last = e.matmul(PS(4 + h % 2, g * w, g * w + w)[0:w], RC[r, g, 0:w], RC[r, 6 + g, 0:w], start=True, stop=True)
                last.then_inc(S("rw_s"), 1)
                steps(gate, 3)
                tt, ti, m1 = (x.rearrange("p h t -> p (h t)") for x in (RTT, RTI, RM1))
                pb = RPB.rearrange("p h k t -> p (h k t)")
                pk = RPK.rearrange("p h k t -> p (h k t)")
                e.wait_ge(S("rw_t"), n * 14 + 2)
                nlev = len(levels)
                for l in range(1, nlev):
                    lh, m = levels[l], w // 2
                    for h in range(4):
                        last = e.matmul(PS(4, h * m, h * m + m)[0:w], pb[0:w, 2 * h * w:2 * h * w + w],
                                        half(ti[0:w, h * w:h * w + w], lh, False), start=True, stop=True)
                    last.then_inc(S("rw_m"), 1)
                    steps(gate, 1)
                    e.wait_ge(S("rw_m1"), n * 6 + l)
                    for h in range(4):
                        last = e.matmul(PS(0, h * m, h * m + m)[0:w], m1[0:w, h * w:h * w + w],
                                        half(tt[0:w, h * w:h * w + w], lh, True), start=True, stop=True)
                    last.then_inc(S("rw_n"), 1)
                    for h in range(4):
                        last = e.matmul(PS(1, h * m, h * m + m)[0:w], tt[0:w, h * w:h * w + w],
                                        half(m1[0:w, h * w:h * w + w], lh, False), start=True, stop=True)
                    last.then_inc(S("rw_n"), 1)
                    if l == 1:
                        for j in range(4):
                            e.transpose(PS(2, j * P, j * P + P)[0:w], RC[:, 4 + j, 0:w], ident)
                        for j in range(2):
                            last = e.transpose(PS(3, j * P, j * P + P)[0:w], RC[:, 8 + j, 0:w], ident)
                        last.then_inc(S("rw_kt"), 1)
                    steps(gate, 1)
                    e.wait_ge(S("rw_t"), n * 14 + 2 + 2 * l)
                e.wait_ge(S("rw_kv"), n + 1)
                if last_tile:
                    e.wait_ge(S("rw_qx"), 1)
                for k in range(2):
                    bank = 4 if k == 0 else 1
                    if k == 1:
                        steps(gate, 1)
                        e.wait_ge(S("rw_r"), n + 1)
                        for h in range(4):
                            last = e.matmul(PS(5, h * 64, h * 64 + 64)[0:w], tt[0:w, h * w:h * w + w], RRS[0:w, h * 64:h * 64 + 64],
                                            start=True, stop=True)
                        last.then_inc(S("rw_u"), 1)
                    for h in range(4):
                        o = (2 * h + k) * w
                        e.matmul(PS(bank, h * 64, h * 64 + 64)[0:w], pk[0:w, o:o + w], RV[0:w, h * 64:h * 64 + 64],
                                 start=h == 0, stop=False, skip_group_check=True)
                    if k == 1:
                        steps(gate, 1)
                        e.wait_ge(S("rw_us"), n + 1)
                        for h in range(4):
                            o = (2 * h + 1) * w
                            e.matmul(PS(1, h * 64, h * 64 + 64)[0:w], pb[0:w, o:o + w], RUS[0:w, h * 64:h * 64 + 64],
                                     start=False, stop=False, skip_group_check=True)
                    ns = SEGS if last_tile else 1
                    for g in range(2):
                        for s in range(ns):
                            lh = RQX[:, k, g, s, :] if last_tile else RC[:, 2 * k + g, 0:w]
                            x0 = RSTATE[:, s, g * P:g * P + P] if last_tile else RXC[:, g * P:g * P + P]
                            last = e.matmul(PS(bank, g * P, g * P + P)[0:w], lh, x0, start=False, stop=s == ns - 1,
                                            skip_group_check=True)
                    last.then_inc(S("rw_rhs" if k == 0 else "rw_y"), 1)
                if last_tile:
                    e.wait_ge(S("rw_vx"), 1)
                    for g in range(2):
                        for s in range(SEGS):
                            b = [0, 1, 2][s // 4]
                            e.matmul(PS(b, (s % 4) * P, (s % 4) * P + P), RKB[0:w, g * P:g * P + P], RVX[0:w, s, g * P:g * P + P],
                                     start=True, stop=False)
                            last = e.matmul(PS(b, (s % 4) * P, (s % 4) * P + P), RKB[0:w, 256 + g * P:256 + g * P + P],
                                            RUX[0:w, s, g * P:g * P + P], start=False, stop=True)
                        last.then_inc(S("rw_ds"), 1)
                        if g == 0:
                            e.wait_ge(S("rw_dsu"), 1)
                else:
                    for g in range(2):
                        e.matmul(PS(0, g * P, g * P + P), RKB[:, g * P:g * P + P], RV[:, g * P:g * P + P], start=True, stop=False)
                        last = e.matmul(PS(0, g * P, g * P + P), RKB[:, 256 + g * P:256 + g * P + P], RUS[:, g * P:g * P + P],
                                        start=False, stop=True)
                    last.then_inc(S("rw_ds"), 1)
                steps(gate, 3)
                e.wait_ge(S("rw_on"), n + 1)
                for g in range(2):
                    last = e.transpose(PS(3, g * P, g * P + w), RY.rearrange("p h c -> p (h c)")[0:w, g * P:g * P + P],
                                       ident[0:w, 0:w])
                last.then_inc(S("rw_ot"), 1)
                steps(gate, 24)

            with e.Fori(0, TILES) as n:
                rw_tile(n, P, False)
            rw_tile(TILES, LASTW, True)
            barrier(e, 4)
            with e.Fori(0, 4) as jj:
                for v in range(2):
                    e.wait_ge(S(f"wb{v}"), (jj + 1) * 16)
                    for br in range(4):
                        u, c = br % 2, 4 * v + br
                        e.wait_ge(S(f"mul{u}"), jj * 4 + (c // 2 + 1))
                        for tg in range(3):
                            for k in range(2):
                                last = e.matmul(PS(3 * u + tg, 0, GRP), WB[:, v, 2 * br + k, :],
                                                OT[:, 2 * br + k, tg * GRP:(tg + 1) * GRP], start=k == 0, stop=k == 1)
                        last.then_inc(S(f"pz{u}"), 1)
                    e.drain().then_inc(S(f"wb_used{v}"), 1)
            e.wait_ge(S("mix_ready"), 1)
            with e.Fori(0, 4) as i:
                for u in range(2):
                    e.wait_ge(S(f"chunk_loaded{u}"), (i + P_OUT + 1) * 16)
                    e.wait_ge(S(f"banks_free{u}"), i + EV_OUT + 1)
                    for g in range(3):
                        for k in range(KD):
                            last = e.matmul(PS(3 * u + g, 0, GRP), RING[:, u, k, :], MIX[:, k, g * GRP:(g + 1) * GRP],
                                            start=k == 0, stop=k == KD - 1)
                    last.then_inc(S(f"chunk_done{u}"), 1)
            e.wait_ge(S("banks_free0"), EV_OUT + 5)
            rms_pe(e, 1)
            barrier(e, 5)
            def up(p, ev):
                for u in range(2):
                    e.wait_ge(S(f"chunk_loaded{u}"), (p + 1) * 16)
                    e.wait_ge(S(f"banks_free{u}"), ev + 1)
                    for g in range(3):
                        for k in range(KD):
                            last = e.matmul(PS(3 * u + g, 0, GRP), RING[:, u, k, :], HN2[:, k, g * GRP:(g + 1) * GRP],
                                            start=k == 0, stop=k == KD - 1)
                    last.then_inc(S(f"chunk_done{u}"), 1)
            with e.Fori(0, 16) as i:
                up(i + P_UP, i + EV_UP)
            barrier(e, 6)
            with e.Fori(0, 4) as jj:
                for v in range(2):
                    e.wait_ge(S(f"down_used{v}"), jj + 1)
                    for c in range(4):
                        u = c % 2
                        e.wait_ge(S(f"chunk_loaded{u}"), (jj * 4 + (P_DOWN + 2 * v + c // 2 + 1)) * 16)
                        for k in range(KD):
                            kk = c * KD + k
                            src = ACTA[:, kk] if kk < 24 else HT[:, kk - 24]
                            for g in range(3):
                                last = e.matmul(PS(3 * v + g, 0, GRP), RING[:, u, k, :], src[:, g * GRP:(g + 1) * GRP],
                                                start=kk == 0, stop=kk == 31)
                        if c < 3:
                            last.then_inc(S(f"chunk_done{u}"), 1)
                        else:
                            last.then_inc(S(f"down{v}"), 1)
                            e.drain().then_inc(S(f"chunk_done{u}"), 1)
            e.wait_ge(S("down_used0"), 5)
            rms_pe(e, 2)

        @block.scalar
        def _(e):
            st = Steps(e, S("act_step"))
            e.dma_start(WGA[0:16, :], A["w_ga"]).then_inc(S("wga"), 16)
            rms_act(e, st, 0, RST, XT, lambda k: e.wait_ge(S(f"x{k}"), 16))
            e.wait_ge(S("small"), 1)
            e.activation(row3(GA[0:16, :]), cols3(3)[0:16], ACT.Copy)
            st.did(e.activation(row3(GA[32:36, :]), cols3(3)[32:36], ACT.Copy))
            st.did(e.activation(row3(GA[64:68, :]), cols3(3)[64:68], ACT.Copy))
            barrier(e, 1)
            e.sem_inc(S("banks_free0"), 1)
            e.sem_inc(S("gt_free"), 2)
            e.sem_inc(S("gt_sent"), 16)
            e.wait_ge(S("ml_zero"), 1)
            e.wait_ge(S("ml_in"), 11 * 16)
            fdec = FP[:, :, NP + 3:].rearrange("p g (q c) -> p g q c", q=NSEQ)

            def pre_conv(g):
                def emit(b):
                    lo = 2 * GRP
                    e.activation(FP[:, g, 3:3 + lo].rearrange("p (g c) -> p g c", g=2), cols3(b)[:, 0:2], ACT.Copy)
                    e.activation(FP[:, g, 3 + lo:3 + NP], PS(b + 2, 0, NP - lo), ACT.Copy)
                    return e.activation(fdec[:, g, :, 3:3 + DSEQ],
                                        PS(b + 2, NP - lo, NT - lo).rearrange("p (q c) -> p q c", q=NSEQ), ACT.Copy)
                return emit
            e.activation(RI, GA[32:36, :], ACT.Copy)
            st.did(e.activation(RF, GA[64:68, :], ACT.Copy))
            st.settle()
            e.activation(RI, RI, ACT.Identity, bias=col("mlstm_i_b", 0, 4))
            e.activation(RF, RF, ACT.Identity, bias=col("mlstm_f_b", 0, 4)).then_inc(S("ml_if"), 1)
            evac(e, 0, 0, pre_conv(0))
            e.wait_ge(S("chunk_done1"), 1)
            ins = pre_conv(1)(3)
            ins.then_inc(S("banks_free1"), 1)
            e.wait_ge(S("banks_free1"), 1 + 1)
            e.wait_ge(S("banks_free0"), 1 + 1)
            e.sem_inc(S("conv_ready"), 1)
            for u in range(2):
                evac(e, u, 1, lambda b: e.activation(row3(OT[:, 6 + u, :]), cols3(b), ACT.Sigmoid))
            e.wait_ge(S("ml_if"), 1)
            st.did(e.activation(RT, RF, ACT.Abs))
            st.settle()
            st.did(e.activation(RT, RT, ACT.Exp, scale=-1.0))
            st.settle()
            e.activation(RT, RT, ACT.Ln, bias=1.0).then_inc(S("ml_ln"), 1)
            for u in range(2):
                evac_v(e, u, 2, lambda t: VA[:, 0:TILES, 2 * u:2 * u + 2, 0:64] if t == 0
                       else VA[0:LASTW, TILES, 2 * u:2 * u + 2, 0:64], True)
            e.wait_ge(S("ml_conv"), 1)
            e.activation(M4[:, 0:2, 0:NT], M4[:, 0:2, 0:NT], ACT.Silu).then_inc(S("ml_silu"), 1)
            e.wait_ge(S("ml_bc"), 1)
            e.wait_ge(S("ml_mt"), 1)
            for q in range(2):
                e.activation(row3(M4[:, 2 + q, :]), cols3(3 * q), ACT.Exp)
            mt = PS(6, 0, 36).rearrange("p (t h) -> p t h", h=4)
            e.activation(EMM[:, 0:TILES], mt[:, 0:TILES], ACT.Exp, scale=-1.0)
            e.activation(EMM[0:LASTW, TILES], mt[0:LASTW, TILES], ACT.Exp, scale=-1.0).then_inc(S("ml_sc"), 1)
            e.wait_ge(S("ml_go"), 2)

            def ml_tile(n, w, last_tile):
                src = M4[:, :, TILES * P:NT] if last_tile else M4[:, :, bass.ds(n * P, P)]
                if not last_tile:
                    e.wait_ge(S("ml_pre"), n + 1)
                else:
                    e.wait_ge(S("ml_pre"), TILES + 1)
                e.activation(MC[:, :, 0:w], src, ACT.Copy).then_inc(S("ml_copied"), 1)
                e.wait_ge(S("ml_kt"), n + 1)
                e.activation(MKH[0:w, :], PS(2, 0, P)[0:w], ACT.Copy).then_inc(S("ml_kh"), 1)
                x = MX.rearrange("p h t -> p (h t)")[0:w, 0:4 * w]
                e.wait_ge(S("ml_x"), n + 1)
                e.activation(x, x, ACT.Exp).then_inc(S("ml_e"), 1)
                e.wait_ge(S("ml_o"), n + 1)
                num = PS(3, 0, 260).rearrange("p (h c) -> p h c", h=4)[0:w, :, 0:64]
                e.activation(MSQ[0:w], num, ACT.Square, scale=0.125).then_inc(S("ml_sq"), 1)
                e.wait_ge(S("ml_ms"), n + 1)
                rstd(e, st, MS[0:w, 6], MS[0:w, 5]).then_inc(S("ml_rs"), 1)
            with e.Fori(0, TILES) as n:
                st.enter(n, 1)
                ml_tile(n, P, False)
            st.leave(TILES)
            ml_tile(TILES, LASTW, True)
            barrier(e, 2)
            evac(e, 0, 3, lambda b: e.activation(row3(GQ[:, 0]), cols3(b), ACT.Copy))
            evac(e, 0, 4, lambda b: e.activation(row3(GB[:, 0]), cols3(b), ACT.Copy))
            for u in range(2):
                evac(e, u, 5, lambda b: e.activation(row3(OT[:, u]), cols3(b), ACT.Silu))
            evac(e, 0, 6, lambda b: e.activation(row3(GQ[:, 2]), cols3(b), ACT.Copy, scale=32 ** -0.5))
            for u in range(2):
                evac(e, u, 7, lambda b: e.activation(row3(OT[:, 4 + u]), cols3(b), ACT.Silu))
            for q in range(2):
                evac_v(e, 0, 8 + q, lambda t: GV[:, 0:TILES, 256 * q:256 * q + P] if t == 0
                       else GV[0:LASTW, TILES, 256 * q:256 * q + P], True)
            e.wait_ge(S("gl_z"), 2)
            e.activation(GB[:, 2, 0:2 * GRP].rearrange("p (g c) -> p g c", g=2),
                         PSt[:, 6 * 512:].rearrange("p (g c) -> p g c", g=2)[:, :, 0:GRP], ACT.Identity, bias=col("gla_gate_b"))
            e.activation(GB[:, 2, 2 * GRP:W], PS(0, 0, GRP), ACT.Identity, bias=col("gla_gate_b")).then_inc(S("gl_zz"), 1)
            e.wait_ge(S("gl_f"), 1)
            e.activation(GK[:, 0:2], GB[:, 0:2], ACT.Sigmoid, scale=-1.0)
            e.wait_ge(S("gl_zz"), 1)
            st.did(e.activation(GT, GB, ACT.Abs))
            st.settle()
            st.did(e.activation(GT, GT, ACT.Exp, scale=-1.0))
            st.settle()
            e.activation(GT, GT, ACT.Ln, bias=1.0).then_inc(S("gl_ln"), 1)

            def gl_tile(n, w, last_tile):
                x, q = (GXL, GEL) if last_tile else (GX, GE)
                nl = len(LHALVES if last_tile else HALVES) + 1

                def tile_of(y):
                    return y[:, :, TILES * P:NT] if last_tile else y[:, :, bass.ds(n * P, P)]
                e.wait_ge(S("gl_x"), 2 * n + 1)
                e.activation(x[:, :, 1:nl, :], x[:, :, 1:nl, :], ACT.Exp).then_inc(S("gl_e"), 1)
                e.wait_ge(S("gl_x"), 2 * n + 2)
                e.activation(x[:, :, 0:nl + 1:nl, :], x[:, :, 0:nl + 1:nl, :], ACT.Exp).then_inc(S("gl_e"), 1)
                e.activation(x[:, :, nl + 1, :], tile_of(GK), ACT.Copy)
                e.activation(q[:, :, 1, :], tile_of(GQ), ACT.Copy).then_inc(S("gl_dk"), 1)
                if not last_tile:
                    for c in range(4):
                        gate_out(e, n, c, 0)
                e.wait_ge(S("gl_kt"), n + 1)
                e.activation(GKH[0:w, :], PS(2, 0, 3 * P)[0:w], ACT.Copy).then_inc(S("gl_kh"), 1)
                e.wait_ge(S("gl_o"), n + 1)
                e.activation(GSQ.rearrange("p h c -> p (h c)")[0:w], PS(3)[0:w], ACT.Square, scale=0.125).then_inc(S("gl_sq"), 1)
                e.wait_ge(S("gl_ms"), n + 1)
                rstd(e, st, GMS[0:w, 1], GMS[0:w, 0]).then_inc(S("gl_rs"), 1)
                if not last_tile:
                    for c in range(4, 6):
                        gate_out(e, n, c, 0)
            with e.Fori(0, TILES) as n:
                st.enter(n, 1)
                gl_tile(n, P, False)
            st.leave(TILES)
            gl_tile(TILES, LASTW, True)
            barrier(e, 3)
            with e.Fori(0, 4) as i:
                e.wait_ge(S("chunk_done0"), i + P_RW + 1)
                e.activation(row3(R10[:, bass.ds(i * 2, 1), :].rearrange("p o t -> p (o t)")), cols3(0),
                             ACT.Copy).then_inc(S("banks_free0"), 1)
            e.wait_ge(S("rw_mix"), 1)
            e.activation(R10[0:64, 6, :], R10[0:64, 6, :], ACT.Tanh)
            e.activation(R10[:, 7, :], R10[:, 7, :], ACT.Sigmoid).then_inc(S("rw_lora"), 1)
            for c in range(6):
                e.wait_ge(S("rw_lor"), c + 1)
                g, src = c % 2, cols3(3 * (c % 2))
                dst = (RWL, RA)[c // 2][:, g] if c < 4 else OT[:, 2 + g]
                if c < 2:
                    e.activation(row3(dst), src, ACT.Sigmoid, bias=col("rwkv_w0", g)).then_inc(S("rw_lev"), 1)
                elif c < 4:
                    e.activation(row3(dst), src, ACT.Sigmoid, bias=col("rwkv_a0", g)).then_inc(S("rw_lev"), 1)
                else:
                    e.activation(row3(dst), src, ACT.Copy).then_inc(S("rw_lev"), 1)
            e.wait_ge(S("rw_kkr"), 1)
            for g in range(2):
                e.activation(RX[:, g], RKK[:, g], ACT.Square).then_inc(S("rw_hs"), 1)
            for g in range(2):
                e.wait_ge(S("rw_lor"), 7 + g)
                e.activation(row3(RE[:, g]), cols3(3 * g), ACT.Sqrt).then_inc(S("rw_lev"), 1)
            e.wait_ge(S("rw_wlx"), 1)
            e.activation(REC, RCS, ACT.Exp, scale=-DECAY)
            e.activation(RE, RWL, ACT.Exp, scale=-DECAY).then_inc(S("rw_ex"), 1)
            e.wait_ge(S("rw_ex_used"), 1)
            e.activation(RE, RWL, ACT.Exp, scale=DECAY).then_inc(S("rw_ex"), 1)
            e.wait_ge(S("rw_ex_used"), 2)
            e.activation(RE, RX, ACT.Exp, scale=-DECAY).then_inc(S("rw_ex"), 1)
            e.wait_ge(S("rw_go"), 1)

            def rw_tile(n, w, last_tile):
                src = R10[:, :, TILES * P:NT] if last_tile else R10[:, :, bass.ds(n * P, P)]
                e.wait_ge(S("rw_pre"), n + 1)
                e.activation(RC[:, :, 0:w], src, ACT.Copy).then_inc(S("rw_copied"), 1)
                levels = LHALVES if last_tile else HALVES
                nlev = len(levels)
                m1 = RM1.rearrange("p h t -> p (h t)")[0:w, 0:4 * w].rearrange("p (h t) -> p h t", h=4)
                for l in range(1, nlev):
                    e.wait_ge(S("rw_m"), n * 6 + l)
                    h = levels[l]
                    e.activation(half(m1, h, False), PS(4, 0, 2 * w)[0:w].rearrange("p (a n t) -> p a n t", a=4, t=h),
                                 ACT.Copy).then_inc(S("rw_m1"), 1)
                    if l % 2 and not last_tile:
                        gate_out(e, n, l // 2, TILES)
                    if l == 1:
                        e.wait_ge(S("rw_kt"), n + 1)
                        e.activation(RKB[0:w], PS(2)[0:w], ACT.Copy)
                        e.activation(RV[0:w], PS(3, 0, 256)[0:w], ACT.Copy).then_inc(S("rw_kv"), 1)
                e.wait_ge(S("rw_rhs"), n + 1)
                e.activation(RRS[0:w], PS(4, 0, 256)[0:w], ACT.Copy).then_inc(S("rw_r"), 1)
                e.wait_ge(S("rw_u"), n + 1)
                e.activation(RUS[0:w], PS(5, 0, 256)[0:w], ACT.Copy).then_inc(S("rw_us"), 1)
                if not last_tile:
                    gate_out(e, n, 3, TILES)
                e.wait_ge(S("rw_yc"), n + 1)
                e.activation(RSQ[0:w], RY[0:w], ACT.Square, scale=0.125).then_inc(S("rw_sq"), 1)
                e.wait_ge(S("rw_ms"), n + 1)
                rstd(e, st, RMS_[0:w, 3], RMS_[0:w, 2], LN_EPS).then_inc(S("rw_rs"), 1)
                if not last_tile:
                    for c in range(4, 6):
                        gate_out(e, n, c, TILES)
            with e.Fori(0, TILES) as n:
                st.enter(n, 1)
                rw_tile(n, P, False)
            st.leave(TILES)
            rw_tile(TILES, LASTW, True)
            barrier(e, 4)
            with e.Fori(0, 4) as jj:
                for c in range(8):
                    u = c % 2
                    e.wait_ge(S(f"z{u}"), (jj * 4 + (c // 2 + 1)) * 16)
                    e.activation(GZ[:, u], GZ[:, u], ACT.Sigmoid).then_inc(S(f"sig{u}"), 1)
            rms_act(e, st, 1, RST2, XR, lambda k: e.wait_ge(S("xr_ready"), k + 1))
            barrier(e, 5)
            for r, (lo, n, base) in enumerate(((0, 12, ACTA), (12, 4, HT))):
                with e.Fori(0, n) as i:
                    for u in range(2):
                        e.wait_ge(S(f"chunk_done{u}"), i + (P_UP + lo + 1))
                        dst = base[:, bass.ds(i * 2 + u, 1), :].rearrange("p o t -> p (o t)")
                        e.activation(row3(dst), cols3(3 * u), ACT.Relu).then_inc(S(f"banks_free{u}"), 1)
            barrier(e, 6)
            e.wait_ge(S("dn_ready"), KD)
            rms_act(e, st, 2, SQ3R, HN2)

        @block.vector
        def _(e):
            st = Steps(e, S("dve_step"))
            e.wait_ge(S("consts"), 48)
            e.tensor_copy(CU[:, :], CUF)
            rms_dve(e, 0, RST, XT, HT, "norm_mix").then_inc(S("ht_ready"), 1)
            barrier(e, 1)
            e.sem_inc(S("banks_free1"), 1)
            e.sem_inc(S("down_used0"), 1)
            e.sem_inc(S("mul0"), 1)
            e.sem_inc(S("mul1"), 1)
            e.sem_inc(S("down_used1"), 1)
            e.sem_inc(S("ml_pre"), 1)
            e.sem_inc(S("rw_pre"), 1)
            e.wait_ge(S("ml_if"), 1)
            e.wait_ge(S("ml_ln"), 1)
            st.did(e.scalar_tensor_tensor(RF, RF, 0.0, RT, ALU.min, ALU.subtract))
            st.settle()
            e.wait_ge(S("ml_zero"), 1)
            e.wait_ge(S("ml_in"), 11 * 16)
            e.memset(RM[:, NT:W], 0.0)
            st.did(e.tensor_tensor_scan(RB, keep[0:4], RF, 0.0, ALU.mult, ALU.add))
            st.did(e.tensor_tensor_scan(RM[:, 0:NP], RF[:, 0:NP], RI[:, 0:NP], 0.0, ALU.add, ALU.max))

            def dec(x, k=None):
                x = x[:, NP:NT].rearrange("p (q c) -> p q c", q=NSEQ)
                return x if k is None else x[:, :, k]
            for k in range(DSEQ):
                prev = RM0[:, 12:20] if k == 0 else dec(RM, k - 1)
                st.did(e.tensor_tensor(dec(RM, k), dec(RF, k), prev, ALU.add))
                st.settle()
                st.did(e.tensor_tensor(dec(RM, k), dec(RM, k), dec(RI, k), ALU.max))
                st.settle()
            ends = RM[:, 0:TILES * P].rearrange("p (n t) -> p n t", t=P)[:, :, P - 1]
            st.did(e.tensor_copy(RM0[:, 1:TILES + 1], ends))
            e.tensor_tensor(RNG, RB, RM, ALU.subtract)
            st.did(e.tensor_tensor(RG, RI, RB, ALU.subtract))
            st.settle()

            def parts(x):
                return (x[:, 0:TILES * P].rearrange("p (n t) -> p n t", t=P),
                        x[:, TILES * P:NP].rearrange("p (n t) -> p n t", n=1),
                        x[:, NP:NT].rearrange("p (n t) -> p n t", t=DSEQ))
            m0s = (RM0[:, 0:TILES], RM0[:, TILES:TILES + 1], RM0[:, 12:20])
            e.memset(RSC[:, NT:W], 0.0)
            e.memset(RKH[:, NT:W], 0.0)
            for q in range(3):
                o, x = parts(RSC)[q], parts(RNG)[q]
                e.tensor_tensor(o, x, bc(m0s[q].unsqueeze(2), x.shape), ALU.add)
                o, x, y = parts(RKH)[q], parts(RG)[q], parts(RNG)[q]
                ins = e.tensor_tensor(o, x, bc(y[:, :, x.shape[2] - 1:x.shape[2]], x.shape), ALU.add)
            ins.then_inc(S("ml_rows"), 1)
            e.wait_ge(S("banks_free0"), 2)
            e.wait_ge(S("banks_free1"), 2)
            fdec = FP[:, :, NP + 3:].rearrange("p g (q c) -> p g q c", q=NSEQ)
            e.sem_inc(S("conv_ready"), 1)
            for j in range(4):
                for g in range(2):
                    cw = col("mlstm_conv_w", 2 * j + g)
                    po, pi = M4[:, g, 0:NP], FP[:, g, j:j + NP]
                    do, di = dec(M4[:, g]), fdec[:, g, :, j:j + DSEQ]
                    if j == 0:
                        e.tensor_scalar(po, pi, cw, col("mlstm_conv_b", g), ALU.mult, ALU.add)
                        ins = e.tensor_scalar(do, di, cw, col("mlstm_conv_b", g), ALU.mult, ALU.add)
                    else:
                        e.scalar_tensor_tensor(po, pi, cw, po, ALU.mult, ALU.add)
                        ins = e.scalar_tensor_tensor(do, di, cw, do, ALU.mult, ALU.add)
                if j < 3:
                    st.did(ins)
                    st.settle()
            ins.then_inc(S("ml_conv"), 1)
            e.wait_ge(S("ml_silu"), 1)
            st.did(e.tensor_scalar(M4[:, 1, :], M4[:, 1, :], 32 ** -0.5, None, ALU.mult))
            e.wait_ge(S("ml_sc"), 1)
            ins = e.tensor_copy(MSL[:, 0:TILES], M4[:, 2, 0:TILES * P].rearrange("p (n t) -> p n t", t=P)[:, :, P - 1])
            e.tensor_copy(MES[:, 0:1], M4[:, 2, NP - 1:NP])
            st.did(e.tensor_copy(MES[:, 1:], dec(M4[:, 2])[:, :, DSEQ - 1]))
            st.settle()
            e.tensor_tensor(M4[:, 2, :], M4[:, 2, :], M4[:, 0, :], ALU.mult)
            e.tensor_tensor(M4[:, 3, :], M4[:, 3, :], M4[:, 1, :], ALU.mult).then_inc(S("ml_go"), 2)

            def ml_tile(n, w, last_tile):
                def tile_of(x):
                    return x[:, TILES * P:NT] if last_tile else x[:, bass.ds(n * P, P)]
                bd4 = const("bd4_l" if last_tile else "bd4", 4).rearrange("p (h t) -> p h t", h=4)
                neg = const("neg_l" if last_tile else "neg", w)
                h4 = [w, 4, w]
                gbd = GBD.rearrange("p h t -> p (h t)")[:, 0:4 * w].rearrange("p (h t) -> p h t", h=4)
                mqh = MQH.rearrange("p h t -> p (h t)")[:, 0:4 * w].rearrange("p (h t) -> p h t", h=4)
                e.tensor_tensor(mqh, bc(tile_of(M4[:, 0]).unsqueeze(1), [P, 4, w]),
                                bc(const("head4").unsqueeze(2), [P, 4, w]), ALU.mult)
                e.tensor_tensor(gbd, bc(tile_of(RNG).unsqueeze(1), [4, 4, w]), bd4, ALU.mult)
                e.tensor_copy(GST[:, 0:w], tile_of(RG)).then_inc(S("ml_gbd"), 1)
                x = MX.rearrange("p h t -> p (h t)")[0:w, 0:4 * w].rearrange("p (h t) -> p h t", h=4)
                att = MATT.rearrange("p h t -> p (h t)")[0:w, 0:4 * w].rearrange("p (h t) -> p h t", h=4)
                pq = [PS(k, 0, 4 * w)[0:w].rearrange("p (h t) -> p h t", h=4) for k in range(2)]
                if last_tile:
                    e.wait_ge(S("ml_copied"), TILES + 1)
                    e.tensor_tensor(MQX, bc(MC[:, 2, 0:w].unsqueeze(1), [P, SEGS, w]),
                                    const("ind_t").rearrange("p (s t) -> p s t", s=SEGS), ALU.mult).then_inc(S("ml_qx"), 1)
                    for s in range(SEGS):
                        ins = e.tensor_scalar(MVX[0:w, s, :], VA[0:w, TILES].rearrange("p h c -> p (h c)"),
                                              const("ind_p", w)[:, s:s + 1], None, ALU.mult)
                    ins.then_inc(S("ml_vx"), 1)
                e.wait_ge(S("ml_s"), n + 1)
                e.tensor_tensor(x, pq[1], bc(neg.unsqueeze(1), h4), ALU.min).then_inc(S("ml_x"), 1)
                e.wait_ge(S("ml_e"), n + 1)
                e.tensor_tensor(att, pq[0], x, ALU.mult).then_inc(S("ml_att"), 1)
                o = PS(3, 0, 260).rearrange("p (h c) -> p h c", h=4)[0:w]
                emm = EMM[0:w, TILES] if last_tile else EMM[:, bass.ds(n, 1)].rearrange("p o h -> p (o h)")
                m = [MS[0:w, k] for k in range(8)]
                e.wait_ge(S("ml_sq"), n + 1)
                st.did(e.tensor_scalar(m[4], o[:, :, 64], -1.0, None, ALU.mult))
                st.settle()
                st.did(e.tensor_tensor(m[0], m[4], o[:, :, 64], ALU.max))
                st.settle()
                st.did(e.tensor_tensor(m[1], m[0], emm, ALU.max))
                st.settle()
                e.reciprocal(m[2], m[1])
                st.did(e.tensor_reduce(m[3], MSQ[0:w], AX.X, ALU.add))
                st.settle()
                st.did(e.tensor_tensor(m[4], m[3], m[2], ALU.mult))
                st.settle()
                e.tensor_tensor(m[5], m[4], m[2], ALU.mult).then_inc(S("ml_ms"), 1)
                e.wait_ge(S("ml_rs"), n + 1)
                st.did(e.tensor_tensor(m[7], m[6], m[2], ALU.mult))
                st.settle()
                e.tensor_tensor(MON[0:w], o[:, :, 0:64], bc(m[7].unsqueeze(2), [w, 4, 64]), ALU.mult).then_inc(S("ml_on"), 1)
                bdm = const("bd_ml")
                if last_tile:
                    e.wait_ge(S("ml_ds"), TILES + 1)
                    st.did(e.tensor_tensor(SM, SM, bc(MES.unsqueeze(2), [P, SEGS, 260]), ALU.mult))
                    for s in range(SEGS):
                        b = [4, 5, 6, 7, 0][s // 2]
                        ins = e.tensor_tensor(MVX[:, s, 0:256], PS(b, (s % 2) * 256, (s % 2) * 256 + 256), bdm[:, 0:256], ALU.mult)
                    st.did(ins)
                    e.wait_ge(S("dve_step"), st.n)
                    e.sem_inc(S("ml_dsu"), 1)
                    e.wait_ge(S("ml_ds"), TILES + 2)
                    st.did(e.tensor_tensor(MVX[:, :, 256:260], PS(4, 0, 36).rearrange("p (s c) -> p s c", c=4),
                                           bc(bdm[:, 256:260].unsqueeze(1), [P, SEGS, 4]), ALU.mult))
                    st.settle()
                    e.tensor_tensor(SM, SM, MVX, ALU.add).then_inc(S("ml_final"), 1)
                else:
                    e.wait_ge(S("ml_ds"), n + 1)
                    st.did(e.tensor_tensor(MTMP, PS(4, 0, 260), bdm, ALU.mult))
                    st.settle()
                    sl = MSL[:, bass.ds(n, 1)]
                    st.did(e.scalar_tensor_tensor(SM[:, 0, :], SM[:, 0, :], sl, MTMP, ALU.mult, ALU.add))
                    st.settle()
                e.wait_ge(S("ml_ot"), n + 1)
                for g in range(2):
                    ot = tile_of(OT[:, 6 + g])
                    ins = e.scalar_tensor_tensor(ot, PS(5, g * P, g * P + w), col("mlstm_norm", g), ot, ALU.mult, ALU.mult)
                ins.then_inc(S("ml_pre"), 1)

            with e.Fori(0, TILES) as n:
                st.enter(n, 8)
                ml_tile(n, P, False)
            st.leave(TILES)
            ml_tile(TILES, LASTW, True)
            barrier(e, 2)
            evac(e, 1, 3, lambda b: e.tensor_copy(row3(GQ[:, 1]), cols3(b)))
            evac(e, 1, 4, lambda b: e.tensor_copy(row3(GB[:, 1]), cols3(b)))
            evac(e, 1, 6, lambda b: e.tensor_copy(row3(GK[:, 2]), cols3(b)))
            e.wait_ge(S("banks_free1"), 8)
            e.sem_inc(S("gl_f"), 1)
            for q in range(2):
                evac_v(e, 1, 8 + q, lambda t: GV[:, 0:TILES, 256 * q + P:256 * q + 2 * P] if t == 0
                       else GV[0:LASTW, TILES, 256 * q + P:256 * q + 2 * P], False)
            e.wait_ge(S("gl_zz"), 1)
            e.wait_ge(S("gl_ln"), 1)
            st.did(e.scalar_tensor_tensor(GL_, GB, 0.0, GT, ALU.min, ALU.subtract))
            st.settle()
            st.did(e.tensor_scalar(GL_[:, 2], GL_[:, 2], 1.0 / 16, None, ALU.mult))
            st.settle()
            for g in range(3):
                st.did(e.tensor_tensor_scan(GB[:, g], keep, GL_[:, g], 0.0, ALU.mult, ALU.add))
            st.settle()
            e.wait_ge(S("gl_zero"), 1)
            e.wait_ge(S("gl_in"), 128)
            e.sem_inc(S("gl_go"), 1)

            def gl_tile(n, w, last_tile):
                x, q = (GXL, GEL) if last_tile else (GX, GE)
                halves = LHALVES if last_tile else HALVES
                nl = len(halves) + 1

                def tile_of(y):
                    i = (slice(None),) * (len(y.shape) - 1)
                    return y[i + (slice(TILES * P, NT),)] if last_tile else y[i + (bass.ds(n * P, P),)]
                b = tile_of(GB)
                for l, h in enumerate(halves):
                    o = x[:, :, l + 1, :]
                    bb = b.rearrange("p g (n t) -> p g n t", t=2 * h)
                    mid = bc(bb[:, :, :, h - 1:h], [P, 3, w // (2 * h), h])
                    e.tensor_tensor(half(o, h, False), mid, bb[:, :, :, 0:h], ALU.subtract)
                    ins = e.tensor_tensor(half(o, h, True), bb[:, :, :, h:], mid, ALU.subtract)
                ins.then_inc(S("gl_x"), 1)
                e.tensor_copy(x[:, :, 0, :], b)
                if last_tile:
                    for lo, hi, m in ((0, TAIL, TAIL), (TAIL, w, DSEQ)):
                        o = x[:, :, nl, lo:hi].rearrange("p g (n t) -> p g n t", t=m)
                        bb = b[:, :, lo:hi].rearrange("p g (n t) -> p g n t", t=m)
                        ins = e.tensor_tensor(o, bc(bb[:, :, :, m - 1:m], o.shape), bb, ALU.subtract)
                else:
                    ins = e.tensor_tensor(x[:, :, nl, :], bc(b[:, :, P - 1:P], b.shape), b, ALU.subtract)
                ins.then_inc(S("gl_x"), 1)
                qt, kt = tile_of(GQ), tile_of(GK)
                e.wait_ge(S("gl_e"), 2 * n + 1)
                for l, h in enumerate(halves):
                    for y, second in ((kt, False), (qt, True)):
                        o = half(x[:, :, l + 1, :], h, second)
                        ins = e.tensor_tensor(o, o, half(y, h, second), ALU.mult)
                    ins.then_inc(S("gl_qk"), 1)
                e.wait_ge(S("gl_e"), 2 * n + 2)
                st.did(e.tensor_tensor(q[:, :, 0, :], x[:, :, 0, :], qt, ALU.mult))
                if last_tile:
                    st.settle()
                    e.tensor_copy(GES[:, :, 0], x[:, :, 0, TAIL - 1])
                    st.did(e.tensor_copy(GES[:, :, 1:], x[:, :, 0, TAIL:w].rearrange("p g (q c) -> p g q c", c=DSEQ)[:, :, :, DSEQ - 1]))
                    for g in range(3):
                        ins = e.tensor_tensor(GQX[:, g], bc(q[:, g, 0:1, :], [P, SEGS, w]),
                                              const("ind_t").rearrange("p (s t) -> p s t", s=SEGS), ALU.mult)
                    ins.then_inc(S("gl_qx"), 1)
                e.tensor_tensor(x[:, :, nl, :], x[:, :, nl, :], kt, ALU.mult).then_inc(S("gl_qe"), 1)
                att = GATT.rearrange("p h t -> p (h t)")[0:w, 0:8 * w].rearrange("p (h t) -> p h t", h=8)
                if last_tile:
                    st.did(e.memset(att, 0.0))
                    st.settle()
                for l in range(1, nl + 1):
                    if l >= 2:
                        e.wait_ge(S("gl_att"), n * 8 + l - 1)
                    e.wait_ge(S("gl_s"), n * 8 + l)
                    ps = PSt[0:w, 3 * (l % 2) * 512:3 * (l % 2 + 1) * 512].rearrange("p (b c) -> p b c", b=3)
                    m = mask8("ll" if last_tile else "lv", l - 1, w)
                    e.sem_inc(S("select_turn"), 1)
                    for j in range(3):
                        k = 3 if j < 2 else 2
                        dst = att[:, 3 * j:3 * j + k]
                        if l < nl:
                            h = halves[l - 1]
                            dst, mk = half(dst, h, True), half(m, h, True)
                            src = ps[:, j, 0:k * w // 2].rearrange("p (a n t) -> p a n t", a=k, t=h)
                        else:
                            mk, src = m, ps[:, j, 0:k * w].rearrange("p (a t) -> p a t", a=k)
                        ins = e.copy_predicated(dst, bc(mk.unsqueeze(1), dst.shape), src)
                    ins.then_inc(S("gl_att"), 1)
                e.wait_ge(S("gl_kh"), n + 1) if last_tile else None
                bdm = const("bd_gl")
                if not last_tile:
                    e.wait_ge(S("gl_ds"), n + 1)
                    st.did(e.tensor_tensor(GTMP, PS(4), bdm, ALU.mult))
                    st.settle()
                    for g in range(3):
                        lo, hi = (g * P, g * P + P) if g < 2 else (256, 512)
                        ins = e.scalar_tensor_tensor(SG[:, 0, lo:hi], SG[:, 0, lo:hi], x[:, g, 0, P - 1:P], GTMP[:, lo:hi], ALU.mult, ALU.add)
                    st.did(ins)
                e.wait_ge(S("gl_sq"), n + 1)
                e.tensor_reduce(GMS[0:w, 0], GSQ[0:w], AX.X, ALU.add).then_inc(S("gl_ms"), 1)
                e.wait_ge(S("gl_rs"), n + 1)
                o = PS(3).rearrange("p (h c) -> p h c", h=8)[0:w]
                e.tensor_tensor(GON[0:w], o, bc(GMS[0:w, 1].unsqueeze(2), [w, 8, 64]), ALU.mult).then_inc(S("gl_on"), 1)
                if last_tile:
                    for g in range(3):
                        lo, hi = (g * P, g * P + P) if g < 2 else (256, 512)
                        if g:
                            e.wait_ge(S("gl_ds"), TILES + g)
                        for s in range(SEGS):
                            ins = e.tensor_scalar(GVX[0:w, s, 0:hi - lo], GV[0:w, TILES, lo:hi], const("ind_p", w)[:, s:s + 1], None, ALU.mult)
                        ins.then_inc(S("gl_vx"), 1)
                        m = hi - lo
                        sg = SG[:, :, lo:hi]
                        st.did(e.tensor_tensor(sg, sg, bc(GES[:, g].unsqueeze(2), [P, SEGS, m]), ALU.mult))
                        e.wait_ge(S("gl_ds"), TILES + g + 1)
                        st.settle()
                        per = 4 if g < 2 else 2
                        for s in range(SEGS):
                            o_ = (s // per) * 512 + (s % per) * m
                            ins = e.tensor_tensor(GTMPL[:, s, 0:m], PSt[:, o_:o_ + m], bdm[:, lo:hi], ALU.mult)
                        st.did(ins)
                        st.settle()
                        ins = e.tensor_tensor(sg, sg, GTMPL[:, :, 0:m], ALU.add)
                        if g < 2:
                            st.did(ins)
                            st.settle()
                            e.sem_inc(S("gl_dsu"), 1)
                            e.sem_inc(S("gl_vx"), 1)
                        else:
                            ins.then_inc(S("gl_final"), 1)
                e.wait_ge(S("gl_ot"), n + 1)
                for j in range(4):
                    slot = (0, 1, 4, 5)[j]
                    ot = tile_of(OT[:, slot])
                    c = col("hgrn_norm", j) if j < 2 else col("gla_norm", j - 2)
                    ins = e.scalar_tensor_tensor(ot, PS(5, j * P, j * P + w), c, ot, ALU.mult, ALU.mult)
                st.did(ins)

            with e.Fori(0, TILES) as n:
                st.enter(n, 4)
                gl_tile(n, P, False)
            st.leave(TILES)
            gl_tile(TILES, LASTW, True)
            barrier(e, 3)
            with e.Fori(0, 4) as i:
                e.wait_ge(S("chunk_done1"), i + P_RW + 1)
                e.tensor_copy(row3(R10[:, bass.ds(i * 2 + 1, 1), :].rearrange("p o t -> p (o t)")), cols3(3)).then_inc(S("banks_free1"), 1)
            e.wait_ge(S("banks_free0"), EV_RW + 5)
            e.wait_ge(S("banks_free1"), EV_RW + 5)
            e.wait_ge(S("rw_w"), 48)
            z = R10[:, 0:8]
            zd = z[:, :, NP:NT].rearrange("p s (q c) -> p s q c", c=DSEQ)
            e.tensor_copy(SHO[:, :, 0:1], z[:, :, NP - 1:NP])
            e.tensor_copy(SHO[:, :, 1:], zd[:, :, :, DSEQ - 1]).then_inc(S("shift_ready"), 1)
            rdd = RD[:, :, NP:NT].rearrange("p s (q c) -> p s q c", c=DSEQ)
            st.did(e.tensor_tensor(RD[:, :, 1:W], z[:, :, 0:W - 1], z[:, :, 1:W], ALU.subtract))
            e.tensor_scalar(RD[:, :, 0:1], z[:, :, 0:1], -1.0, None, ALU.mult)
            st.settle()
            st.did(e.tensor_tensor(rdd[:, :, :, 0], SHI, zd[:, :, :, 0], ALU.subtract))
            st.settle()
            for s in range(8):
                ins = e.scalar_tensor_tensor(z[:, s], RD[:, s], col("rwkv_mu", s), z[:, s], ALU.mult, ALU.add)
            ins.then_inc(S("rw_mix"), 1)
            e.wait_ge(S("rw_mix"), 1)
            for g in range(2):
                ins = e.tensor_scalar(RKK[:, g], z[:, 2 + g], col("rwkv_k_k", g), None, ALU.mult)
            ins.then_inc(S("rw_kkr"), 1)
            st.did(e.tensor_scalar(OMK, CC[:, COLS["rwkv_k_a"][0]:COLS["rwkv_k_a"][0] + 2], -1.0, 1.0, ALU.mult, ALU.add))
            e.wait_ge(S("rw_lev"), 6)
            st.settle()
            for g in range(2):
                st.did(e.tensor_scalar(RKP[:, g], RA[:, g], col("rwkv_k_a", g), OMK[:, g:g + 1], ALU.mult, ALU.add))
            st.settle()
            st.did(e.tensor_tensor(RKP, RKP, z[:, 2:4], ALU.mult))
            e.wait_ge(S("rw_lev"), 8)
            st.did(e.tensor_scalar(RE, RE, 1e-12, None, ALU.max))
            st.settle()
            st.did(e.reciprocal(RE, RE))
            st.settle()
            st.did(e.tensor_tensor(RKK, RKK, RE, ALU.mult))
            st.settle()
            for g in range(2):
                e.scalar_tensor_tensor(RX[:, g], z[:, g], col("rwkv_r_k", g), RKP[:, g], ALU.mult, ALU.mult).then_inc(S("rw_hs"), 1)
            for g in range(2):
                e.wait_ge(S("rw_lor"), 9 + g)
                st.did(e.tensor_tensor(row3(RBV[:, g]), cols3(3 * g), row3(z[:, 4 + g]), ALU.mult))
                st.settle()
                e.tensor_scalar(RBV[:, g], RBV[:, g], col("rwkv_ln_b", g), None, ALU.add).then_inc(S("rw_lev"), 1)
            st.did(e.tensor_copy(RX, RWL))
            st.settle()
            for g in range(2):
                ins = e.tensor_tensor_scan(RWL[:, g], keep, RX[:, g], 0.0, ALU.mult, ALU.add)
            st.did(ins)
            st.settle()
            full = RWL[:, :, 0:TILES * P].rearrange("p g (n t) -> p g n t", t=P)
            st.did(e.tensor_scalar(RCS, full[:, :, :, P - 1], 0.5, None, ALU.mult))
            st.settle()
            st.did(e.tensor_tensor(full, full, bc(RCS.unsqueeze(3), full.shape), ALU.subtract))
            st.settle()
            e.tensor_tensor(RX, RWL, RX, ALU.subtract).then_inc(S("rw_wlx"), 1)
            e.wait_ge(S("rw_ex"), 1)
            e.tensor_tensor(REC2, REC, REC, ALU.mult)
            e.tensor_copy(RES[:, :, 0:1], RE[:, :, NP - 1:NP])
            e.tensor_copy(RES[:, :, 1:], RE[:, :, NP:NT].rearrange("p g (q c) -> p g q c", c=DSEQ)[:, :, :, DSEQ - 1])
            st.did(e.scalar_tensor_tensor(RA, RA, -1.0, RKK, ALU.mult, ALU.mult))
            e.tensor_tensor(R10[:, 2:4], z[:, 0:2], RE, ALU.mult).then_inc(S("rw_ex_used"), 1)
            st.did(e.tensor_copy(R10[:, 8:10], z[:, 4:6]))
            e.wait_ge(S("rw_ex"), 2)
            st.settle()
            e.tensor_tensor(R10[:, 4:6], RKP, RE, ALU.mult)
            e.tensor_tensor(R10[:, 6:8], RA, RE, ALU.mult).then_inc(S("rw_ex_used"), 1)
            e.wait_ge(S("rw_ex"), 3)
            st.did(e.tensor_tensor(R10[:, 0:2], RKK, RE, ALU.mult))
            st.settle()
            e.wait_ge(S("rw_zero"), 1)
            e.wait_ge(S("rw_in"), 64)
            e.sem_inc(S("rw_go"), 1)
            e.wait_ge(S("rw_lev"), 10)
            e.wait_ge(S("rw_ex"), 3)

            def rw_tile(n, w, last_tile):
                def tile_of(y):
                    return y[:, TILES * P:NT] if last_tile else y[:, bass.ds(n * P, P)]

                def v4(x, k=4):
                    return x[0:w].rearrange("p (h t) -> p h t", h=k)
                flat = [x.rearrange("p h t -> p (h t)")[:, 0:4 * w] for x in (RTI, RTT)]
                ti, tt = v4(flat[0]), v4(flat[1])
                idw = ident[0:w, 0:w]
                pb = RPB.rearrange("p h k t -> p (h k t)")[0:w, 0:8 * w]
                pk = RPK.rearrange("p h k t -> p (h k t)")[0:w, 0:8 * w]
                cm = const("causal_l" if last_tile else "causal", w)
                if not last_tile:
                    for g in range(2):
                        ec = REC[:, g, bass.ds(n, 1)]
                        ins = e.tensor_scalar(RXC[:, g * P:g * P + P], RSTATE[:, 0, g * P:g * P + P], ec, None, ALU.mult)
                    st.did(ins)
                e.tensor_copy(ti, bc(idw.unsqueeze(1), [w, 4, w]))
                st.did(e.tensor_copy(tt, bc(idw.unsqueeze(1), [w, 4, w])))
                e.wait_ge(S("rw_s"), n + 1)
                st.settle()
                e.sem_inc(S("select_turn"), 1)
                mk = bc(mask8("ll" if last_tile else "lv", 0, w).unsqueeze(1), [w, 2, w])
                mkt = bc(mask8("llt" if last_tile else "lvt", 0, w).unsqueeze(1), [w, 2, w])
                for j in range(2):
                    ins = e.copy_predicated(ti[:, j:4:2, :], mkt, PS(4 + j, 0, 2 * w)[0:w].rearrange("p (h t) -> p h t", h=2))
                ins.then_inc(S("rw_t"), 1)
                for j in range(2):
                    for (dst, bank) in ((pb, 0), (pk, 2)):
                        dst = dst.rearrange("p (i j c) -> p i j c", i=2, j=2)[:, :, j, :]
                        e.tensor_tensor(dst, PS(bank + j, 0, 4 * w)[0:w].rearrange("p (i c) -> p i c", i=2),
                                        bc(cm.unsqueeze(1), [w, 2, 2 * w]), ALU.mult)
                for j in range(2):
                    src = PS(j, 0, 4 * w)[0:w].rearrange("p (i k t) -> p i k t", i=2, k=2)[:, :, 0, :]
                    ins = e.copy_predicated(tt[:, j:4:2, :], mk, src)
                ins.then_inc(S("rw_t"), 1)
                if last_tile:
                    e.wait_ge(S("rw_copied"), TILES + 1)
                    for k in range(2):
                        for g in range(2):
                            ins = e.tensor_tensor(RQX[:, k, g], bc(RC[:, 2 * k + g, 0:w].unsqueeze(1), [P, SEGS, w]),
                                                  const("ind_t").rearrange("p (s t) -> p s t", s=SEGS), ALU.mult)
                    ins.then_inc(S("rw_qx"), 1)
                levels = LHALVES if last_tile else HALVES
                for l, h in list(enumerate(levels))[1:]:
                    for q, (dst, bank, mk) in enumerate(((tt, 0, "ll" if last_tile else "lv"), (ti, 1, "llt" if last_tile else "lvt"))):
                        dst, mk = half(dst, h, q == 0), half(mask8(mk, l, w), h, q == 0)
                        e.wait_ge(S("rw_t"), n * 14 + 2 * l)
                        e.wait_ge(S("rw_n"), n * 12 + 2 * l)
                        e.sem_inc(S("select_turn"), 1)
                        e.copy_predicated(dst, bc(mk.unsqueeze(1), dst.shape),
                                          PS(bank, 0, 2 * w)[0:w].rearrange("p (a n t) -> p a n t", a=4, t=h)).then_inc(S("rw_t"), 1)
                y = PS(1, 0, 256).rearrange("p (h c) -> p h c", h=4)[0:w]
                r = [RMS_[0:w, k] for k in range(4)]
                e.wait_ge(S("rw_y"), n + 1)
                st.did(e.tensor_reduce(r[0], y, AX.X, ALU.add))
                st.settle()
                st.did(e.tensor_scalar(r[1], r[0], 1.0 / 64, None, ALU.mult))
                st.settle()
                e.tensor_tensor(RY[0:w], y, bc(r[1].unsqueeze(2), [w, 4, 64]), ALU.subtract).then_inc(S("rw_yc"), 1)
                if last_tile:
                    for s in range(SEGS):
                        e.tensor_scalar(RVX[0:w, s, :], RV[0:w], const("ind_p", w)[:, s:s + 1], None, ALU.mult)
                        ins = e.tensor_scalar(RUX[0:w, s, :], RUS[0:w], const("ind_p", w)[:, s:s + 1], None, ALU.mult)
                    ins.then_inc(S("rw_vx"), 1)
                    for g in range(2):
                        e.wait_ge(S("rw_ds"), TILES + g + 1)
                        sg = RSTATE[:, :, g * P:g * P + P]
                        for s in range(SEGS):
                            o_ = (s // 4) * 512 + (s % 4) * P
                            ins = e.tensor_tensor(RDSL[:, s, :], PSt[:, o_:o_ + P], bd2, ALU.mult)
                        st.did(ins)
                        st.settle()
                        if g == 0:
                            e.sem_inc(S("rw_dsu"), 1)
                        st.did(e.tensor_tensor(RDSL, RDSL, sg, ALU.add))
                        st.settle()
                        ins = e.tensor_tensor(sg, RDSL, bc(RES[:, g].unsqueeze(2), [P, SEGS, P]), ALU.mult)
                        if g == 0:
                            st.did(ins)
                            st.settle()
                        else:
                            ins.then_inc(S("rw_final"), 1)
                else:
                    e.wait_ge(S("rw_ds"), n + 1)
                    for g in range(2):
                        ins = e.scalar_tensor_tensor(RTM[:, g * P:g * P + P], PS(0, g * P, g * P + P), REC[:, g, bass.ds(n, 1)], bd2, ALU.mult, ALU.mult)
                    st.did(ins)
                    st.settle()
                    for g in range(2):
                        sg = RSTATE[:, 0, g * P:g * P + P]
                        ins = e.scalar_tensor_tensor(sg, sg, REC2[:, g, bass.ds(n, 1)], RTM[:, g * P:g * P + P], ALU.mult, ALU.add)
                    st.did(ins)
                e.wait_ge(S("rw_sq"), n + 1)
                e.tensor_reduce(r[2], RSQ[0:w], AX.X, ALU.add).then_inc(S("rw_ms"), 1)
                e.wait_ge(S("rw_rs"), n + 1)
                e.tensor_tensor(RY[0:w], RY[0:w], bc(r[3].unsqueeze(2), [w, 4, 64]), ALU.mult).then_inc(S("rw_on"), 1)
                e.wait_ge(S("rw_ot"), n + 1)
                for g in range(2):
                    bv = tile_of(RBV[:, g])
                    ins = e.scalar_tensor_tensor(bv, PS(3, g * P, g * P + w), col("rwkv_ln_w", g), bv, ALU.mult, ALU.add)
                st.did(ins)
                st.settle()
                for g in range(2):
                    ot = tile_of(OT[:, 2 + g])
                    ins = e.tensor_tensor(ot, tile_of(RBV[:, g]), ot, ALU.mult)
                ins.then_inc(S("rw_pre"), 1)

            with e.Fori(0, TILES) as n:
                st.enter(n, 7)
                rw_tile(n, P, False)
            st.leave(TILES)
            rw_tile(TILES, LASTW, True)
            barrier(e, 4)
            with e.Fori(0, 4) as jj:
                for c in range(8):
                    u, br = c % 2, c % 4
                    e.wait_ge(S(f"sig{u}"), jj * 4 + (c // 2 + 1))
                    e.wait_ge(S(f"pz{u}"), jj * 4 + (c // 2 + 1))
                    mix = MIX[:, bass.ds(jj * 2 + c // 4, 1), :].rearrange("p o t -> p (o t)")
                    if br == 0:
                        e.tensor_tensor(row3(mix), cols3(3 * u), row3(GZ[:, u]), ALU.mult).then_inc(S(f"mul{u}"), 1)
                    else:
                        if br >= 2:
                            e.wait_ge(S("mix_add"), jj * 6 + (3 * (c // 4) + br - 1))
                        e.tensor_tensor(row3(GPR[:, br - 1]), cols3(3 * u), row3(GZ[:, u]), ALU.mult).then_inc(S(f"mul{u}"), 1)
                        e.wait_ge(S(f"mul{u}"), jj * 4 + (c // 2 + 2))
                        e.tensor_tensor(mix, mix, GPR[:, br - 1], ALU.add).then_inc(S("mix_add"), 1)
            e.wait_ge(S("mix_add"), 24)
            e.sem_inc(S("mix_ready"), 1)
            e.wait_ge(S("xr"), 16 * KD)
            with e.Fori(0, 4) as i:
                for u in range(2):
                    e.wait_ge(S(f"chunk_done{u}"), i + P_OUT + 1)
                    xr = row3(XR[:, bass.ds(i * 2 + u, 1), :].rearrange("p o t -> p (o t)"))
                    e.tensor_tensor(xr, cols3(3 * u), xr, ALU.add).then_inc(S("xr_ready"), 1)
                    e.wait_ge(S("xr_ready"), i * 2 + (u + 1))
                    e.sem_inc(S(f"banks_free{u}"), 1)
            rms_dve(e, 1, RST2, XR, HN2, "norm_mlp")
            barrier(e, 5)
            for r, (lo, n, base) in enumerate(((0, 12, ACTA), (12, 4, HT))):
                with e.Fori(0, n) as i:
                    for u in range(2):
                        e.wait_ge(S(f"banks_free{u}"), i + (EV_UP + lo + 2))
                        x = base[:, bass.ds(i * 2 + u, 1), :].rearrange("p o t -> p (o t)")
                        e.tensor_tensor(x, x, x, ALU.mult)
            barrier(e, 6)
            for k in range(KD):
                v = k % 2
                e.wait_ge(S(f"down{v}"), k // 2 + 1)
                e.wait_ge(S(f"xj{v}"), (k // 2 + 1) * 16)
                e.tensor_tensor(row3(HN2[:, k]), cols3(3 * v), row3(XJ[:, v]), ALU.add).then_inc(S("dn_ready"), 1)
                e.wait_ge(S("dn_ready"), k + 1)
                e.sem_inc(S(f"down_used{v}"), 1)
                e.sem_inc(S("res_used"), 1)
            rms_dve(e, 2, SQ3R, HN2, HN2, "norm_final", lambda ins: ins.then_inc(S("y_ready"), 1))


def kernel(**inputs):
    import concourse.bacc as bacc
    from concourse.bass_utils import run_bass_kernel_spmd

    I = {k: np.asarray(v) for k, v in inputs.items()}
    assert I["hgrn_lb"].shape[0] == DEPTH == 1
    f32 = np.float32

    def chunk(w, c):
        return w[:, c:c + P].reshape(KD, P, P).transpose(1, 0, 2)

    w_in, w_br, w_out = I["w_in"][0], I["w_branch"][0], I["w_out"][0]
    w_up, w_down = I["w_up"][0], I["w_down"][0]
    gates = [O_GATE + b * D + j * P for j in range(KD) for b in range(4)]
    chunks = [chunk(w_in, c) for c in ML_T + ML_V + GL_T + GL_V + gates[:16] + RW_T + gates[16:]]
    chunks += [chunk(w_out, j * P) for j in range(KD)]
    chunks += [chunk(w_up, j * P) for j in range(FF // P)]
    chunks += [chunk(w_down[c * D:(c + 1) * D], j * P) for j in range(KD) for c in range(4)]
    small = np.zeros((D, 68), f32)
    for c, n, at in SMALL:
        small[:, at:at + n] = w_in[:, c:c + n]
    x = np.concatenate([I["meta_tokens"], I["x_prompt"][0], I["x_sample"].reshape(-1, D)], 0)
    xT = np.zeros((D, W), f32)
    xT[:, :NT] = x.T
    cols = np.zeros((P, NCOLS), f32)
    for name, (o, n) in COLS.items():
        v = I[name].reshape(-1)
        if name in ("mlstm_i_b", "mlstm_f_b"):
            cols[:4, o] = v
        else:
            cols[:, o:o + n] = v.reshape(n, P).T
    cf, cu = constants()

    def pack(parts):
        at, where = 0, {}
        for k, v in parts.items():
            where[k] = (at, v.shape[1])
            at += v.shape[1]
        return np.concatenate(list(parts.values()), 1), where

    cfa, fcols = pack(cf)
    cua, ucols = pack(cu)
    conv = I["state_mlstm_conv"][0]
    arrays = {
        "cf": cfa, "cu": cua, "cols": cols, "xT": xT.reshape(KD, P, W),
        "w_small": small.reshape(KD, P, 68).transpose(1, 0, 2), "w_all": np.stack(chunks),
        "w_br": w_br.reshape(4, 2, P, KD, P).transpose(3, 2, 0, 1, 4).reshape(KD, P, 8, P),
        "w_ga": I["gla_gate_up"][0],
        "rw_wa": np.concatenate([I["rwkv_w_up"][0], I["rwkv_a_up"][0]], 0), "rw_g": I["rwkv_g_up"][0],
        "hg": I["state_hgrn"][0], "gl": I["state_gla"][0], "mc": I["state_mlstm_c"][0],
        "mn": I["state_mlstm_n"][0], "mm": I["state_mlstm_m"][0],
        "rw": I["state_rwkv"][0].transpose(0, 1, 3, 2),
        "shift": I["state_rwkv_shift"][0].reshape(NSEQ, 8, P).transpose(2, 1, 0),
        "conv": conv.reshape(NSEQ, 3, 2, P).transpose(3, 2, 0, 1),
    }
    outs = {
        "yT": (KD, P, NT), "hg": (SEGS, 4, 64, 64), "rw": (SEGS, 4, 64, 64), "shift": (P, 8, SEGS),
        "gl": (SEGS, 4, 32, 64), "mc": (SEGS, 4, 32, 64), "mn": (SEGS, 4, 32), "mm": (SEGS, 4),
        "conv_p": (P, 2, 3), "conv_s": (P, 2, NSEQ, 3),
    }
    nc = bacc.Bacc("TRN2", target_bir_lowering=False, num_devices=1)
    feeds, A, OUT = {}, {}, {}
    for name, a in arrays.items():
        a = np.ascontiguousarray(a)
        feeds[f"in_{name}"] = a
        A[name] = nc.dram_tensor(f"in_{name}", a.shape, mybir.dt.from_np(a.dtype), kind="ExternalInput").ap()
    for name, shape in outs.items():
        OUT[name] = nc.dram_tensor(f"out_{name}", shape, F32, kind="ExternalOutput").ap()
    A["gates"] = nc.dram_tensor("gates", (32, P, W), F32, kind="Internal").ap()
    A["x2"] = nc.dram_tensor("residual", (KD, P, W), F32, kind="Internal").ap()
    build(nc, A, OUT, fcols, ucols, cfa.shape[1], cua.shape[1])
    R = run_bass_kernel_spmd(nc, [feeds], core_ids=[0]).results[0]
    o = {name: R[f"out_{name}"] for name in outs}
    y = o["yT"].reshape(D, NT).T
    rw = o["rw"].transpose(0, 1, 3, 2)
    shift = o["shift"].transpose(2, 1, 0).reshape(SEGS, 8 * P)
    conv_p = o["conv_p"].transpose(2, 1, 0).reshape(1, 3, 2 * P)
    conv_s = o["conv_s"].transpose(2, 3, 1, 0).reshape(NSEQ, 3, 2 * P)

    def both(a):
        return a[None, 0:1], a[None, 1:]

    st = [both(a) for a in (o["hg"], rw, shift, o["gl"], o["mc"], o["mn"], o["mm"])]
    st.append((conv_p[None], conv_s[None]))
    c = np.ascontiguousarray
    return tuple(c(a) for a in [y[META:NP][None], y[NP:].reshape(NSEQ, DSEQ, D)]
                 + [s[0] for s in st] + [s[1] for s in st])
```

```python
import numpy as np
import concourse.bass as bass
from concourse import mybir
from contextlib import ExitStack

F32 = mybir.dt.float32
U8 = mybir.dt.uint8
ALU = mybir.AluOpType
ACT = mybir.ActivationFunctionType
AX = mybir.AxisListType

D, META, SEQ, NSEQ, DSEQ, FF = 1024, 16, 1024, 8, 4, 4096
P = 128
NP = META + SEQ
NT = NP + NSEQ * DSEQ
GRP = 358
W = 3 * GRP
TILES = NT // P
LASTW = NT - TILES * P
TAIL = NP - TILES * P
SEGS = 1 + NSEQ
KD = D // P
EPS, LN_EPS = 1e-6, 64e-5
DECAY = float(np.exp(-0.5))
HALVES = [1, 2, 4, 8, 16, 32, 64]
LHALVES = [1, 2, 4, 8]
BIG = 1e30
DEPTH = 1

O_HG, O_RW, O_GL, O_ML, O_GATE = 0, 1024, 2048, 2832, 3608
ML_T = [O_ML, O_ML + 128, O_ML + 520, O_ML + 648]
ML_V = [O_ML + 256, O_ML + 384]
GL_T = [O_HG, O_HG + 128, O_HG + 256, O_HG + 384, O_HG + 768, O_HG + 896,
        O_GL, O_GL + 128, O_GL + 528, O_GL + 656]
GL_V = [O_HG + 512, O_HG + 640, O_GL + 256, O_GL + 384]
RW_T = [O_RW + 128 * j for j in range(8)]
SMALL = [(O_GL + 512, 16, 0), (O_ML + 512, 4, 32), (O_ML + 516, 4, 64)]

COLS = {}
for _name, _n in [("norm_mix", 8), ("norm_mlp", 8), ("norm_final", 8), ("hgrn_norm", 2), ("gla_norm", 2),
                  ("mlstm_norm", 2), ("rwkv_mu", 8), ("rwkv_w0", 2), ("rwkv_a0", 2), ("rwkv_k_k", 2),
                  ("rwkv_k_a", 2), ("rwkv_r_k", 2), ("rwkv_ln_w", 2), ("rwkv_ln_b", 2), ("gla_gate_b", 1),
                  ("mlstm_conv_w", 8), ("mlstm_conv_b", 2), ("mlstm_i_b", 1), ("mlstm_f_b", 1)]:
    COLS[_name] = (sum(n for _, n in COLS.values()), _n)
NCOLS = sum(n for _, n in COLS.values())


def constants():
    s, t = np.arange(P)[:, None], np.arange(P)[None, :]
    seg = np.where(np.arange(P) < TAIL, 0, 1 + (np.arange(P) - TAIL) // DSEQ)
    same = seg[:, None] == seg[None, :]

    def pair(h):
        return ((s // (2 * h)) == (t // (2 * h))) & (s % (2 * h) < h) & (t % (2 * h) >= h)

    lv = [pair(h) for h in HALVES]
    ll = [pair(h) & same for h in LHALVES]
    f = {
        "eps": np.tile(np.array([[EPS, LN_EPS]]), (P, 1)),
        "ident": np.eye(P), "ones": np.ones((P, P)),
        "bd_gl": np.concatenate([np.kron(np.eye(2), np.ones((64, 64)))] * 2
                                + [np.kron(np.eye(4), np.ones((32, 64)))], 1),
        "causal": np.stack([s < t, s <= t], 1),
        "causal_l": np.stack([(s < t) & same, (s <= t) & same], 1)[:, :, :LASTW],
        "keep": np.tile((np.where(np.arange(W) < NP, np.arange(W) % P,
                                  (np.arange(W) - NP) % DSEQ) != 0)[None], (P, 1)),
        "ind_t": np.tile((np.arange(SEGS)[:, None] == seg[None, :LASTW])[None], (P, 1, 1)),
        "ind_p": (seg[:, None] == np.arange(SEGS)[None]) & (s < LASTW),
        "bd_ml": np.kron(np.eye(4), np.ones((32, 65))),
        "neg": np.where(s <= t, 0, -BIG), "neg_l": np.where((s <= t) & same, 0, -BIG)[:, :LASTW],
        "head4": np.kron(np.eye(4), np.ones((32, 1))),
        "sel4": (t // 32 == s) & (s < 4),
        "bd4": np.kron(np.eye(P, 4), np.ones((1, P))),
        "bd4_l": np.kron(np.eye(P, 4), np.ones((1, LASTW))),
    }
    u = {"lv": np.stack(lv + [s == t], 1), "lvt": np.stack([m.T for m in lv], 1),
         "ll": np.stack(ll + [s == t], 1)[:, :, :LASTW], "llt": np.stack([m.T for m in ll], 1)[:, :, :LASTW]}
    f = {k: v.reshape(P, -1).astype(np.float32) for k, v in f.items()}
    u = {k: v.reshape(P, -1).astype(np.float32) for k, v in u.items()}
    return f, u


SEMAPHORES = """
    act_back act_hi act_parts act_spilled0 act_spilled1 act_sq act_step act_used banks_free0
    banks_free1 chunk_done0 chunk_done1 chunk_loaded0 chunk_loaded1 consts conv_ready dn_ready down0
    down1 down_used0 down_used1 dve_step gl_att gl_dk gl_ds gl_dsu gl_e gl_f gl_go gl_kh gl_kt gl_ln
    gl_ms gl_o gl_on gl_ot gl_qb gl_qe gl_qk gl_qx gl_rs gl_s gl_sq gl_third gl_vx gl_x gl_z gl_zz
    gt_done gt_free gt_sent hn_ready ht_ready mix_add mix_ready ml_att ml_bc ml_conv ml_copied ml_ds
    ml_dsu ml_e ml_gbd ml_go ml_if ml_kh ml_kt ml_ln ml_ms ml_mt ml_o ml_on ml_ot ml_pre ml_qx
    ml_rows ml_rs ml_s ml_sc ml_silu ml_sq ml_vx ml_x mul0 mul1 out parts phase pz res_back rstd
    rw_copied rw_ds rw_dsu rw_ex rw_ex_used rw_go rw_hs rw_kkr rw_kt rw_kv rw_lev rw_lor rw_lora
    rw_m rw_m1 rw_mix rw_ms rw_n rw_on rw_ot rw_pre rw_qx rw_r rw_rhs rw_rs rw_s rw_sq rw_t rw_u
    rw_us rw_vx rw_w rw_wlx rw_y rw_yc select_turn shift_ready sig small spilled split0 split1
    sq_ready sq_used states_final states_in wb0 wb1 wb_used0 wb_used1 weights_hi wga ws x0 x1 x2 x3
    xr xr_ready y_out y_ready z0 z1 zeroed
""".split()


GL_DIAG = {0: (0, 0), 2: (0, 1), 4: (0, 2), 1: (1, 0), 3: (1, 1), 6: (1, 2), 5: (2, 0), 7: (2, 1)}


class Steps:

    def __init__(self, eng, sem):
        self.eng, self.sem, self.n, self.i = eng, sem, 0, None

    def did(self, ins):
        ins.then_inc(self.sem, 1)
        self.n += 1

    def settle(self):
        if self.i is None:
            self.eng.wait_ge(self.sem, self.n)
        else:
            self.eng.wait_ge(self.sem, self.i * self.per + self.n)

    def enter(self, i, per):
        self.i, self.per, self.start = i, per, self.n

    def leave(self, times):
        assert self.n - self.start == self.per, (self.n - self.start, self.per)
        self.n, self.i = self.start + self.per * times, None


def build(nc, A, OUT, fcols, ucols, fdim, udim):
    ctx = ExitStack()
    with ctx:
        def sb(name, cols, dt=F32):
            return ctx.enter_context(nc.sbuf_tensor(name, [P, cols], dt))

        def sb_twice(name, cols):
            with nc.sbuf_tensor(name + "_parts", [P, cols], mybir.dt.float32r) as parts:
                pass
            return sb(name, cols), parts

        sems = {name: ctx.enter_context(nc.semaphore(name)) for name in SEMAPHORES}

        def S(name):
            return sems[name]

        (HT, HT_R), (OT, OT_R) = ([x[:, :].rearrange("p (k t) -> p k t", k=KD) for x in sb_twice(name, KD * W)]
                                  for name in ("HT", "OT"))
        CF, CF_R = sb_twice("CF", fdim)
        CU = sb("CU", udim, U8)
        CC = sb("CC", NCOLS)
        WGA = sb("WGA", P)
        RING, RING_R = (x[:, :].rearrange("p (u k c) -> p u k c", u=2, k=8) for x in sb_twice("RING", 2 * 8 * P))
        PSt = ctx.enter_context(nc.psum_tensor("PS", [P, 8 * 512], F32))

        def PS(b, lo=0, hi=512):
            return PSt[:, b * 512 + lo:b * 512 + hi]

        NA = (nc.sbuf_usable_end - nc.sbuf_base) // 4 - 16
        with nc.sbuf_tensor("MIX_parts", [P, KD * W], mybir.dt.float32r) as MIX_R:
            with nc.sbuf_tensor("between", [P, KD * W], F32):
                with nc.sbuf_tensor("HN_parts", [P, KD * W], mybir.dt.float32r) as HNH_R:
                    with nc.sbuf_tensor("ACT_parts", [P, 3 * W], mybir.dt.float32r) as ACT_R:
                        pass
        AR = sb("AR", NA)
        MIX_R, HNH_R = (x[:, :].rearrange("p (k t) -> p k t", k=KD) for x in (MIX_R, HNH_R))

        def const(name, rows=P):
            o, n = fcols[name]
            return CF[0:rows, o:o + n]

        def mask8(name, k, rows=P):
            o, n = ucols[name]
            w = {"lv": P, "lvt": P, "ll": LASTW, "llt": LASTW}[name]
            return CU[0:rows, o + k * w:o + (k + 1) * w]

        def col(name, j=0, rows=P, lo=0):
            o, _ = COLS[name]
            return CC[lo:rows, o + j:o + j + 1]

        ZS = CF[:, fcols["bd_ml"][0]:fcols["bd_ml"][0] + W]

        class Arena:
            def __init__(self, at=0):
                self.at = at

            def take(self, pattern=None, rows=P, **dims):
                n = 1
                for v in dims.values():
                    n *= v
                o = self.at
                self.at += n
                assert self.at <= NA, (self.at, NA)
                x = AR[0:rows, o:o + n]
                if len(dims) > 1:
                    names = " ".join(dims)
                    x = x.rearrange(f"p ({names}) -> p {names}", **dims)
                return x

        EPS_COL = {EPS: slice(0, 1), LN_EPS: slice(1, 2)}
        ident, ones, keep = const("ident"), const("ones"), const("keep")
        bd2 = const("bd_gl")[:, 0:P]

        def cols3(b):
            return PSt[:, b * 512:(b + 3) * 512].rearrange("p (g c) -> p g c", g=3)[:, :, 0:GRP]

        def half(x, h, second):
            names = " ".join("abc"[:len(x.shape) - 2])
            y = x.rearrange(f"p {names} (n t) -> p {names} n t", t=2 * h)
            return y[(slice(None),) * (len(y.shape) - 1) + (slice(h, 2 * h) if second else slice(0, h),)]

        def row3(x):
            return x.rearrange("p (g c) -> p g c", g=3)

        def bc(x, shape):
            return x.to_broadcast(shape)

        a = Arena()
        GA = a.take(c=W)
        KEEPTO = a.at
        a = Arena(KEEPTO)
        XT = a.take(k=KD, t=W)
        SQB = a.take(u=2, t=W)
        RST = a.take(t=W)
        WS = a.take(k=KD, c=68)
        CUF = a.take(c=udim)
        a = Arena(KEEPTO)
        RI, RF, RT, RB, RM, RNG, RG, RSC, RKH = (a.take(rows=4, c=W) for _ in range(9))
        a.at = max(a.at, 0)
        WS_END = KEEPTO + KD * W + 3 * W + KD * 68
        RM0 = a.take(rows=4, c=20)
        FP = a.take(g=2, c=NP + 3 + NSEQ * (DSEQ + 3))
        M4 = a.take(s=4, t=W)
        VA = a.take(t=TILES + 1, h=4, c=65)
        SM = a.take(s=SEGS, c=260)
        EMM = a.take(t=TILES + 1, h=4)
        MC = a.take(s=4, t=P)
        GBD = a.take(rows=4, h=4, t=P)
        GST = a.take(rows=4, t=P)
        MX = a.take(h=4, t=P)
        MQH = a.take(h=4, t=P)
        MATT = a.take(h=4, t=P)
        MKH = a.take(c=P)
        MON = a.take(h=4, c=64)
        MSQ = a.take(h=4, c=64)
        MTMP = a.take(c=260)
        MS = a.take(k=8, h=4)
        MQX = a.take(s=SEGS, t=LASTW)
        MVX = a.take(s=SEGS, c=260)
        MES = a.take(s=SEGS)
        MSL = a.take(n=TILES)
        a = Arena(KEEPTO)
        GQ = a.take(g=3, t=W)
        GK = a.take(g=3, t=W)
        GB0 = a.at
        GB = a.take(g=3, t=W)
        GV = a.take(t=TILES + 1, c=512)
        GX0 = a.at
        GX = a.take(g=3, l=10, t=P)
        GE0 = a.at
        GE = a.take(g=3, l=2, t=P)
        GQC = a.take(l=7, g=3, t=P // 2)
        GQB = a.take(b=2, c=8 * (P // 2))
        a.at = max(a.at, GE0 + 3 * W)
        GATT = a.take(h=8, t=P)
        GKH = a.take(c=3 * P)
        b = Arena(0)
        GSQ = b.take(h=8, c=64)
        GON = b.take(h=8, c=64)
        GTMP = a.take(c=512)
        GMS = a.take(k=2, h=8)
        SG = a.take(s=SEGS, c=512)
        GES = a.take(g=3, s=SEGS)
        b = Arena(GX0)
        GT = b.take(g=3, t=W)
        GTMPL = Arena(GB0).take(s=SEGS, c=256)
        GXL = Arena(GX0).take(g=3, l=7, t=LASTW)
        b = Arena(GX0 + 3 * 7 * LASTW)
        GVX = b.take(s=SEGS, c=256)
        assert b.at <= GE0
        b = Arena(GE0)
        GL_ = b.take(g=3, t=W)
        b = Arena(GE0)
        GEL = b.take(g=3, l=2, t=LASTW)
        GQX = Arena(GX0 + 3 * 7 * LASTW).take(g=3, s=SEGS, t=LASTW)
        a = Arena()
        R10 = a.take(s=10, t=W)
        RBV = a.take(g=2, t=W)
        RTMP0 = a.at
        RA = a.take(g=2, t=W)
        RWL = a.take(g=2, t=W)
        RKK = a.take(g=2, t=W)
        RE = a.take(g=2, t=W)
        RX = a.take(g=2, t=W)
        RKP = a.take(g=2, t=W)
        RCS = a.take(g=2, t=TILES)
        REC = a.take(g=2, t=TILES)
        REC2 = a.take(g=2, t=TILES)
        RES = a.take(g=2, s=SEGS)
        SHI = a.take(s=8, q=NSEQ)
        SHO = a.take(s=8, q=SEGS)
        OMK = a.take(g=2)
        RWK = a.take(w=256)
        RGU = a.take(w=256)
        RSTATE = a.take(s=SEGS, c=256)
        RXC = a.take(c=256)
        assert a.at <= NA
        b = Arena(RTMP0)
        RD = b.take(s=8, t=W)
        b = Arena(RTMP0)
        RC = b.take(s=10, t=P)
        RD0 = b.at
        RPB = b.take(h=4, k=2, t=P)
        RPK = b.take(h=4, k=2, t=P)
        RTT = b.take(h=4, t=P)
        RTI = b.take(h=4, t=P)
        RM10 = b.at
        RM1 = b.take(h=4, t=P)
        RKB = b.take(c=512)
        RV = b.take(c=256)
        RRS = b.take(c=256)
        RUS = b.take(c=256)
        RY = b.take(h=4, c=64)
        RMS_ = b.take(k=4, h=4)
        RTM = Arena(b.at).take(c=256)
        RSQ = Arena(RM10).take(h=4, c=64)
        RQX = b.take(k=2, g=2, s=SEGS, t=LASTW)
        RVX = b.take(s=SEGS, c=256)
        RUX = b.take(s=SEGS, c=256)
        RDSL = Arena(RD0).take(s=SEGS, c=P)
        assert b.at <= RTMP0 + 12 * W, b.at - RTMP0 - 12 * W
        a = Arena(0)
        MIX = a.take(k=KD, t=W)
        XR = a.take(k=KD, t=W)
        HNH0 = a.at
        WB = a.take(u=2, k=8, c=P)
        GZ = a.take(u=2, t=W)
        GPR = a.take(u=3, t=W)
        assert HNH0 == 2 * KD * W
        a = Arena(HNH0 + KD * W)
        SQ2 = a.take(u=2, t=W)
        RST2 = a.take(t=W)
        HN2 = OT
        WHI_R = CF_R[:, fcols["bd_gl"][0]:fcols["bd_gl"][0] + 2 * KD * P].rearrange("p (u k c) -> p u k c", u=2, k=KD)
        ACTA = Arena(0).take(k=2 * KD, t=W)
        ACTB = Arena(HNH0).take(k=KD, t=W)
        STG = SQ2
        w0 = fcols["bd_gl"][0] + 2 * KD * P
        AHI_R = [ACT_R[:, 0:W], ACT_R[:, W:2 * W]]
        ALO_R = [ACT_R[:, 2 * W:3 * W], CF_R[:, w0:w0 + W]]

        def act_row(r):
            return ACTA[:, r] if r < 16 else HT[:, r - 16] if r < 24 else ACTB[:, r - 24]
        SQ3 = Arena(0).take(u=2, t=W)
        SQ3R = Arena(2 * W).take(t=W)

        xs, ys = A["xT"], OUT["yT"]
        block = ctx.enter_context(nc.Block())

        def barrier(e, k):
            e.drain().then_inc(S("phase"), 1)
            e.wait_ge(S("phase"), 4 * k)

        def pe_chunk(e, u, bank):
            for g in range(3):
                for k in range(KD):
                    last = e.matmul(PS(bank + g, 0, GRP), RING[:, u, k, :], HT[:, k, g * GRP:(g + 1) * GRP],
                                    start=k == 0, stop=k == KD - 1)
            return last

        def pe_pair(e, p, ev):
            for u in range(2):
                e.wait_ge(S(f"chunk_loaded{u}"), (p + 1) * 16)
                e.wait_ge(S(f"banks_free{u}"), ev + 1)
                pe_chunk(e, u, 3 * u).then_inc(S(f"chunk_done{u}"), 1)

        def gate_work(e, n, first_pair, first_tile):
            for u in range(2):
                for g in range(3):
                    c = 3 * u + g
                    if g == 0:
                        e.wait_ge(S(f"chunk_loaded{u}"), (n + first_pair + 1) * 16)
                    e.wait_ge(S("gt_free"), (n + first_tile) * 6 + (c + 1))
                    for k in range(KD):
                        last = e.matmul(PS(6 + c % 2, 0, GRP), RING[:, u, k, :], HT[:, k, g * GRP:(g + 1) * GRP],
                                        start=k == 0, stop=k == KD - 1)
                        if k % 2 and k < KD - 1:
                            yield
                    last.then_inc(S("gt_done"), 1)
                    if g == 2:
                        e.drain().then_inc(S(f"chunk_done{u}"), 1)
                    yield

        def gate_out(e, n, c, first_tile):
            u, g = c // 3, c % 3
            if g == 0:
                e.wait_ge(S("gt_sent"), ((n + first_tile) * 2 + (u + 1)) * 16)
            e.wait_ge(S("gt_done"), (n + first_tile) * 6 + (c + 1))
            e.activation(ZS[:, g * GRP:(g + 1) * GRP], PS(6 + c % 2, 0, GRP), ACT.Copy).then_inc(S("gt_free"), 1)
            if g == 2:
                e.wait_ge(S("gt_free"), (n + first_tile) * 6 + (c + 3))
                e.dma_start(A["gates"][bass.ds(n * 2 + (2 * first_tile + u), 1)].rearrange("o p t -> (o p) t"),
                            ZS).then_inc(S("gt_sent"), 16)

        def steps(work, k):
            for _ in range(k):
                next(work, None)

        def pe_vpair(e, p, ev):
            for u in range(2):
                e.wait_ge(S(f"chunk_loaded{u}"), (p + 1) * 16)
                e.wait_ge(S(f"banks_free{u}"), ev + 1)
                for t in range(TILES + 1):
                    w = P if t < TILES else LASTW
                    o = 3 * u * 512 + t * P
                    for k in range(KD):
                        last = e.matmul(PSt[0:w, o:o + P], HT[:, k, t * P:t * P + w], RING[:, u, k, :],
                                        start=k == 0, stop=k == KD - 1)
                last.then_inc(S(f"chunk_done{u}"), 1)

        def evac(e, u, p, emit, copy_in=None):
            e.wait_ge(S(f"chunk_done{u}"), p + 1)
            emit(3 * u).then_inc(S(f"banks_free{u}"), 1)

        def evac_v(e, u, p, dst, eng_act):
            def emit(b):
                src = PSt[:, b * 512:b * 512 + TILES * P].rearrange("p (t c) -> p t c", t=TILES)
                tail = PSt[0:LASTW, b * 512 + TILES * P:b * 512 + (TILES + 1) * P]
                for t in range(2):
                    o, i = (dst(0), src) if t == 0 else (dst(1), tail)
                    if len(o.shape) - len(i.shape) == 1:
                        i = i.rearrange("p (h c) -> p h c", c=64) if t else i.rearrange("p t (h c) -> p t h c", c=64)
                    if eng_act:
                        last = e.activation(o, i, ACT.Copy)
                    else:
                        last = e.tensor_copy(o, i)
                return last
            evac(e, u, p, emit)

        def rms_pe(e, r, bank=0):
            for k in range(KD):
                e.wait_ge(S("sq_ready"), r * KD + k + 1)
                for g in range(3):
                    last = e.matmul(PS(bank + g, 0, GRP), ones, rms_sq[r][:, k % 2, g * GRP:(g + 1) * GRP],
                                    start=k == 0, stop=k == KD - 1)
                last.then_inc(S("sq_used"), 1)

        def rms_act(e, st, r, rst, src, ready=None, bank=0):
            for k in range(KD):
                if ready is not None:
                    ready(k)
                if k >= 2:
                    e.wait_ge(S("sq_used"), r * KD + k - 1)
                e.activation(rms_sq[r][:, k % 2, :], src[:, k, :], ACT.Square,
                             scale=D ** -0.5).then_inc(S("sq_ready"), 1)
            e.wait_ge(S("sq_used"), (r + 1) * KD)
            rstd(e, st, row3(rst), cols3(bank)).then_inc(S("rstd"), 1)

        def rstd(e, st, out, in_, eps=EPS):
            st.did(e.activation(out, in_, ACT.Ln, bias=const("eps", in_.shape[0])[:, EPS_COL[eps]]))
            st.settle()
            return e.activation(out, out, ACT.Exp, scale=-0.5)

        def exp_ln_table(e):
            e.preload_act_table_set("natural_log_exp_and_others")

        def rms_dve(e, r, rst, src, dst, name, each=None):
            e.wait_ge(S("rstd"), r + 1)
            for k in range(KD):
                ins = e.scalar_tensor_tensor(dst[:, k, :], src[:, k, :], col(name, k), rst, ALU.mult, ALU.mult)
                if each is not None:
                    each(ins)
            return ins

        rms_sq = [SQB, SQ2, SQ3]


        def split_hi(e, hi, x):
            return e.tensor_copy(hi, x)

        def split_lo(e, lo, hi, x):
            return e.tensor_tensor(lo, x, hi.bitcast(F32), ALU.subtract)

        def split_chunk(e, u, p):
            e.wait_ge(S(f"chunk_loaded{u}"), (p + 1) * 16)
            split_hi(e, WHI_R[:, u], RING[:, u]).then_inc(S("weights_hi"), 1)
            e.wait_ge(S("weights_hi"), p * 2 - (2 * P_OUT - u - 1))
            split_lo(e, RING_R[:, u], WHI_R[:, u], RING[:, u]).then_inc(S(f"split{u}"), 1)

        def pe_split_pair(e, p, ev, xhi, xlo, before_second=None):
            for u in range(2):
                e.wait_ge(S(f"split{u}"), p - (P_OUT - 1))
                e.wait_ge(S(f"banks_free{u}"), ev + 1)
                if u and before_second is not None:
                    before_second()
                for g in range(3):
                    t = slice(g * GRP, (g + 1) * GRP)
                    for k in range(KD):
                        for i, (a_, b_) in enumerate(((WHI_R, xhi), (WHI_R, xlo), (RING_R, xhi))):
                            last = e.matmul(PS(3 * u + g, 0, GRP), a_[:, u, k, :], b_[:, k, t],
                                            start=k == 0 and i == 0, stop=k == KD - 1 and i == 2)
                last.then_inc(S(f"chunk_done{u}"), 1)

        P_ML, P_GL, P_G1, P_RW, P_G2 = 0, 3, 10, 18, 22
        P_OUT, P_UP, P_DOWN = 30, 34, 50
        EV_RW = 10
        EV_OUT, EV_UP = 14, 18

        @block.sync
        def _(e):
            e.dma_start(CF[:, :], A["cf"]).then_inc(S("consts"), 16)
            e.dma_start(CUF, A["cu"]).then_inc(S("consts"), 16)
            e.dma_start(CC[:, :], A["cols"]).then_inc(S("consts"), 16)
            for k in range(KD):
                e.dma_start(XT[:, k, :], xs[k]).then_inc(S(f"x{k // 2}"), 16)
            e.dma_start(WS, A["w_small"]).then_inc(S("ws"), 16)

            def load(u, p):
                e.dma_start(RING[:, u], A["w_all"][bass.ds(p * 2 + u, 1)].rearrange(
                    "o p k c -> (o p) k c")).then_inc(S(f"chunk_loaded{u}"), 16)

            for u in range(2):
                load(u, 0)
            with e.Fori(1, P_DOWN + 16) as p:
                for u in range(2):
                    e.wait_ge(S(f"chunk_done{u}"), p)
                    load(u, p)
            for k in range(KD):
                e.wait_ge(S("y_ready"), k + 1)
                e.dma_start(ys[k], HN2[:, k, 0:NT]).then_inc(S("y_out"), 16)
            e.wait_ge(S("y_out"), 16 * KD)

        def pool_program(e):
            barrier(e, 1)
            e.memset(SM, 0.0)
            e.memset(VA, 1.0)
            e.memset(MATT, 0.0)
            e.memset(M4[:, :, NT:W], 0.0)
            e.memset(RM0, 0.0)
            e.memset(FP[:, :, 0:3], 0.0).then_inc(S("zeroed"), 1)
            e.wait_ge(S("zeroed"), 1)
            fdec = FP[:, :, NP + 3:].rearrange("p g (q c) -> p g q c", q=NSEQ)
            for g in range(2):
                e.dma_start(fdec[:, g, :, 0:3], A["conv"][:, g]).then_inc(S("states_in"), 16)
            for h in range(4):
                r = slice(32 * h, 32 * h + 32)
                e.dma_start(SM[r, 1:, h * 65:h * 65 + 64], A["mc"][:, h].rearrange("s k v -> k s v")).then_inc(S("states_in"), 16)
                e.dma_start(SM[r, 1:, h * 65 + 64], A["mn"][:, h].rearrange("s k -> k s")).then_inc(S("states_in"), 16)
            e.dma_start(RM0[:, 12:20], A["mm"].rearrange("s h -> h s")).then_inc(S("states_in"), 16)
            e.wait_ge(S("states_in"), 11 * 16)
            e.wait_ge(S("conv_ready"), 2)
            for g in range(2):
                e.dma_start(OUT["conv_p"][:, g], FP[:, g, NP:NP + 3]).then_inc(S("out"), 16)
                e.dma_start(OUT["conv_s"][:, g], fdec[:, g, :, DSEQ:DSEQ + 3]).then_inc(S("out"), 16)
            e.wait_ge(S("states_final"), 1)
            for h in range(4):
                r = slice(32 * h, 32 * h + 32)
                e.dma_start(OUT["mc"][:, h].rearrange("s k v -> k s v"), SM[r, :, h * 65:h * 65 + 64]).then_inc(S("out"), 16)
                e.dma_start(OUT["mn"][:, h].rearrange("s k -> k s"), SM[r, :, h * 65 + 64]).then_inc(S("out"), 16)
            e.dma_start(OUT["mm"][0:1].rearrange("s h -> h s"), RM[:, NP - 1:NP]).then_inc(S("out"), 16)
            e.dma_start(OUT["mm"][1:].rearrange("s h -> h s"),
                        RM[:, NP:NT].rearrange("p (q c) -> p q c", q=NSEQ)[:, :, DSEQ - 1]).then_inc(S("out"), 16)
            e.wait_ge(S("out"), 14 * 16)
            barrier(e, 2)
            e.memset(SG, 0.0)
            e.memset(GATT, 0.0).then_inc(S("zeroed"), 1)
            e.wait_ge(S("zeroed"), 2)

            def gl_states(out):
                for h in range(4):
                    r = slice(64 * (h % 2), 64 * (h % 2) + 64)
                    c = (h // 2) * P + (h % 2) * 64
                    q = slice(32 * h, 32 * h + 32)
                    if out:
                        e.dma_start(OUT["hg"][:, h].rearrange("s k v -> k s v"), SG[r, :, c:c + 64]).then_inc(S("out"), 16)
                        e.dma_start(OUT["gl"][:, h].rearrange("s k v -> k s v"), SG[q, :, 256 + 64 * h:320 + 64 * h]).then_inc(S("out"), 16)
                    else:
                        e.dma_start(SG[r, 1:, c:c + 64], A["hg"][:, h].rearrange("s k v -> k s v")).then_inc(S("states_in"), 16)
                        e.dma_start(SG[q, 1:, 256 + 64 * h:320 + 64 * h], A["gl"][:, h].rearrange("s k v -> k s v")).then_inc(S("states_in"), 16)
            gl_states(False)

            def gl_by_head(n, w, halves):
                m = w // 2
                heads2, heads4 = const("bd_gl")[:, 0:P:64], const("bd_gl")[:, 2 * P:4 * P:64]
                for l in range(1, len(halves) + 1):
                    e.wait_ge(S("gl_qk"), n * 7 + l)
                    if l > 2:
                        e.wait_ge(S("gl_s"), n * 8 + (l - 2))
                    qc, qb = GQC[:, l - 1, :, 0:m], GQB[:, l % 2]
                    o = qb[:, 0:4 * m].rearrange("p (g h t) -> p g h t", g=2, h=2)
                    for g in range(2):
                        e.tensor_tensor(o[:, g], bc(qc[:, g:g + 1], [P, 2, m]), bc(heads2.unsqueeze(2), [P, 2, m]), ALU.mult)
                    o = qb[:, 4 * m:8 * m].rearrange("p (h t) -> p h t", h=4)
                    e.tensor_tensor(o, bc(qc[:, 2:3], [P, 4, m]), bc(heads4.unsqueeze(2), [P, 4, m]),
                                    ALU.mult).then_inc(S("gl_qb"), 1)
            with e.Fori(0, TILES) as n:
                gl_by_head(n, P, HALVES)
            gl_by_head(TILES, LASTW, LHALVES)
            e.wait_ge(S("states_final"), 2)
            gl_states(True)
            e.wait_ge(S("out"), 22 * 16)
            barrier(e, 3)
            e.memset(RSTATE, 0.0).then_inc(S("zeroed"), 1)
            e.wait_ge(S("zeroed"), 3)
            e.dma_start(SHI, A["shift"]).then_inc(S("rw_w"), 16)
            e.dma_start(RWK, A["rw_wa"]).then_inc(S("rw_w"), 16)
            e.dma_start(RGU, A["rw_g"]).then_inc(S("rw_w"), 16)

            def rw_states(out):
                for h in range(4):
                    r = slice(64 * (h % 2), 64 * (h % 2) + 64)
                    c = (h // 2) * P + (h % 2) * 64
                    if out:
                        e.dma_start(OUT["rw"][:, h].rearrange("s k v -> k s v"), RSTATE[r, :, c:c + 64]).then_inc(S("out"), 16)
                    else:
                        e.dma_start(RSTATE[r, 1:, c:c + 64], A["rw"][:, h].rearrange("s k v -> k s v")).then_inc(S("states_in"), 16)
            rw_states(False)
            e.wait_ge(S("shift_ready"), 4)
            e.dma_start(OUT["shift"], SHO).then_inc(S("out"), 16)
            e.wait_ge(S("states_final"), 3)
            rw_states(True)
            barrier(e, 4)
            def wb(j, u):
                e.dma_start(WB[:, u], A["w_br"][bass.ds(j, 1)].rearrange("o p k c -> (o p) k c")).then_inc(S(f"wb{u}"), 16)

            def zrow(r, u):
                e.dma_start(GZ[:, u], A["gates"][bass.ds(r, 1)].rearrange("o p t -> (o p) t")).then_inc(S(f"z{u}"), 16)
            e.wait_ge(S("gt_sent"), (1 + 4 * KD) * 16)
            for u in range(2):
                wb(u, u)
                zrow(u, u)
            e.wait_ge(S("out"), 27 * 16)
            for k in range(KD):
                e.dma_start(XR[:, k, :], xs[k]).then_inc(S("xr"), 16)
            for c in range(2, 8):
                e.wait_ge(S(f"mul{c % 2}"), c // 2 + 1)
                zrow(c, c % 2)
            with e.Fori(1, 4) as jj:
                for c in range(8):
                    if c % 4 == 0:
                        e.wait_ge(S(f"wb_used{c // 4}"), jj)
                        wb(jj * 2 + c // 4, c // 4)
                    e.wait_ge(S(f"mul{c % 2}"), jj * 4 + (c // 2 + 1))
                    zrow(jj * 8 + c, c % 2)
            e.wait_ge(S("xr_ready"), 8)
            for k in range(KD):
                e.dma_start(A["x2"][k], XR[:, k, :]).then_inc(S("spilled"), 16)
            e.wait_ge(S("spilled"), 16 * KD)
            with e.Fori(0, 4) as i:
                for u in range(2):
                    e.wait_ge(S("act_sq"), i * 2 + (u + 1))
                    e.dma_start(A["acts"][bass.ds(i * 2 + u, 1)].rearrange("o p t -> (o p) t"),
                                STG[:, u]).then_inc(S(f"act_spilled{u}"), 16)
            for u in range(2):
                e.wait_ge(S(f"act_spilled{u}"), 4 * 16)
            barrier(e, 5)
            for k in range(KD):
                e.dma_start(ACTB[:, k, :], A["acts"][k]).then_inc(S("act_back"), 16)
            for k in range(KD):
                e.dma_start(HN2[:, k, :], A["x2"][k]).then_inc(S("res_back"), 16)

        @block.gpsimd
        def _(e):
            with nc.allow_non_contiguous_dma(reason="normalisers and stabilisers: a few hundred values"):
                pool_program(e)

        @block.tensor
        def _(e):
            e.wait_ge(S("consts"), 48)
            rms_pe(e, 0)
            e.wait_ge(S("ws"), 16)
            for k in range(KD):
                e.wait_ge(S("ht_ready"), k + 1)
                for g in range(3):
                    last = e.matmul(PS(3 + g, 0, GRP)[0:68], WS[:, k, :], HT[:, k, g * GRP:(g + 1) * GRP],
                                    start=k == 0, stop=k == KD - 1)
            last.then_inc(S("small"), 1)
            barrier(e, 1)
            for p in range(2):
                pe_pair(e, P_ML + p, P_ML + p)
            pe_vpair(e, P_ML + 2, P_ML + 2)
            e.wait_ge(S("ml_rows"), 1)
            e.wait_ge(S("banks_free1"), 3 + 1)
            for q, src in enumerate((RSC, RKH)):
                for g in range(3):
                    last = e.matmul(PS(3 * q + g, 0, GRP), const("sel4", 4), src[:, g * GRP:(g + 1) * GRP],
                                    start=True, stop=True)
            last.then_inc(S("ml_bc"), 1)
            for t in range(TILES + 1):
                w = P if t < TILES else LASTW
                last = e.transpose(PS(6)[0:w, 4 * t:4 * t + 4], RM[:, t * P:t * P + w], ident[0:4, 0:4])
            last.then_inc(S("ml_mt"), 1)
            e.wait_ge(S("ml_go"), 2)

            def ml_tile(n, w, last_tile):
                v = VA[0:w, bass.ds(n, 1)].rearrange("p o h c -> p (o h) c") if not last_tile else VA[0:w, TILES]
                bd4 = const("bd4_l" if last_tile else "bd4", 4)
                e.wait_ge(S("ml_copied"), n + 1)
                e.wait_ge(S("ml_gbd"), n + 1)
                mqh = MQH.rearrange("p h t -> p (h t)")[:, 0:4 * w]
                e.matmul(PS(0, 0, 4 * w)[0:w], MC[:, 1, 0:w], mqh, start=True, stop=True)
                gbd = GBD.rearrange("p h t -> p (h t)")[:, 0:4 * w]
                e.matmul(PS(1, 0, 4 * w)[0:w], ones[0:4, 0:w], gbd, start=True, stop=False)
                e.matmul(PS(1, 0, 4 * w)[0:w], GST[:, 0:w], bd4, start=False, stop=True).then_inc(S("ml_s"), 1)
                e.transpose(PS(2, 0, P)[0:w], MC[:, 3, 0:w], ident).then_inc(S("ml_kt"), 1)
                e.wait_ge(S("ml_att"), n + 1)
                att = MATT.rearrange("p h t -> p (h t)")
                for h in range(4):
                    e.matmul(PS(3, h * 65, h * 65 + 65)[0:w], att[0:w, h * w:h * w + w], v[:, h, :],
                             start=h == 0, stop=False, skip_group_check=True)
                if last_tile:
                    e.wait_ge(S("ml_qx"), 1)
                    for s in range(SEGS):
                        last = e.matmul(PS(3, 0, 260)[0:w], MQX[:, s, :], SM[:, s, :], start=False, stop=s == SEGS - 1,
                                        skip_group_check=True)
                else:
                    last = e.matmul(PS(3, 0, 260)[0:w], MC[:, 2, 0:w], SM[:, 0, :], start=False, stop=True,
                                    skip_group_check=True)
                last.then_inc(S("ml_o"), 1)
                e.wait_ge(S("ml_kh"), n + 1)
                if last_tile:
                    e.wait_ge(S("ml_vx"), 1)
                    for s in range(SEGS):
                        b = [4, 5, 6, 7, 0][s // 2]
                        last = e.matmul(PS(b, (s % 2) * 256, (s % 2) * 256 + 256), MKH[0:w, :], MVX[0:w, s, 0:256],
                                        start=True, stop=True)
                    last.then_inc(S("ml_ds"), 1)
                    e.wait_ge(S("ml_dsu"), 1)
                    for s in range(SEGS):
                        last = e.matmul(PS(4, 4 * s, 4 * s + 4), MKH[0:w, :], MVX[0:w, s, 256:260], start=True, stop=True)
                    last.then_inc(S("ml_ds"), 1)
                else:
                    e.matmul(PS(4, 0, 260), MKH[0:w, :], v.rearrange("p h c -> p (h c)"), start=True, stop=True).then_inc(S("ml_ds"), 1)
                e.wait_ge(S("ml_on"), n + 1)
                for g in range(2):
                    last = e.transpose(PS(5, g * P, g * P + w), MON.rearrange("p h c -> p (h c)")[0:w, g * P:g * P + P],
                                       ident[0:w, 0:w])
                last.then_inc(S("ml_ot"), 1)

            with e.Fori(0, TILES) as n:
                ml_tile(n, P, False)
            ml_tile(TILES, LASTW, True)
            barrier(e, 2)
            with e.Fori(0, 5) as i:
                pe_pair(e, i + P_GL, i + P_GL)
            for q in range(2):
                pe_vpair(e, P_GL + 5 + q, P_GL + 5 + q)
            e.wait_ge(S("wga"), 16)
            for g in range(2):
                last = e.matmul(PS(6 + g, 0, GRP), WGA[0:16, :], GA[0:16, g * GRP:(g + 1) * GRP], start=True, stop=True)
            last.then_inc(S("gl_z"), 1)
            e.wait_ge(S("banks_free0"), 10 + 1)
            e.matmul(PS(0, 0, GRP), WGA[0:16, :], GA[0:16, 2 * GRP:W], start=True, stop=True).then_inc(S("gl_z"), 1)
            e.wait_ge(S("gl_go"), 1)

            def gl_tile(n, w, last_tile):
                x, q = (GXL, GEL) if last_tile else (GX, GE)
                halves = LHALVES if last_tile else HALVES
                nl = len(halves) + 1
                v = GV[0:w, TILES] if last_tile else GV[0:w, bass.ds(n, 1)].rearrange("p o c -> p (o c)")
                att = GATT.rearrange("p h t -> p (h t)")[0:w, 0:8 * w]
                gate = gate_work(e, n, P_G1, 0) if not last_tile else iter(())
                steps(gate, 8)
                for l in range(1, nl + 1):
                    if l >= 3:
                        e.wait_ge(S("gl_att"), n * 8 + l - 2)
                    if l < nl:
                        e.wait_ge(S("gl_qb"), n * 7 + l)
                        m = w // 2
                        for g in range(3):
                            lo, hi = ((0, 2), (2, 4), (4, 8))[g]
                            last = e.matmul(PS(3 * (l % 2), lo * m, hi * m)[0:w], x[:, g, l, 0:w],
                                            GQB[:, l % 2, lo * m:hi * m], start=True, stop=True)
                    else:
                        e.wait_ge(S("gl_dk"), n + 1)
                        for h in (5, 0, 2, 4, 1, 3, 6, 7):
                            r, g = ((slice(64 * (h % 2), 64 * (h % 2) + 64), h // 2) if h < 4
                                    else (slice(32 * (h - 4), 32 * (h - 4) + 32), 2))
                            if h == 7:
                                e.wait_ge(S("gl_third"), n + 1)
                            b, c = GL_DIAG[h]
                            last = e.matmul(PS(3 * (l % 2) + b, c * w, c * w + w)[0:w], x[r, g, nl + 1, 0:w],
                                            q[r, g, 1, 0:w], start=True, stop=True)
                            if h == 5:
                                last.then_inc(S("gl_third"), 1)
                    last.then_inc(S("gl_s"), 1)
                    steps(gate, 1)
                steps(gate, 1)
                e.wait_ge(S("gl_att"), n * 8 + nl)
                e.wait_ge(S("gl_qe"), n + 1)
                for g in range(3):
                    last = e.transpose(PS(2, g * P, g * P + P)[0:w], x[:, g, nl, 0:w], ident)
                last.then_inc(S("gl_kt"), 1)
                if last_tile:
                    e.wait_ge(S("gl_qx"), 1)
                for h in range(8):
                    ao = h * w
                    e.matmul(PS(3, h * 64, h * 64 + 64)[0:w], att[:, ao:ao + w], v[:, h * 64:h * 64 + 64],
                             start=h == 0, stop=False, skip_group_check=True)
                for g in range(3):
                    lo, hi = (g * P, g * P + P) if g < 2 else (256, 512)
                    ns = SEGS if last_tile else 1
                    for s in range(ns):
                        qs = GQX[:, g, s, :] if last_tile else q[:, g, 0, 0:w]
                        last = e.matmul(PS(3, lo, hi)[0:w], qs, SG[:, s, lo:hi], start=False, stop=s == ns - 1,
                                        skip_group_check=True)
                last.then_inc(S("gl_o"), 1)
                e.wait_ge(S("gl_kh"), n + 1)
                if last_tile:
                    for g in range(2):
                        e.wait_ge(S("gl_vx"), 2 * g + 1)
                        for s in range(SEGS):
                            b = [0, 1, 2][s // 4]
                            last = e.matmul(PS(b, (s % 4) * P, (s % 4) * P + P), GKH[0:w, g * P:g * P + P],
                                            GVX[0:w, s, 0:P], start=True, stop=True)
                        last.then_inc(S("gl_ds"), 1)
                        e.wait_ge(S("gl_dsu"), g + 1)
                    e.wait_ge(S("gl_vx"), 5)
                    for s in range(SEGS):
                        b = [0, 1, 2, 3, 4][s // 2]
                        last = e.matmul(PS(b, (s % 2) * 256, (s % 2) * 256 + 256), GKH[0:w, 2 * P:3 * P],
                                        GVX[0:w, s, :], start=True, stop=True)
                    last.then_inc(S("gl_ds"), 1)
                else:
                    for g in range(3):
                        lo, hi = (g * P, g * P + P) if g < 2 else (256, 512)
                        last = e.matmul(PS(4, lo, hi), GKH[0:w, g * P:g * P + P], v[:, lo:hi], start=True, stop=True)
                    last.then_inc(S("gl_ds"), 1)
                steps(gate, 4)
                e.wait_ge(S("gl_on"), n + 1)
                on = GON.rearrange("p h c -> p (h c)")
                for j in range(4):
                    last = e.transpose(PS(5, j * P, j * P + w), on[0:w, j * P:j * P + P], ident[0:w, 0:w])
                last.then_inc(S("gl_ot"), 1)
                steps(gate, 24)

            with e.Fori(0, TILES) as n:
                gl_tile(n, P, False)
            gl_tile(TILES, LASTW, True)
            barrier(e, 3)
            with e.Fori(0, 4) as i:
                pe_pair(e, i + P_RW, i + EV_RW)
            e.wait_ge(S("rw_w"), 48)
            e.wait_ge(S("rw_lora"), 1)
            e.wait_ge(S("banks_free0"), 14 + 1)
            e.wait_ge(S("banks_free1"), 14 + 1)
            c = 0
            for kind in range(3):
                for g in range(2):
                    if c >= 2:
                        e.wait_ge(S("rw_lev"), c - 1)
                    for tg in range(3):
                        rows = [slice(0, 64), slice(64, 128), slice(0, 128)][kind]
                        wl = (RGU if kind == 2 else RWK)[rows, g * P:g * P + P]
                        src = R10[rows, 7 if kind == 2 else 6, tg * GRP:(tg + 1) * GRP]
                        last = e.matmul(PS(3 * (c % 2) + tg, 0, GRP), wl, src, start=True, stop=True)
                    last.then_inc(S("rw_lor"), 1)
                    c += 1
            for kind in range(2):
                for g in range(2):
                    e.wait_ge(S("rw_lev"), c - 1)
                    e.wait_ge(S("rw_hs"), 2 * kind + g + 1)
                    for tg in range(3):
                        last = e.matmul(PS(3 * (c % 2) + tg, 0, GRP), bd2, RX[:, g, tg * GRP:(tg + 1) * GRP],
                                        start=True, stop=True)
                    last.then_inc(S("rw_lor"), 1)
                    c += 1
            e.wait_ge(S("rw_go"), 1)

            def rw_tile(n, w, last_tile):
                levels = LHALVES if last_tile else HALVES
                gate = gate_work(e, n, P_G2, TILES) if not last_tile else iter(())
                e.wait_ge(S("rw_copied"), n + 1)
                for h in range(4):
                    r, g = slice(64 * (h % 2), 64 * (h % 2) + 64), h // 2
                    rhs = RC[r, g:g + 3:2, 0:w]
                    e.matmul(PS(h % 2, g * 2 * w, (g + 1) * 2 * w)[0:w], RC[r, 6 + g, 0:w], rhs, start=True, stop=True)
                    e.matmul(PS(2 + h % 2, g * 2 * w, (g + 1) * 2 * w)[0:w], RC[r, 4 + g, 0:w], rhs, start=True, stop=True)
                    last = e.matmul(PS(4 + h % 2, g * w, g * w + w)[0:w], RC[r, g, 0:w], RC[r, 6 + g, 0:w], start=True, stop=True)
                last.then_inc(S("rw_s"), 1)
                steps(gate, 3)
                tt, ti, m1 = (x.rearrange("p h t -> p (h t)") for x in (RTT, RTI, RM1))
                pb = RPB.rearrange("p h k t -> p (h k t)")
                pk = RPK.rearrange("p h k t -> p (h k t)")
                e.wait_ge(S("rw_t"), n * 14 + 2)
                nlev = len(levels)
                for l in range(1, nlev):
                    lh, m = levels[l], w // 2
                    for h in range(4):
                        last = e.matmul(PS(4, h * m, h * m + m)[0:w], pb[0:w, 2 * h * w:2 * h * w + w],
                                        half(ti[0:w, h * w:h * w + w], lh, False), start=True, stop=True)
                    last.then_inc(S("rw_m"), 1)
                    steps(gate, 1)
                    e.wait_ge(S("rw_m1"), n * 6 + l)
                    for h in range(4):
                        last = e.matmul(PS(0, h * m, h * m + m)[0:w], m1[0:w, h * w:h * w + w],
                                        half(tt[0:w, h * w:h * w + w], lh, True), start=True, stop=True)
                    last.then_inc(S("rw_n"), 1)
                    for h in range(4):
                        last = e.matmul(PS(1, h * m, h * m + m)[0:w], tt[0:w, h * w:h * w + w],
                                        half(m1[0:w, h * w:h * w + w], lh, False), start=True, stop=True)
                    last.then_inc(S("rw_n"), 1)
                    if l == 1:
                        for j in range(4):
                            e.transpose(PS(2, j * P, j * P + P)[0:w], RC[:, 4 + j, 0:w], ident)
                        for j in range(2):
                            last = e.transpose(PS(3, j * P, j * P + P)[0:w], RC[:, 8 + j, 0:w], ident)
                        last.then_inc(S("rw_kt"), 1)
                    steps(gate, 1)
                    e.wait_ge(S("rw_t"), n * 14 + 2 + 2 * l)
                e.wait_ge(S("rw_kv"), n + 1)
                if last_tile:
                    e.wait_ge(S("rw_qx"), 1)
                for k in range(2):
                    bank = 4 if k == 0 else 1
                    if k == 1:
                        steps(gate, 1)
                        e.wait_ge(S("rw_r"), n + 1)
                        for h in range(4):
                            last = e.matmul(PS(5, h * 64, h * 64 + 64)[0:w], tt[0:w, h * w:h * w + w], RRS[0:w, h * 64:h * 64 + 64],
                                            start=True, stop=True)
                        last.then_inc(S("rw_u"), 1)
                    for h in range(4):
                        o = (2 * h + k) * w
                        e.matmul(PS(bank, h * 64, h * 64 + 64)[0:w], pk[0:w, o:o + w], RV[0:w, h * 64:h * 64 + 64],
                                 start=h == 0, stop=False, skip_group_check=True)
                    if k == 1:
                        steps(gate, 1)
                        e.wait_ge(S("rw_us"), n + 1)
                        for h in range(4):
                            o = (2 * h + 1) * w
                            e.matmul(PS(1, h * 64, h * 64 + 64)[0:w], pb[0:w, o:o + w], RUS[0:w, h * 64:h * 64 + 64],
                                     start=False, stop=False, skip_group_check=True)
                    ns = SEGS if last_tile else 1
                    for g in range(2):
                        for s in range(ns):
                            lh = RQX[:, k, g, s, :] if last_tile else RC[:, 2 * k + g, 0:w]
                            x0 = RSTATE[:, s, g * P:g * P + P] if last_tile else RXC[:, g * P:g * P + P]
                            last = e.matmul(PS(bank, g * P, g * P + P)[0:w], lh, x0, start=False, stop=s == ns - 1,
                                            skip_group_check=True)
                    last.then_inc(S("rw_rhs" if k == 0 else "rw_y"), 1)
                if last_tile:
                    e.wait_ge(S("rw_vx"), 1)
                    for g in range(2):
                        for s in range(SEGS):
                            b = [0, 1, 2][s // 4]
                            e.matmul(PS(b, (s % 4) * P, (s % 4) * P + P), RKB[0:w, g * P:g * P + P], RVX[0:w, s, g * P:g * P + P],
                                     start=True, stop=False)
                            last = e.matmul(PS(b, (s % 4) * P, (s % 4) * P + P), RKB[0:w, 256 + g * P:256 + g * P + P],
                                            RUX[0:w, s, g * P:g * P + P], start=False, stop=True)
                        last.then_inc(S("rw_ds"), 1)
                        if g == 0:
                            e.wait_ge(S("rw_dsu"), 1)
                else:
                    for g in range(2):
                        e.matmul(PS(0, g * P, g * P + P), RKB[:, g * P:g * P + P], RV[:, g * P:g * P + P], start=True, stop=False)
                        last = e.matmul(PS(0, g * P, g * P + P), RKB[:, 256 + g * P:256 + g * P + P], RUS[:, g * P:g * P + P],
                                        start=False, stop=True)
                    last.then_inc(S("rw_ds"), 1)
                steps(gate, 4)
                e.wait_ge(S("rw_on"), n + 1)
                for g in range(2):
                    last = e.transpose(PS(3, g * P, g * P + w), RY.rearrange("p h c -> p (h c)")[0:w, g * P:g * P + P],
                                       ident[0:w, 0:w])
                last.then_inc(S("rw_ot"), 1)
                steps(gate, 24)

            with e.Fori(0, TILES) as n:
                rw_tile(n, P, False)
            rw_tile(TILES, LASTW, True)
            barrier(e, 4)
            with e.Fori(0, 4) as jj:
                for v in range(2):
                    e.wait_ge(S(f"wb{v}"), (jj + 1) * 16)
                    for br in range(4):
                        u, c = br % 2, 4 * v + br
                        e.wait_ge(S(f"mul{u}"), jj * 4 + (c // 2 + 1))
                        for tg in range(3):
                            for k in range(2):
                                last = e.matmul(PS(3 * u + tg, 0, GRP), WB[:, v, 2 * br + k, :],
                                                OT[:, 2 * br + k, tg * GRP:(tg + 1) * GRP], start=k == 0, stop=k == 1)
                        last.then_inc(S("pz"), 1)
                    e.drain().then_inc(S(f"wb_used{v}"), 1)
            e.wait_ge(S("mix_ready"), KD)
            with e.Fori(0, 4) as i:
                pe_split_pair(e, i + P_OUT, i + EV_OUT, HT_R, MIX_R)
            e.wait_ge(S("banks_free1"), EV_OUT + 5)
            rms_pe(e, 1, 3)
            e.wait_ge(S("hn_ready"), KD)
            pe_split_pair(e, P_UP, EV_UP, HNH_R, OT_R, lambda: e.wait_ge(S("rstd"), 2))
            with e.Fori(1, 16) as i:
                pe_split_pair(e, i + P_UP, i + EV_UP, HNH_R, OT_R)
            barrier(e, 5)
            with e.Fori(0, 4) as jj:
                for r in range(FF // P):
                    q, b = r // 4, r % 2
                    u = q % 2
                    if r % 4 == 0:
                        e.wait_ge(S(f"split{u}"), jj * 4 + (P_DOWN - P_OUT + q // 2 + 1))
                    e.wait_ge(S("act_parts"), jj * 32 + (r + 1))
                    for v in range(2):
                        if r == 0:
                            e.wait_ge(S(f"down_used{v}"), jj + 1)
                        for g in range(3):
                            t = slice(g * GRP, (g + 1) * GRP)
                            for i, (a_, b_) in enumerate(((WHI_R, AHI_R), (WHI_R, ALO_R), (RING_R, AHI_R))):
                                last = e.matmul(PS(3 * v + g, 0, GRP), a_[:, u, 4 * v + r % 4, :], b_[b][:, t],
                                                start=r == 0 and i == 0, stop=r == 31 and i == 2)
                        if r == 31:
                            last.then_inc(S(f"down{v}"), 1)
                    if r < 31:
                        last.then_inc(S("act_used"), 1)
                    else:
                        e.drain().then_inc(S("act_used"), 1)
                    if r % 4 == 3:
                        e.drain().then_inc(S(f"chunk_done{u}"), 1)
            e.wait_ge(S("down_used0"), 5)
            rms_pe(e, 2)

        @block.scalar
        def _(e):
            exp_ln_table(e)
            st = Steps(e, S("act_step"))
            e.dma_start(WGA[0:16, :], A["w_ga"]).then_inc(S("wga"), 16)
            rms_act(e, st, 0, RST, XT, lambda k: e.wait_ge(S(f"x{k // 2}"), 32))
            e.wait_ge(S("small"), 1)
            e.activation(row3(GA[0:16, :]), cols3(3)[0:16], ACT.Copy)
            st.did(e.activation(row3(GA[32:36, :]), cols3(3)[32:36], ACT.Copy))
            st.did(e.activation(row3(GA[64:68, :]), cols3(3)[64:68], ACT.Copy))
            barrier(e, 1)
            e.sem_inc(S("banks_free0"), 1)
            e.sem_inc(S("gt_free"), 2)
            e.sem_inc(S("gt_sent"), 16)
            e.wait_ge(S("zeroed"), 1)
            e.wait_ge(S("states_in"), 11 * 16)
            fdec = FP[:, :, NP + 3:].rearrange("p g (q c) -> p g q c", q=NSEQ)

            def pre_conv(g):
                def emit(b):
                    lo = 2 * GRP
                    e.activation(FP[:, g, 3:3 + lo].rearrange("p (g c) -> p g c", g=2), cols3(b)[:, 0:2], ACT.Copy)
                    e.activation(FP[:, g, 3 + lo:3 + NP], PS(b + 2, 0, NP - lo), ACT.Copy)
                    return e.activation(fdec[:, g, :, 3:3 + DSEQ],
                                        PS(b + 2, NP - lo, NT - lo).rearrange("p (q c) -> p q c", q=NSEQ), ACT.Copy)
                return emit
            e.activation(RI, GA[32:36, :], ACT.Copy)
            st.did(e.activation(RF, GA[64:68, :], ACT.Copy))
            st.settle()
            e.activation(RI, RI, ACT.Identity, bias=col("mlstm_i_b", 0, 4))
            e.activation(RF, RF, ACT.Identity, bias=col("mlstm_f_b", 0, 4)).then_inc(S("ml_if"), 1)
            evac(e, 0, 0, pre_conv(0))
            e.wait_ge(S("chunk_done1"), 1)
            ins = pre_conv(1)(3)
            ins.then_inc(S("banks_free1"), 1)
            e.wait_ge(S("banks_free1"), 1 + 1)
            e.wait_ge(S("banks_free0"), 1 + 1)
            e.sem_inc(S("conv_ready"), 1)
            for u in range(2):
                evac(e, u, 1, lambda b: e.activation(row3(OT[:, 6 + u, :]), cols3(b), ACT.Sigmoid))
            e.wait_ge(S("ml_if"), 1)
            exp_ln_table(e)
            st.did(e.activation(RT, RF, ACT.Abs))
            st.settle()
            st.did(e.activation(RT, RT, ACT.Exp, scale=-1.0))
            st.settle()
            e.activation(RT, RT, ACT.Ln, bias=1.0).then_inc(S("ml_ln"), 1)
            for u in range(2):
                evac_v(e, u, 2, lambda t: VA[:, 0:TILES, 2 * u:2 * u + 2, 0:64] if t == 0
                       else VA[0:LASTW, TILES, 2 * u:2 * u + 2, 0:64], True)
            e.wait_ge(S("ml_conv"), 1)
            e.activation(M4[:, 0:2, 0:NT], M4[:, 0:2, 0:NT], ACT.Silu).then_inc(S("ml_silu"), 1)
            exp_ln_table(e)
            e.wait_ge(S("ml_bc"), 1)
            e.wait_ge(S("ml_mt"), 1)
            for q in range(2):
                e.activation(row3(M4[:, 2 + q, :]), cols3(3 * q), ACT.Exp)
            mt = PS(6, 0, 36).rearrange("p (t h) -> p t h", h=4)
            e.activation(EMM[:, 0:TILES], mt[:, 0:TILES], ACT.Exp, scale=-1.0)
            e.activation(EMM[0:LASTW, TILES], mt[0:LASTW, TILES], ACT.Exp, scale=-1.0).then_inc(S("ml_sc"), 1)
            e.wait_ge(S("ml_go"), 2)

            def ml_tile(n, w, last_tile):
                src = M4[:, :, TILES * P:NT] if last_tile else M4[:, :, bass.ds(n * P, P)]
                if not last_tile:
                    e.wait_ge(S("ml_pre"), n + 1)
                else:
                    e.wait_ge(S("ml_pre"), TILES + 1)
                e.activation(MC[:, :, 0:w], src, ACT.Copy).then_inc(S("ml_copied"), 1)
                e.wait_ge(S("ml_kt"), n + 1)
                e.activation(MKH[0:w, :], PS(2, 0, P)[0:w], ACT.Copy).then_inc(S("ml_kh"), 1)
                x = MX.rearrange("p h t -> p (h t)")[0:w, 0:4 * w]
                e.wait_ge(S("ml_x"), n + 1)
                e.activation(x, x, ACT.Exp).then_inc(S("ml_e"), 1)
                e.wait_ge(S("ml_o"), n + 1)
                num = PS(3, 0, 260).rearrange("p (h c) -> p h c", h=4)[0:w, :, 0:64]
                e.activation(MSQ[0:w], num, ACT.Square, scale=0.125).then_inc(S("ml_sq"), 1)
                e.wait_ge(S("ml_ms"), n + 1)
                rstd(e, st, MS[0:w, 6], MS[0:w, 5]).then_inc(S("ml_rs"), 1)
            with e.Fori(0, TILES) as n:
                st.enter(n, 1)
                ml_tile(n, P, False)
            st.leave(TILES)
            ml_tile(TILES, LASTW, True)
            barrier(e, 2)
            evac(e, 0, 3, lambda b: e.activation(row3(GQ[:, 0]), cols3(b), ACT.Copy))
            evac(e, 0, 4, lambda b: e.activation(row3(GB[:, 0]), cols3(b), ACT.Copy))
            for u in range(2):
                evac(e, u, 5, lambda b: e.activation(row3(OT[:, u]), cols3(b), ACT.Silu))
            evac(e, 0, 6, lambda b: e.activation(row3(GQ[:, 2]), cols3(b), ACT.Copy, scale=32 ** -0.5))
            for u in range(2):
                evac(e, u, 7, lambda b: e.activation(row3(OT[:, 4 + u]), cols3(b), ACT.Silu))
            for q in range(2):
                evac_v(e, 0, 8 + q, lambda t: GV[:, 0:TILES, 256 * q:256 * q + P] if t == 0
                       else GV[0:LASTW, TILES, 256 * q:256 * q + P], True)
            e.wait_ge(S("gl_z"), 2)
            e.activation(GB[:, 2, 0:2 * GRP].rearrange("p (g c) -> p g c", g=2),
                         PSt[:, 6 * 512:].rearrange("p (g c) -> p g c", g=2)[:, :, 0:GRP], ACT.Identity, bias=col("gla_gate_b"))
            e.activation(GB[:, 2, 2 * GRP:W], PS(0, 0, GRP), ACT.Identity, bias=col("gla_gate_b")).then_inc(S("gl_zz"), 1)
            e.wait_ge(S("gl_f"), 1)
            e.activation(GK[:, 0:2], GB[:, 0:2], ACT.Sigmoid, scale=-1.0)
            e.wait_ge(S("gl_zz"), 1)
            exp_ln_table(e)
            st.did(e.activation(GT, GB, ACT.Abs))
            st.settle()
            st.did(e.activation(GT, GT, ACT.Exp, scale=-1.0))
            st.settle()
            e.activation(GT, GT, ACT.Ln, bias=1.0).then_inc(S("gl_ln"), 1)

            def gl_tile(n, w, last_tile):
                x, q = (GXL, GEL) if last_tile else (GX, GE)
                nl = len(LHALVES if last_tile else HALVES) + 1

                def tile_of(y):
                    return y[:, :, TILES * P:NT] if last_tile else y[:, :, bass.ds(n * P, P)]
                e.wait_ge(S("gl_x"), 2 * n + 1)
                e.activation(x[:, :, 1:nl, :], x[:, :, 1:nl, :], ACT.Exp).then_inc(S("gl_e"), 1)
                e.wait_ge(S("gl_x"), 2 * n + 2)
                e.activation(x[:, :, 0:nl + 1:nl, :], x[:, :, 0:nl + 1:nl, :], ACT.Exp).then_inc(S("gl_e"), 1)
                e.activation(x[:, :, nl + 1, :], tile_of(GK), ACT.Copy)
                e.activation(q[:, :, 1, :], tile_of(GQ), ACT.Copy).then_inc(S("gl_dk"), 1)
                if not last_tile:
                    for c in range(4):
                        gate_out(e, n, c, 0)
                e.wait_ge(S("gl_kt"), n + 1)
                e.activation(GKH[0:w, :], PS(2, 0, 3 * P)[0:w], ACT.Copy).then_inc(S("gl_kh"), 1)
                e.wait_ge(S("gl_o"), n + 1)
                e.activation(GSQ.rearrange("p h c -> p (h c)")[0:w], PS(3)[0:w], ACT.Square, scale=0.125).then_inc(S("gl_sq"), 1)
                e.wait_ge(S("gl_ms"), n + 1)
                rstd(e, st, GMS[0:w, 1], GMS[0:w, 0]).then_inc(S("gl_rs"), 1)
                if not last_tile:
                    for c in range(4, 6):
                        gate_out(e, n, c, 0)
            with e.Fori(0, TILES) as n:
                st.enter(n, 1)
                gl_tile(n, P, False)
            st.leave(TILES)
            gl_tile(TILES, LASTW, True)
            barrier(e, 3)
            with e.Fori(0, 4) as i:
                e.wait_ge(S("chunk_done0"), i + P_RW + 1)
                e.activation(row3(R10[:, bass.ds(i * 2, 1), :].rearrange("p o t -> p (o t)")), cols3(0),
                             ACT.Copy).then_inc(S("banks_free0"), 1)
            e.wait_ge(S("rw_mix"), 4)
            e.activation(R10[0:64, 6, :], R10[0:64, 6, :], ACT.Tanh)
            e.activation(R10[:, 7, :], R10[:, 7, :], ACT.Sigmoid).then_inc(S("rw_lora"), 1)
            e.activation(R10[:, 8:10], R10[:, 4:6], ACT.Copy)
            for c in range(6):
                e.wait_ge(S("rw_lor"), c + 1)
                g, src = c % 2, cols3(3 * (c % 2))
                dst = (RWL, RA)[c // 2][:, g] if c < 4 else OT[:, 2 + g]
                if c < 2:
                    e.activation(row3(dst), src, ACT.Sigmoid, bias=col("rwkv_w0", g)).then_inc(S("rw_lev"), 1)
                elif c < 4:
                    e.activation(row3(dst), src, ACT.Sigmoid, bias=col("rwkv_a0", g)).then_inc(S("rw_lev"), 1)
                else:
                    e.activation(row3(dst), src, ACT.Copy).then_inc(S("rw_lev"), 1)
            e.wait_ge(S("rw_kkr"), 1)
            for g in range(2):
                e.activation(RX[:, g], RKK[:, g], ACT.Square).then_inc(S("rw_hs"), 1)
            for g in range(2):
                e.wait_ge(S("rw_lor"), 7 + g)
                e.activation(row3(RE[:, g]), cols3(3 * g), ACT.Sqrt).then_inc(S("rw_lev"), 1)
            exp_ln_table(e)
            e.wait_ge(S("rw_wlx"), 1)
            e.activation(REC, RCS, ACT.Exp, scale=-DECAY)
            e.wait_ge(S("rw_ex_used"), 1)
            e.activation(RE, RWL, ACT.Exp, scale=-DECAY).then_inc(S("rw_ex"), 1)
            e.wait_ge(S("rw_ex_used"), 2)
            e.activation(RE, RWL, ACT.Exp, scale=DECAY).then_inc(S("rw_ex"), 1)
            e.wait_ge(S("rw_ex_used"), 3)
            e.activation(RE, RBV, ACT.Exp, scale=-DECAY).then_inc(S("rw_ex"), 1)
            e.wait_ge(S("rw_go"), 1)

            def rw_tile(n, w, last_tile, first=False):
                src = R10[:, :, TILES * P:NT] if last_tile else R10[:, :, bass.ds(n * P, P)]
                e.wait_ge(S("rw_pre"), n + 1)
                e.activation(RC[:, :, 0:w], src, ACT.Copy).then_inc(S("rw_copied"), 1)
                if not first:
                    gate_out(e, n - 1, 5, TILES)
                levels = LHALVES if last_tile else HALVES
                nlev = len(levels)
                m1 = RM1.rearrange("p h t -> p (h t)")[0:w, 0:4 * w].rearrange("p (h t) -> p h t", h=4)
                for l in range(1, nlev):
                    e.wait_ge(S("rw_m"), n * 6 + l)
                    h = levels[l]
                    e.activation(half(m1, h, False), PS(4, 0, 2 * w)[0:w].rearrange("p (a n t) -> p a n t", a=4, t=h),
                                 ACT.Copy).then_inc(S("rw_m1"), 1)
                    if l % 2 and not last_tile:
                        gate_out(e, n, l // 2, TILES)
                    if l == 1:
                        e.wait_ge(S("rw_kt"), n + 1)
                        e.activation(RKB[0:w], PS(2)[0:w], ACT.Copy)
                        e.activation(RV[0:w], PS(3, 0, 256)[0:w], ACT.Copy).then_inc(S("rw_kv"), 1)
                e.wait_ge(S("rw_rhs"), n + 1)
                e.activation(RRS[0:w], PS(4, 0, 256)[0:w], ACT.Copy).then_inc(S("rw_r"), 1)
                e.wait_ge(S("rw_u"), n + 1)
                e.activation(RUS[0:w], PS(5, 0, 256)[0:w], ACT.Copy).then_inc(S("rw_us"), 1)
                if not last_tile:
                    gate_out(e, n, 3, TILES)
                e.wait_ge(S("rw_yc"), n + 1)
                e.activation(RSQ[0:w], RY[0:w], ACT.Square, scale=0.125).then_inc(S("rw_sq"), 1)
                e.wait_ge(S("rw_ms"), n + 1)
                rstd(e, st, RMS_[0:w, 3], RMS_[0:w, 2], LN_EPS).then_inc(S("rw_rs"), 1)
                if not last_tile:
                    gate_out(e, n, 4, TILES)
            rw_tile(0, P, False, True)
            with e.Fori(1, TILES) as n:
                st.enter(n - 1, 1)
                rw_tile(n, P, False)
            st.leave(TILES - 1)
            rw_tile(TILES, LASTW, True)
            barrier(e, 4)
            with e.Fori(0, 4) as jj:
                for c in range(8):
                    u = c % 2
                    e.wait_ge(S(f"z{u}"), (jj * 4 + (c // 2 + 1)) * 16)
                    e.activation(GZ[:, u], GZ[:, u], ACT.Sigmoid).then_inc(S("sig"), 1)
            exp_ln_table(e)
            rms_act(e, st, 1, RST2, XR, lambda k: e.wait_ge(S("xr_ready"), k + 1), 3)
            for lo, n, base in ((0, 8, ACTA), (8, 4, HT)):
                with e.Fori(0, n) as i:
                    for u in range(2):
                        e.wait_ge(S(f"banks_free{u}"), i + (EV_UP + lo + 2))
                        x = base[:, bass.ds(i * 2 + u, 1), :].rearrange("p o t -> p (o t)")
                        e.activation(x, x, ACT.Square)
            with e.Fori(0, 4) as i:
                for u in range(2):
                    e.wait_ge(S(f"banks_free{u}"), i + (EV_UP + 14))
                    e.activation(STG[:, u], STG[:, u], ACT.Square).then_inc(S("act_sq"), 1)
            barrier(e, 5)
            with e.Fori(0, 4) as jj:
                for r in range(FF // P):
                    if r == 24:
                        e.wait_ge(S("act_back"), 8 * 16)
                    e.wait_ge(S("act_used"), jj * 32 + (r + 1))
                    e.activation(AHI_R[r % 2], act_row(r), ACT.Copy).then_inc(S("act_hi"), 1)
            e.wait_ge(S("dn_ready"), KD)
            rms_act(e, st, 2, SQ3R, HN2)

        @block.vector
        def _(e):
            st = Steps(e, S("dve_step"))
            e.wait_ge(S("consts"), 48)
            e.tensor_copy(CU[:, :], CUF)
            rms_dve(e, 0, RST, XT, HT, "norm_mix", lambda ins: ins.then_inc(S("ht_ready"), 1))
            barrier(e, 1)
            e.sem_inc(S("banks_free1"), 1)
            e.sem_inc(S("down_used0"), 1)
            e.sem_inc(S("act_used"), 2)
            e.sem_inc(S("mul0"), 1)
            e.sem_inc(S("mul1"), 1)
            e.sem_inc(S("down_used1"), 1)
            e.sem_inc(S("ml_pre"), 1)
            e.sem_inc(S("rw_pre"), 1)
            e.wait_ge(S("ml_if"), 1)
            e.wait_ge(S("ml_ln"), 1)
            st.did(e.scalar_tensor_tensor(RF, RF, 0.0, RT, ALU.min, ALU.subtract))
            st.settle()
            e.wait_ge(S("zeroed"), 1)
            e.wait_ge(S("states_in"), 11 * 16)
            e.memset(RM[:, NT:W], 0.0)
            st.did(e.tensor_tensor_scan(RB, keep[0:4], RF, 0.0, ALU.mult, ALU.add))
            st.did(e.tensor_tensor_scan(RM[:, 0:NP], RF[:, 0:NP], RI[:, 0:NP], 0.0, ALU.add, ALU.max))

            def dec(x, k=None):
                x = x[:, NP:NT].rearrange("p (q c) -> p q c", q=NSEQ)
                return x if k is None else x[:, :, k]
            for k in range(DSEQ):
                prev = RM0[:, 12:20] if k == 0 else dec(RM, k - 1)
                st.did(e.tensor_tensor(dec(RM, k), dec(RF, k), prev, ALU.add))
                st.settle()
                st.did(e.tensor_tensor(dec(RM, k), dec(RM, k), dec(RI, k), ALU.max))
                st.settle()
            ends = RM[:, 0:TILES * P].rearrange("p (n t) -> p n t", t=P)[:, :, P - 1]
            st.did(e.tensor_copy(RM0[:, 1:TILES + 1], ends))
            e.tensor_tensor(RNG, RB, RM, ALU.subtract)
            st.did(e.tensor_tensor(RG, RI, RB, ALU.subtract))
            st.settle()

            def parts(x):
                return (x[:, 0:TILES * P].rearrange("p (n t) -> p n t", t=P),
                        x[:, TILES * P:NP].rearrange("p (n t) -> p n t", n=1),
                        x[:, NP:NT].rearrange("p (n t) -> p n t", t=DSEQ))
            m0s = (RM0[:, 0:TILES], RM0[:, TILES:TILES + 1], RM0[:, 12:20])
            e.memset(RSC[:, NT:W], 0.0)
            e.memset(RKH[:, NT:W], 0.0)
            for q in range(3):
                o, x = parts(RSC)[q], parts(RNG)[q]
                e.tensor_tensor(o, x, bc(m0s[q].unsqueeze(2), x.shape), ALU.add)
                o, x, y = parts(RKH)[q], parts(RG)[q], parts(RNG)[q]
                ins = e.tensor_tensor(o, x, bc(y[:, :, x.shape[2] - 1:x.shape[2]], x.shape), ALU.add)
            ins.then_inc(S("ml_rows"), 1)
            e.wait_ge(S("banks_free0"), 2)
            e.wait_ge(S("banks_free1"), 2)
            fdec = FP[:, :, NP + 3:].rearrange("p g (q c) -> p g q c", q=NSEQ)
            e.sem_inc(S("conv_ready"), 1)
            for j in range(4):
                for g in range(2):
                    cw = col("mlstm_conv_w", 2 * j + g)
                    po, pi = M4[:, g, 0:NP], FP[:, g, j:j + NP]
                    do, di = dec(M4[:, g]), fdec[:, g, :, j:j + DSEQ]
                    if j == 0:
                        e.tensor_scalar(po, pi, cw, col("mlstm_conv_b", g), ALU.mult, ALU.add)
                        ins = e.tensor_scalar(do, di, cw, col("mlstm_conv_b", g), ALU.mult, ALU.add)
                    else:
                        e.scalar_tensor_tensor(po, pi, cw, po, ALU.mult, ALU.add)
                        ins = e.scalar_tensor_tensor(do, di, cw, do, ALU.mult, ALU.add)
                if j < 3:
                    st.did(ins)
                    st.settle()
            ins.then_inc(S("ml_conv"), 1)
            e.wait_ge(S("ml_silu"), 1)
            st.did(e.tensor_scalar(M4[:, 1, :], M4[:, 1, :], 32 ** -0.5, None, ALU.mult))
            e.wait_ge(S("ml_sc"), 1)
            ins = e.tensor_copy(MSL[:, 0:TILES], M4[:, 2, 0:TILES * P].rearrange("p (n t) -> p n t", t=P)[:, :, P - 1])
            e.tensor_copy(MES[:, 0:1], M4[:, 2, NP - 1:NP])
            st.did(e.tensor_copy(MES[:, 1:], dec(M4[:, 2])[:, :, DSEQ - 1]))
            st.settle()
            e.tensor_tensor(M4[:, 2, :], M4[:, 2, :], M4[:, 0, :], ALU.mult)
            e.tensor_tensor(M4[:, 3, :], M4[:, 3, :], M4[:, 1, :], ALU.mult).then_inc(S("ml_go"), 2)

            def ml_tile(n, w, last_tile):
                def tile_of(x):
                    return x[:, TILES * P:NT] if last_tile else x[:, bass.ds(n * P, P)]
                bd4 = const("bd4_l" if last_tile else "bd4", 4).rearrange("p (h t) -> p h t", h=4)
                neg = const("neg_l" if last_tile else "neg", w)
                h4 = [w, 4, w]
                gbd = GBD.rearrange("p h t -> p (h t)")[:, 0:4 * w].rearrange("p (h t) -> p h t", h=4)
                mqh = MQH.rearrange("p h t -> p (h t)")[:, 0:4 * w].rearrange("p (h t) -> p h t", h=4)
                e.tensor_tensor(mqh, bc(tile_of(M4[:, 0]).unsqueeze(1), [P, 4, w]),
                                bc(const("head4").unsqueeze(2), [P, 4, w]), ALU.mult)
                e.tensor_tensor(gbd, bc(tile_of(RNG).unsqueeze(1), [4, 4, w]), bd4, ALU.mult)
                e.tensor_copy(GST[:, 0:w], tile_of(RG)).then_inc(S("ml_gbd"), 1)
                x = MX.rearrange("p h t -> p (h t)")[0:w, 0:4 * w].rearrange("p (h t) -> p h t", h=4)
                att = MATT.rearrange("p h t -> p (h t)")[0:w, 0:4 * w].rearrange("p (h t) -> p h t", h=4)
                pq = [PS(k, 0, 4 * w)[0:w].rearrange("p (h t) -> p h t", h=4) for k in range(2)]
                if last_tile:
                    e.wait_ge(S("ml_copied"), TILES + 1)
                    e.tensor_tensor(MQX, bc(MC[:, 2, 0:w].unsqueeze(1), [P, SEGS, w]),
                                    const("ind_t").rearrange("p (s t) -> p s t", s=SEGS), ALU.mult).then_inc(S("ml_qx"), 1)
                    for s in range(SEGS):
                        ins = e.tensor_scalar(MVX[0:w, s, :], VA[0:w, TILES].rearrange("p h c -> p (h c)"),
                                              const("ind_p", w)[:, s:s + 1], None, ALU.mult)
                    ins.then_inc(S("ml_vx"), 1)
                e.wait_ge(S("ml_s"), n + 1)
                e.tensor_tensor(x, pq[1], bc(neg.unsqueeze(1), h4), ALU.min).then_inc(S("ml_x"), 1)
                e.wait_ge(S("ml_e"), n + 1)
                e.tensor_tensor(att, pq[0], x, ALU.mult).then_inc(S("ml_att"), 1)
                o = PS(3, 0, 260).rearrange("p (h c) -> p h c", h=4)[0:w]
                emm = EMM[0:w, TILES] if last_tile else EMM[:, bass.ds(n, 1)].rearrange("p o h -> p (o h)")
                m = [MS[0:w, k] for k in range(8)]
                e.wait_ge(S("ml_sq"), n + 1)
                st.did(e.tensor_scalar(m[4], o[:, :, 64], -1.0, None, ALU.mult))
                st.settle()
                st.did(e.tensor_tensor(m[0], m[4], o[:, :, 64], ALU.max))
                st.settle()
                st.did(e.tensor_tensor(m[1], m[0], emm, ALU.max))
                st.settle()
                e.reciprocal(m[2], m[1])
                st.did(e.tensor_reduce(m[3], MSQ[0:w], AX.X, ALU.add))
                st.settle()
                st.did(e.tensor_tensor(m[4], m[3], m[2], ALU.mult))
                st.settle()
                e.tensor_tensor(m[5], m[4], m[2], ALU.mult).then_inc(S("ml_ms"), 1)
                e.wait_ge(S("ml_rs"), n + 1)
                st.did(e.tensor_tensor(m[7], m[6], m[2], ALU.mult))
                st.settle()
                e.tensor_tensor(MON[0:w], o[:, :, 0:64], bc(m[7].unsqueeze(2), [w, 4, 64]), ALU.mult).then_inc(S("ml_on"), 1)
                bdm = const("bd_ml")
                if last_tile:
                    e.wait_ge(S("ml_ds"), TILES + 1)
                    st.did(e.tensor_tensor(SM, SM, bc(MES.unsqueeze(2), [P, SEGS, 260]), ALU.mult))
                    for s in range(SEGS):
                        b = [4, 5, 6, 7, 0][s // 2]
                        ins = e.tensor_tensor(MVX[:, s, 0:256], PS(b, (s % 2) * 256, (s % 2) * 256 + 256), bdm[:, 0:256], ALU.mult)
                    st.did(ins)
                    e.wait_ge(S("dve_step"), st.n)
                    e.sem_inc(S("ml_dsu"), 1)
                    e.wait_ge(S("ml_ds"), TILES + 2)
                    st.did(e.tensor_tensor(MVX[:, :, 256:260], PS(4, 0, 36).rearrange("p (s c) -> p s c", c=4),
                                           bc(bdm[:, 256:260].unsqueeze(1), [P, SEGS, 4]), ALU.mult))
                    st.settle()
                    e.tensor_tensor(SM, SM, MVX, ALU.add).then_inc(S("states_final"), 1)
                else:
                    e.wait_ge(S("ml_ds"), n + 1)
                    st.did(e.tensor_tensor(MTMP, PS(4, 0, 260), bdm, ALU.mult))
                    st.settle()
                    sl = MSL[:, bass.ds(n, 1)]
                    st.did(e.scalar_tensor_tensor(SM[:, 0, :], SM[:, 0, :], sl, MTMP, ALU.mult, ALU.add))
                    st.settle()
                e.wait_ge(S("ml_ot"), n + 1)
                for g in range(2):
                    ot = tile_of(OT[:, 6 + g])
                    ins = e.scalar_tensor_tensor(ot, PS(5, g * P, g * P + w), col("mlstm_norm", g), ot, ALU.mult, ALU.mult)
                ins.then_inc(S("ml_pre"), 1)

            with e.Fori(0, TILES) as n:
                st.enter(n, 8)
                ml_tile(n, P, False)
            st.leave(TILES)
            ml_tile(TILES, LASTW, True)
            barrier(e, 2)
            evac(e, 1, 3, lambda b: e.tensor_copy(row3(GQ[:, 1]), cols3(b)))
            evac(e, 1, 4, lambda b: e.tensor_copy(row3(GB[:, 1]), cols3(b)))
            evac(e, 1, 6, lambda b: e.tensor_copy(row3(GK[:, 2]), cols3(b)))
            e.wait_ge(S("banks_free1"), 8)
            e.sem_inc(S("gl_f"), 1)
            for q in range(2):
                evac_v(e, 1, 8 + q, lambda t: GV[:, 0:TILES, 256 * q + P:256 * q + 2 * P] if t == 0
                       else GV[0:LASTW, TILES, 256 * q + P:256 * q + 2 * P], False)
            e.wait_ge(S("gl_zz"), 1)
            e.wait_ge(S("gl_ln"), 1)
            st.did(e.scalar_tensor_tensor(GL_, GB, 0.0, GT, ALU.min, ALU.subtract))
            st.settle()
            st.did(e.tensor_scalar(GL_[:, 2], GL_[:, 2], 1.0 / 16, None, ALU.mult))
            st.settle()
            for g in range(3):
                st.did(e.tensor_tensor_scan(GB[:, g], keep, GL_[:, g], 0.0, ALU.mult, ALU.add))
            st.settle()
            e.wait_ge(S("zeroed"), 2)
            e.wait_ge(S("states_in"), (11 + 8) * 16)
            e.sem_inc(S("gl_go"), 1)

            def gl_tile(n, w, last_tile):
                x, q = (GXL, GEL) if last_tile else (GX, GE)
                halves = LHALVES if last_tile else HALVES
                nl = len(halves) + 1

                def tile_of(y):
                    i = (slice(None),) * (len(y.shape) - 1)
                    return y[i + (slice(TILES * P, NT),)] if last_tile else y[i + (bass.ds(n * P, P),)]
                b = tile_of(GB)
                for l, h in enumerate(halves):
                    o = x[:, :, l + 1, :]
                    bb = b.rearrange("p g (n t) -> p g n t", t=2 * h)
                    mid = bc(bb[:, :, :, h - 1:h], [P, 3, w // (2 * h), h])
                    e.tensor_tensor(half(o, h, False), mid, bb[:, :, :, 0:h], ALU.subtract)
                    ins = e.tensor_tensor(half(o, h, True), bb[:, :, :, h:], mid, ALU.subtract)
                ins.then_inc(S("gl_x"), 1)
                e.tensor_copy(x[:, :, 0, :], b)
                if last_tile:
                    for lo, hi, m in ((0, TAIL, TAIL), (TAIL, w, DSEQ)):
                        o = x[:, :, nl, lo:hi].rearrange("p g (n t) -> p g n t", t=m)
                        bb = b[:, :, lo:hi].rearrange("p g (n t) -> p g n t", t=m)
                        ins = e.tensor_tensor(o, bc(bb[:, :, :, m - 1:m], o.shape), bb, ALU.subtract)
                else:
                    ins = e.tensor_tensor(x[:, :, nl, :], bc(b[:, :, P - 1:P], b.shape), b, ALU.subtract)
                ins.then_inc(S("gl_x"), 1)
                qt, kt = tile_of(GQ), tile_of(GK)
                e.wait_ge(S("gl_e"), 2 * n + 1)
                for l, h in enumerate(halves):
                    o = half(x[:, :, l + 1, :], h, False)
                    e.tensor_tensor(o, o, half(kt, h, False), ALU.mult)
                    o = GQC[:, l, :, 0:w // 2].rearrange("p g (n t) -> p g n t", t=h)
                    e.tensor_tensor(o, half(x[:, :, l + 1, :], h, True), half(qt, h, True), ALU.mult).then_inc(S("gl_qk"), 1)
                e.wait_ge(S("gl_e"), 2 * n + 2)
                st.did(e.tensor_tensor(q[:, :, 0, :], x[:, :, 0, :], qt, ALU.mult))
                if last_tile:
                    st.settle()
                    e.tensor_copy(GES[:, :, 0], x[:, :, 0, TAIL - 1])
                    st.did(e.tensor_copy(GES[:, :, 1:], x[:, :, 0, TAIL:w].rearrange("p g (q c) -> p g q c", c=DSEQ)[:, :, :, DSEQ - 1]))
                    for g in range(3):
                        ins = e.tensor_tensor(GQX[:, g], bc(q[:, g, 0:1, :], [P, SEGS, w]),
                                              const("ind_t").rearrange("p (s t) -> p s t", s=SEGS), ALU.mult)
                    ins.then_inc(S("gl_qx"), 1)
                e.tensor_tensor(x[:, :, nl, :], x[:, :, nl, :], kt, ALU.mult).then_inc(S("gl_qe"), 1)
                att = GATT.rearrange("p h t -> p (h t)")[0:w, 0:8 * w].rearrange("p (h t) -> p h t", h=8)
                if last_tile:
                    st.did(e.memset(att, 0.0))
                    st.settle()
                for l in range(1, nl + 1):
                    if l >= 2:
                        e.wait_ge(S("gl_att"), n * 8 + l - 1)
                    e.wait_ge(S("gl_s"), n * 8 + l)
                    m = mask8("ll" if last_tile else "lv", l - 1, w)
                    e.sem_inc(S("select_turn"), 1)
                    if l < nl:
                        h = halves[l - 1]
                        dst = half(att, h, True)
                        ins = e.copy_predicated(dst, bc(half(m, h, True).unsqueeze(1), dst.shape),
                                                PS(3 * (l % 2), 0, 4 * w)[0:w].rearrange("p (a n t) -> p a n t", a=8, t=h))
                    else:
                        for heads in (slice(0, 5, 2), slice(1, 4, 2), slice(6, 7), slice(5, 8, 2)):
                            b, c = GL_DIAG[heads.start]
                            dst = att[:, heads]
                            k = dst.shape[1]
                            ins = e.copy_predicated(dst, bc(m.unsqueeze(1), dst.shape), PS(
                                3 * (l % 2) + b, c * w, (c + k) * w)[0:w].rearrange("p (a t) -> p a t", a=k))
                    ins.then_inc(S("gl_att"), 1)
                e.wait_ge(S("gl_kh"), n + 1) if last_tile else None
                bdm = const("bd_gl")
                if not last_tile:
                    e.wait_ge(S("gl_ds"), n + 1)
                    st.did(e.tensor_tensor(GTMP, PS(4), bdm, ALU.mult))
                    st.settle()
                    for g in range(3):
                        lo, hi = (g * P, g * P + P) if g < 2 else (256, 512)
                        ins = e.scalar_tensor_tensor(SG[:, 0, lo:hi], SG[:, 0, lo:hi], x[:, g, 0, P - 1:P], GTMP[:, lo:hi], ALU.mult, ALU.add)
                    st.did(ins)
                e.wait_ge(S("gl_sq"), n + 1)
                e.tensor_reduce(GMS[0:w, 0], GSQ[0:w], AX.X, ALU.add).then_inc(S("gl_ms"), 1)
                e.wait_ge(S("gl_rs"), n + 1)
                o = PS(3).rearrange("p (h c) -> p h c", h=8)[0:w]
                e.tensor_tensor(GON[0:w], o, bc(GMS[0:w, 1].unsqueeze(2), [w, 8, 64]), ALU.mult).then_inc(S("gl_on"), 1)
                if last_tile:
                    for g in range(3):
                        lo, hi = (g * P, g * P + P) if g < 2 else (256, 512)
                        if g:
                            e.wait_ge(S("gl_ds"), TILES + g)
                        for s in range(SEGS):
                            ins = e.tensor_scalar(GVX[0:w, s, 0:hi - lo], GV[0:w, TILES, lo:hi], const("ind_p", w)[:, s:s + 1], None, ALU.mult)
                        ins.then_inc(S("gl_vx"), 1)
                        m = hi - lo
                        sg = SG[:, :, lo:hi]
                        st.did(e.tensor_tensor(sg, sg, bc(GES[:, g].unsqueeze(2), [P, SEGS, m]), ALU.mult))
                        e.wait_ge(S("gl_ds"), TILES + g + 1)
                        st.settle()
                        per = 4 if g < 2 else 2
                        for s in range(SEGS):
                            o_ = (s // per) * 512 + (s % per) * m
                            ins = e.tensor_tensor(GTMPL[:, s, 0:m], PSt[:, o_:o_ + m], bdm[:, lo:hi], ALU.mult)
                        st.did(ins)
                        st.settle()
                        ins = e.tensor_tensor(sg, sg, GTMPL[:, :, 0:m], ALU.add)
                        if g < 2:
                            st.did(ins)
                            st.settle()
                            e.sem_inc(S("gl_dsu"), 1)
                            e.sem_inc(S("gl_vx"), 1)
                        else:
                            ins.then_inc(S("states_final"), 1)
                e.wait_ge(S("gl_ot"), n + 1)
                for j in range(4):
                    slot = (0, 1, 4, 5)[j]
                    ot = tile_of(OT[:, slot])
                    c = col("hgrn_norm", j) if j < 2 else col("gla_norm", j - 2)
                    ins = e.scalar_tensor_tensor(ot, PS(5, j * P, j * P + w), c, ot, ALU.mult, ALU.mult)
                st.did(ins)

            with e.Fori(0, TILES) as n:
                st.enter(n, 4)
                gl_tile(n, P, False)
            st.leave(TILES)
            gl_tile(TILES, LASTW, True)
            barrier(e, 3)
            z = R10[:, 0:8]
            e.wait_ge(S("rw_w"), 48)
            with e.Fori(0, 4) as i:
                st.enter(i, 2)
                e.wait_ge(S("chunk_done1"), i + P_RW + 1)
                e.tensor_copy(row3(R10[:, bass.ds(i * 2 + 1, 1), :].rearrange("p o t -> p (o t)")), cols3(3)).then_inc(S("banks_free1"), 1)
                for u in range(2):
                    e.wait_ge(S(f"banks_free{u}"), i + (EV_RW + 2))
                zp, rd = z[:, bass.ds(i * 2, 2)], RD[:, bass.ds(i * 2, 2)]
                zd = zp[:, :, NP:NT].rearrange("p s (q c) -> p s q c", c=DSEQ)
                rdd = rd[:, :, NP:NT].rearrange("p s (q c) -> p s q c", c=DSEQ)
                sho = SHO[:, bass.ds(i * 2, 2)]
                e.tensor_copy(sho[:, :, 0:1], zp[:, :, NP - 1:NP])
                e.tensor_copy(sho[:, :, 1:], zd[:, :, :, DSEQ - 1]).then_inc(S("shift_ready"), 1)
                st.did(e.tensor_tensor(rd[:, :, 1:W], zp[:, :, 0:W - 1], zp[:, :, 1:W], ALU.subtract))
                e.tensor_scalar(rd[:, :, 0:1], zp[:, :, 0:1], -1.0, None, ALU.mult)
                st.settle()
                st.did(e.tensor_tensor(rdd[:, :, :, 0], SHI[:, bass.ds(i * 2, 2)], zd[:, :, :, 0], ALU.subtract))
                st.settle()
                for q in range(2):
                    zs, rs = (y[:, bass.ds(i * 2 + q, 1)].rearrange("p o t -> p (o t)") for y in (z, RD))
                    ins = e.scalar_tensor_tensor(zs, rs, CC[:, bass.ds(i * 2 + (COLS["rwkv_mu"][0] + q), 1)], zs, ALU.mult, ALU.add)
                ins.then_inc(S("rw_mix"), 1)
            st.leave(4)
            e.wait_ge(S("rw_mix"), 4)
            for g in range(2):
                ins = e.tensor_scalar(RKK[:, g], z[:, 2 + g], col("rwkv_k_k", g), None, ALU.mult)
            ins.then_inc(S("rw_kkr"), 1)
            st.did(e.tensor_scalar(OMK, CC[:, COLS["rwkv_k_a"][0]:COLS["rwkv_k_a"][0] + 2], -1.0, 1.0, ALU.mult, ALU.add))
            e.wait_ge(S("rw_lev"), 2)
            st.did(e.tensor_copy(RBV, RWL))
            st.settle()
            for g in range(2):
                ins = e.tensor_tensor_scan(RWL[:, g], keep, RBV[:, g], 0.0, ALU.mult, ALU.add)
            st.did(ins)
            st.settle()
            full = RWL[:, :, 0:TILES * P].rearrange("p g (n t) -> p g n t", t=P)
            st.did(e.tensor_scalar(RCS, full[:, :, :, P - 1], 0.5, None, ALU.mult))
            st.settle()
            st.did(e.tensor_tensor(full, full, bc(RCS.unsqueeze(3), full.shape), ALU.subtract))
            st.settle()
            e.tensor_tensor(RBV, RWL, RBV, ALU.subtract).then_inc(S("rw_wlx"), 1)
            e.wait_ge(S("rw_lev"), 6)
            st.settle()
            for g in range(2):
                st.did(e.tensor_scalar(RKP[:, g], RA[:, g], col("rwkv_k_a", g), OMK[:, g:g + 1], ALU.mult, ALU.add))
            st.settle()
            st.did(e.tensor_tensor(RKP, RKP, z[:, 2:4], ALU.mult))
            e.wait_ge(S("rw_lev"), 8)
            st.did(e.tensor_scalar(RE, RE, 1e-12, None, ALU.max))
            st.settle()
            st.did(e.reciprocal(RE, RE))
            st.settle()
            st.did(e.tensor_tensor(RKK, RKK, RE, ALU.mult))
            st.settle()
            e.sem_inc(S("rw_ex_used"), 1)
            for g in range(2):
                e.scalar_tensor_tensor(RX[:, g], z[:, g], col("rwkv_r_k", g), RKP[:, g], ALU.mult, ALU.mult).then_inc(S("rw_hs"), 1)
            e.wait_ge(S("rw_ex"), 1)
            e.tensor_tensor(REC2, REC, REC, ALU.mult)
            e.tensor_copy(RES[:, :, 0:1], RE[:, :, NP - 1:NP])
            e.tensor_copy(RES[:, :, 1:], RE[:, :, NP:NT].rearrange("p g (q c) -> p g q c", c=DSEQ)[:, :, :, DSEQ - 1])
            st.did(e.scalar_tensor_tensor(RA, RA, -1.0, RKK, ALU.mult, ALU.mult))
            e.tensor_tensor(R10[:, 2:4], z[:, 0:2], RE, ALU.mult).then_inc(S("rw_ex_used"), 1)
            e.wait_ge(S("rw_ex"), 2)
            st.settle()
            e.tensor_tensor(R10[:, 4:6], RKP, RE, ALU.mult)
            e.tensor_tensor(R10[:, 6:8], RA, RE, ALU.mult).then_inc(S("rw_ex_used"), 1)
            e.wait_ge(S("rw_ex"), 3)
            st.did(e.tensor_tensor(R10[:, 0:2], RKK, RE, ALU.mult))
            for g in range(2):
                e.wait_ge(S("rw_lor"), 9 + g)
                st.did(e.tensor_tensor(row3(RBV[:, g]), cols3(3 * g), row3(R10[:, 8 + g]), ALU.mult))
                st.settle()
                e.tensor_scalar(RBV[:, g], RBV[:, g], col("rwkv_ln_b", g), None, ALU.add).then_inc(S("rw_lev"), 1)
            st.settle()
            e.wait_ge(S("zeroed"), 3)
            e.wait_ge(S("states_in"), (11 + 8 + 4) * 16)
            e.sem_inc(S("rw_go"), 1)
            e.wait_ge(S("rw_lev"), 10)
            e.wait_ge(S("rw_ex"), 3)

            def rw_tile(n, w, last_tile):
                def tile_of(y):
                    return y[:, TILES * P:NT] if last_tile else y[:, bass.ds(n * P, P)]

                def v4(x, k=4):
                    return x[0:w].rearrange("p (h t) -> p h t", h=k)
                flat = [x.rearrange("p h t -> p (h t)")[:, 0:4 * w] for x in (RTI, RTT)]
                ti, tt = v4(flat[0]), v4(flat[1])
                idw = ident[0:w, 0:w]
                pb = RPB.rearrange("p h k t -> p (h k t)")[0:w, 0:8 * w]
                pk = RPK.rearrange("p h k t -> p (h k t)")[0:w, 0:8 * w]
                cm = const("causal_l" if last_tile else "causal", w)
                if not last_tile:
                    for g in range(2):
                        ec = REC[:, g, bass.ds(n, 1)]
                        ins = e.tensor_scalar(RXC[:, g * P:g * P + P], RSTATE[:, 0, g * P:g * P + P], ec, None, ALU.mult)
                    st.did(ins)
                e.tensor_copy(ti, bc(idw.unsqueeze(1), [w, 4, w]))
                st.did(e.tensor_copy(tt, bc(idw.unsqueeze(1), [w, 4, w])))
                e.wait_ge(S("rw_s"), n + 1)
                st.settle()
                e.sem_inc(S("select_turn"), 1)
                mk = bc(mask8("ll" if last_tile else "lv", 0, w).unsqueeze(1), [w, 2, w])
                mkt = bc(mask8("llt" if last_tile else "lvt", 0, w).unsqueeze(1), [w, 2, w])
                for j in range(2):
                    ins = e.copy_predicated(ti[:, j:4:2, :], mkt, PS(4 + j, 0, 2 * w)[0:w].rearrange("p (h t) -> p h t", h=2))
                ins.then_inc(S("rw_t"), 1)
                for j in range(2):
                    for (dst, bank) in ((pb, 0), (pk, 2)):
                        dst = dst.rearrange("p (i j c) -> p i j c", i=2, j=2)[:, :, j, :]
                        e.tensor_tensor(dst, PS(bank + j, 0, 4 * w)[0:w].rearrange("p (i c) -> p i c", i=2),
                                        bc(cm.unsqueeze(1), [w, 2, 2 * w]), ALU.mult)
                for j in range(2):
                    src = PS(j, 0, 4 * w)[0:w].rearrange("p (i k t) -> p i k t", i=2, k=2)[:, :, 0, :]
                    ins = e.copy_predicated(tt[:, j:4:2, :], mk, src)
                ins.then_inc(S("rw_t"), 1)
                if last_tile:
                    e.wait_ge(S("rw_copied"), TILES + 1)
                    for k in range(2):
                        for g in range(2):
                            ins = e.tensor_tensor(RQX[:, k, g], bc(RC[:, 2 * k + g, 0:w].unsqueeze(1), [P, SEGS, w]),
                                                  const("ind_t").rearrange("p (s t) -> p s t", s=SEGS), ALU.mult)
                    ins.then_inc(S("rw_qx"), 1)
                levels = LHALVES if last_tile else HALVES
                for l, h in list(enumerate(levels))[1:]:
                    for q, (dst, bank, mk) in enumerate(((tt, 0, "ll" if last_tile else "lv"), (ti, 1, "llt" if last_tile else "lvt"))):
                        dst, mk = half(dst, h, q == 0), half(mask8(mk, l, w), h, q == 0)
                        e.wait_ge(S("rw_t"), n * 14 + 2 * l)
                        e.wait_ge(S("rw_n"), n * 12 + 2 * l)
                        e.sem_inc(S("select_turn"), 1)
                        e.copy_predicated(dst, bc(mk.unsqueeze(1), dst.shape),
                                          PS(bank, 0, 2 * w)[0:w].rearrange("p (a n t) -> p a n t", a=4, t=h)).then_inc(S("rw_t"), 1)
                y = PS(1, 0, 256).rearrange("p (h c) -> p h c", h=4)[0:w]
                r = [RMS_[0:w, k] for k in range(4)]
                e.wait_ge(S("rw_y"), n + 1)
                st.did(e.tensor_reduce(r[0], y, AX.X, ALU.add))
                st.settle()
                st.did(e.tensor_scalar(r[1], r[0], 1.0 / 64, None, ALU.mult))
                st.settle()
                e.tensor_tensor(RY[0:w], y, bc(r[1].unsqueeze(2), [w, 4, 64]), ALU.subtract).then_inc(S("rw_yc"), 1)
                if last_tile:
                    for s in range(SEGS):
                        e.tensor_scalar(RVX[0:w, s, :], RV[0:w], const("ind_p", w)[:, s:s + 1], None, ALU.mult)
                        ins = e.tensor_scalar(RUX[0:w, s, :], RUS[0:w], const("ind_p", w)[:, s:s + 1], None, ALU.mult)
                    ins.then_inc(S("rw_vx"), 1)
                    for g in range(2):
                        e.wait_ge(S("rw_ds"), TILES + g + 1)
                        sg = RSTATE[:, :, g * P:g * P + P]
                        for s in range(SEGS):
                            o_ = (s // 4) * 512 + (s % 4) * P
                            ins = e.tensor_tensor(RDSL[:, s, :], PSt[:, o_:o_ + P], bd2, ALU.mult)
                        st.did(ins)
                        st.settle()
                        if g == 0:
                            e.sem_inc(S("rw_dsu"), 1)
                        st.did(e.tensor_tensor(RDSL, RDSL, sg, ALU.add))
                        st.settle()
                        ins = e.tensor_tensor(sg, RDSL, bc(RES[:, g].unsqueeze(2), [P, SEGS, P]), ALU.mult)
                        if g == 0:
                            st.did(ins)
                            st.settle()
                        else:
                            ins.then_inc(S("states_final"), 1)
                else:
                    e.wait_ge(S("rw_ds"), n + 1)
                    for g in range(2):
                        ins = e.scalar_tensor_tensor(RTM[:, g * P:g * P + P], PS(0, g * P, g * P + P), REC[:, g, bass.ds(n, 1)], bd2, ALU.mult, ALU.mult)
                    st.did(ins)
                    st.settle()
                    for g in range(2):
                        sg = RSTATE[:, 0, g * P:g * P + P]
                        ins = e.scalar_tensor_tensor(sg, sg, REC2[:, g, bass.ds(n, 1)], RTM[:, g * P:g * P + P], ALU.mult, ALU.add)
                    st.did(ins)
                e.wait_ge(S("rw_sq"), n + 1)
                e.tensor_reduce(r[2], RSQ[0:w], AX.X, ALU.add).then_inc(S("rw_ms"), 1)
                e.wait_ge(S("rw_rs"), n + 1)
                e.tensor_tensor(RY[0:w], RY[0:w], bc(r[3].unsqueeze(2), [w, 4, 64]), ALU.mult).then_inc(S("rw_on"), 1)
                e.wait_ge(S("rw_ot"), n + 1)
                for g in range(2):
                    bv = tile_of(RBV[:, g])
                    ins = e.scalar_tensor_tensor(bv, PS(3, g * P, g * P + w), col("rwkv_ln_w", g), bv, ALU.mult, ALU.add)
                st.did(ins)
                st.settle()
                for g in range(2):
                    ot = tile_of(OT[:, 2 + g])
                    ins = e.tensor_tensor(ot, tile_of(RBV[:, g]), ot, ALU.mult)
                ins.then_inc(S("rw_pre"), 1)

            with e.Fori(0, TILES) as n:
                st.enter(n, 7)
                rw_tile(n, P, False)
            st.leave(TILES)
            rw_tile(TILES, LASTW, True)
            barrier(e, 4)
            for u in range(2):
                split_chunk(e, u, P_OUT)
            with e.Fori(0, 4) as jj:
                for c in range(8):
                    u, br = c % 2, c % 4
                    e.wait_ge(S("sig"), jj * 8 + (c + 1))
                    e.wait_ge(S("pz"), jj * 8 + (c + 1))
                    mix = MIX[:, bass.ds(jj * 2 + c // 4, 1), :].rearrange("p o t -> p (o t)")
                    if br == 0:
                        e.tensor_tensor(row3(mix), cols3(3 * u), row3(GZ[:, u]), ALU.mult).then_inc(S(f"mul{u}"), 1)
                    else:
                        if br >= 2:
                            e.wait_ge(S("mix_add"), jj * 6 + (3 * (c // 4) + br - 1))
                        e.tensor_tensor(row3(GPR[:, br - 1]), cols3(3 * u), row3(GZ[:, u]), ALU.mult).then_inc(S(f"mul{u}"), 1)
                        e.wait_ge(S(f"mul{u}"), jj * 4 + (c // 2 + 2))
                        e.tensor_tensor(mix, mix, GPR[:, br - 1], ALU.add).then_inc(S("mix_add"), 1)
                    if br == 3:
                        e.wait_ge(S("mix_add"), jj * 6 + 3 * (c // 4 + 1))
                        hi, lo = (y[:, bass.ds(jj * 2 + c // 4, 1), :].rearrange("p o t -> p (o t)") for y in (HT_R, MIX_R))
                        split_hi(e, hi, mix).then_inc(S("parts"), 1)
                        e.wait_ge(S("parts"), jj * 2 + (c // 4 + 1))
                        split_lo(e, lo, hi, mix).then_inc(S("mix_ready"), 1)
            e.wait_ge(S("xr"), 16 * KD)
            def residual(i, u):
                e.wait_ge(S(f"chunk_done{u}"), i + P_OUT + 1)
                xr = row3(XR[:, bass.ds(i * 2 + u, 1), :].rearrange("p o t -> p (o t)"))
                e.tensor_tensor(xr, cols3(3 * u), xr, ALU.add).then_inc(S("xr_ready"), 1)
                e.wait_ge(S("xr_ready"), i * 2 + (u + 1))
                e.sem_inc(S(f"banks_free{u}"), 1)
            with e.Fori(0, 4) as i:
                for u in range(2):
                    residual(i, u)
                    k = i * 2 + u
                    x, hn, hi, lo = (y[:, bass.ds(k, 1), :].rearrange("p o t -> p (o t)") for y in (XR, HN2, HNH_R, OT_R))
                    c0 = COLS["norm_mlp"][0]
                    e.tensor_scalar(hn, x, CC[:, bass.ds(k + c0, 1)], None, ALU.mult).then_inc(S("parts"), 1)
                    e.wait_ge(S("parts"), i * 4 + (KD + 2 * u + 1))
                    split_hi(e, hi, hn).then_inc(S("parts"), 1)
                    e.wait_ge(S("parts"), i * 4 + (KD + 2 * u + 2))
                    split_lo(e, lo, hi, hn).then_inc(S("hn_ready"), 1)
                    split_chunk(e, u, i + P_OUT + 1)
            e.wait_ge(S("rstd"), 2)

            def relu(i, u, dst):
                e.wait_ge(S(f"chunk_done{u}"), i + (P_UP + 1))
                e.scalar_tensor_tensor(row3(dst), cols3(3 * u), 0.0, row3(RST2), ALU.max, ALU.mult).then_inc(S(f"banks_free{u}"), 1)

            def relu_rows(lo, n, base):
                with e.Fori(0, n) as i:
                    for u in range(2):
                        relu(i + lo, u, base[:, bass.ds(i * 2 + u, 1), :].rearrange("p o t -> p (o t)"))
                        split_chunk(e, u, i + (P_UP + lo + 1))
            relu_rows(0, 4, MIX)
            e.wait_ge(S("spilled"), 16 * KD)
            relu_rows(4, 4, XR)
            relu_rows(8, 4, HT)
            for u in range(2):
                relu(12, u, STG[:, u])
                split_chunk(e, u, P_UP + 13)
            with e.Fori(1, 3) as i:
                for u in range(2):
                    e.wait_ge(S(f"act_spilled{u}"), i * 16)
                    relu(i + 12, u, STG[:, u])
                    split_chunk(e, u, i + (P_UP + 13))
            for u in range(2):
                e.wait_ge(S(f"act_spilled{u}"), 3 * 16)
                relu(15, u, STG[:, u])
                split_chunk(e, u, P_DOWN)
            barrier(e, 5)
            def add_residual(k, n, v):
                e.wait_ge(S(f"down{v}"), n + 1)
                x = HN2[:, bass.ds(k, 1), :].rearrange("p o t -> p (o t)")
                e.tensor_tensor(row3(x), cols3(3 * v), row3(x), ALU.add).then_inc(S("dn_ready"), 1)
                e.wait_ge(S("dn_ready"), k + 1)
                e.sem_inc(S(f"down_used{v}"), 1)

            def down_parts(jj, first, last):
                for r in range(FF // P):
                    e.wait_ge(S("act_hi"), jj * 32 + (r + 1))
                    if r == 24:
                        e.wait_ge(S("act_back"), 8 * 16)
                    split_lo(e, ALO_R[r % 2], AHI_R[r % 2], act_row(r)).then_inc(S("act_parts"), 1)
                    if r == 0 and not first:
                        for v in range(2):
                            add_residual(jj * 2 + (v - 2), jj - 1, v)
                    if r % 4 == 3 and not (r < 7 and first) and not (r == 31 and last):
                        q = r // 4 + 1
                        split_chunk(e, q % 2, jj * 4 + (P_DOWN + q // 2))
            down_parts(0, True, False)
            e.wait_ge(S("res_back"), 16 * KD)
            with e.Fori(1, 3) as jj:
                down_parts(jj, False, False)
            down_parts(3, False, True)
            for v in range(2):
                add_residual(6 + v, 3, v)
            rms_dve(e, 2, SQ3R, HN2, HN2, "norm_final", lambda ins: ins.then_inc(S("y_ready"), 1))


def kernel(**inputs):
    import concourse.bacc as bacc
    from concourse.bass_utils import run_bass_kernel_spmd

    I = {k: np.asarray(v) for k, v in inputs.items()}
    assert I["hgrn_lb"].shape[0] == DEPTH == 1
    f32 = np.float32

    def chunk(w, c):
        return w[:, c:c + P].reshape(KD, P, P).transpose(1, 0, 2)

    w_in, w_br, w_out = I["w_in"][0], I["w_branch"][0], I["w_out"][0]
    w_up, w_down = I["w_up"][0], I["w_down"][0]
    gates = [O_GATE + b * D + j * P for j in range(KD) for b in range(4)]
    chunks = [chunk(w_in, c) for c in ML_T + ML_V + GL_T + GL_V + gates[:16] + RW_T + gates[16:]]
    chunks += [chunk(w_out, j * P) for j in range(KD)]
    chunks += [chunk(w_up, j * P) for j in range(FF // P)]
    down = w_down.reshape(8, 4, P, 4, 2, P).transpose(3, 0, 2, 4, 1, 5)
    chunks += list(down.reshape(4 * 8, P, KD, P))
    small = np.zeros((D, 68), f32)
    for c, n, at in SMALL:
        small[:, at:at + n] = w_in[:, c:c + n]
    x = np.concatenate([I["meta_tokens"], I["x_prompt"][0], I["x_sample"].reshape(-1, D)], 0)
    xT = np.zeros((D, W), f32)
    xT[:, :NT] = x.T
    cols = np.zeros((P, NCOLS), f32)
    for name, (o, n) in COLS.items():
        v = I[name].reshape(-1)
        if name in ("mlstm_i_b", "mlstm_f_b"):
            cols[:4, o] = v
        else:
            cols[:, o:o + n] = v.reshape(n, P).T
    cf, cu = constants()

    def pack(parts):
        at, where = 0, {}
        for k, v in parts.items():
            where[k] = (at, v.shape[1])
            at += v.shape[1]
        return np.concatenate(list(parts.values()), 1), where

    cfa, fcols = pack(cf)
    cua, ucols = pack(cu)
    conv = I["state_mlstm_conv"][0]
    arrays = {
        "cf": cfa, "cu": cua, "cols": cols, "xT": xT.reshape(KD, P, W),
        "w_small": small.reshape(KD, P, 68).transpose(1, 0, 2), "w_all": np.stack(chunks),
        "w_br": w_br.reshape(4, 2, P, KD, P).transpose(3, 2, 0, 1, 4).reshape(KD, P, 8, P),
        "w_ga": I["gla_gate_up"][0],
        "rw_wa": np.concatenate([I["rwkv_w_up"][0], I["rwkv_a_up"][0]], 0), "rw_g": I["rwkv_g_up"][0],
        "hg": I["state_hgrn"][0], "gl": I["state_gla"][0], "mc": I["state_mlstm_c"][0],
        "mn": I["state_mlstm_n"][0], "mm": I["state_mlstm_m"][0],
        "rw": I["state_rwkv"][0].transpose(0, 1, 3, 2),
        "shift": I["state_rwkv_shift"][0].reshape(NSEQ, 8, P).transpose(2, 1, 0),
        "conv": conv.reshape(NSEQ, 3, 2, P).transpose(3, 2, 0, 1),
    }
    outs = {
        "yT": (KD, P, NT), "hg": (SEGS, 4, 64, 64), "rw": (SEGS, 4, 64, 64), "shift": (P, 8, SEGS),
        "gl": (SEGS, 4, 32, 64), "mc": (SEGS, 4, 32, 64), "mn": (SEGS, 4, 32), "mm": (SEGS, 4),
        "conv_p": (P, 2, 3), "conv_s": (P, 2, NSEQ, 3),
    }
    nc = bacc.Bacc("TRN2", target_bir_lowering=False, num_devices=1)
    feeds, A, OUT = {}, {}, {}
    for name, a in arrays.items():
        a = np.ascontiguousarray(a)
        feeds[f"in_{name}"] = a
        A[name] = nc.dram_tensor(f"in_{name}", a.shape, mybir.dt.from_np(a.dtype), kind="ExternalInput").ap()
    for name, shape in outs.items():
        OUT[name] = nc.dram_tensor(f"out_{name}", shape, F32, kind="ExternalOutput").ap()
    A["acts"] = nc.dram_tensor("acts", (KD, P, W), F32, kind="Internal").ap()
    A["gates"] = nc.dram_tensor("gates", (32, P, W), F32, kind="Internal").ap()
    A["x2"] = nc.dram_tensor("residual", (KD, P, W), F32, kind="Internal").ap()
    build(nc, A, OUT, fcols, ucols, cfa.shape[1], cua.shape[1])
    R = run_bass_kernel_spmd(nc, [feeds], core_ids=[0]).results[0]
    o = {name: R[f"out_{name}"] for name in outs}
    y = o["yT"].reshape(D, NT).T
    rw = o["rw"].transpose(0, 1, 3, 2)
    shift = o["shift"].transpose(2, 1, 0).reshape(SEGS, 8 * P)
    conv_p = o["conv_p"].transpose(2, 1, 0).reshape(1, 3, 2 * P)
    conv_s = o["conv_s"].transpose(2, 3, 1, 0).reshape(NSEQ, 3, 2 * P)

    def both(a):
        return a[None, 0:1], a[None, 1:]

    st = [both(a) for a in (o["hg"], rw, shift, o["gl"], o["mc"], o["mn"], o["mm"])]
    st.append((conv_p[None], conv_s[None]))
    c = np.ascontiguousarray
    return tuple(c(a) for a in [y[META:NP][None], y[NP:].reshape(NSEQ, DSEQ, D)]
                 + [s[0] for s in st] + [s[1] for s in st])
```
